# Optimizing a Trainium2 kernel written in Bass

```python
import jax
import jax.numpy as jnp
from jax import lax
import numpy as np

D_MODEL = 1024
BATCH = 1
SEQ = 128
DEPTH = 2
DEC_BATCH = 1
DEC_SEQ = 512
PAST_LEN = 128

GRID_W = 64
H_A = 4
Q_RANK = 192
KV_RANK = 128
NOPE_A = 64
ROPE_A = 32
V_A = 64
H_B = 4
P_B = 64
G_B = 2
N_B = 64
D_CONV = 5
SSD_CHUNK = 128
D_B = H_B * P_B
CONV_CH = D_B + 2 * G_B * N_B
H_C = 4
K_C = 64
V_C = 64
HGRN_CHUNK = 16
D_C = H_C * V_C
H_D = 4
KV_D = 2
G_D = H_D // KV_D
HD_D = 64
WINDOW = 128
ATTN_BLOCK = 128
ROPE_BASE = 10000.0
D_MIX = H_A * V_A + D_B + D_C + H_D * HD_D
D_FF = 2816
N_SUB = 3
ALPHA = (2 * DEPTH) ** 0.25
BETA = (8 * DEPTH) ** -0.25
EPS = 1e-6
F_MIN = 1e-6
IN_SIZES = (Q_RANK, KV_RANK, ROPE_A,
            D_B, CONV_CH, 2 * H_B,
            H_C * K_C, 2 * H_C * K_C, D_C, D_C,
            H_D * HD_D, KV_D * HD_D, KV_D * HD_D)
D_IN = sum(IN_SIZES)
IN_SPLITS = tuple(int(v) for v in np.cumsum(IN_SIZES)[:-1])
F32 = jnp.float32
NEG = -1e30

kernel_name = 'hybrid_diffusion_prefix_trunk_step'

def rms_norm(x, g):
    xf = x.astype(F32)
    y = xf * lax.rsqrt(jnp.mean(xf * xf, axis=-1, keepdims=True) + EPS)
    return (y * g.astype(F32)).astype(x.dtype)

def layer_norm(x, g, b):
    xf = x.astype(F32)
    xc = xf - jnp.mean(xf, axis=-1, keepdims=True)
    var = jnp.mean(xc * xc, axis=-1, keepdims=True)
    return (xc * lax.rsqrt(var + EPS) * g.astype(F32) + b.astype(F32)).astype(x.dtype)

def rope_1d(x, pos):
    half = x.shape[-1] // 2
    inv = ROPE_BASE ** (-jnp.arange(half, dtype=F32) / half)
    ang = pos[:, None] * inv[None, :]
    cos = jnp.cos(ang)[None, :, None, :]
    sin = jnp.sin(ang)[None, :, None, :]
    x1 = x[..., :half].astype(F32)
    x2 = x[..., half:].astype(F32)
    return jnp.concatenate([x1 * cos - x2 * sin, x1 * sin + x2 * cos], axis=-1)

def axial_rope(x):
    t_len = x.shape[1]
    rows = t_len // GRID_W
    row = jnp.repeat(jnp.arange(rows, dtype=F32), GRID_W)
    col = (jnp.arange(t_len) % GRID_W).astype(F32)
    r = x.shape[-1] // 2
    return jnp.concatenate([rope_1d(x[..., :r], row), rope_1d(x[..., r:], col)], axis=-1).astype(x.dtype)

def sink_softmax(s, sink):
    if sink is None:
        return jax.nn.softmax(s, axis=-1)
    sk = sink.astype(F32)[:, :, None]
    m = jnp.maximum(jnp.max(s, axis=-1), sk)
    e = jnp.exp(s - m[..., None])
    den = jnp.sum(e, axis=-1) + jnp.exp(sk - m)
    return e / den[..., None]

def dense_attention(q, k, v, sink):
    B, Tq, Hk, G, Dq = q.shape
    scale = Dq ** -0.5
    qb = jnp.moveaxis(q.reshape(B, Tq // ATTN_BLOCK, ATTN_BLOCK, Hk, G, Dq), 1, 0)

    def one_block(q_blk):
        s = jnp.einsum('bqhgd,bkhd->bhgqk', q_blk, k, preferred_element_type=F32) * scale
        p = sink_softmax(s, sink)
        return jnp.einsum('bhgqk,bkhd->bqhgd', p.astype(v.dtype), v)

    o = lax.map(one_block, qb)
    return jnp.moveaxis(o, 0, 1).reshape(B, Tq, Hk, G, v.shape[-1])

def banded_attention(q, k, v, kc, vc, sink):
    B, T, Hk, G, D = q.shape
    W = WINDOW
    nb = T // W
    scale = D ** -0.5
    qb = q.reshape(B, nb, W, Hk, G, D)
    pad = ((0, 0), (W, W), (0, 0), (0, 0))
    kp = jnp.pad(k, pad).reshape(B, nb + 2, W, Hk, D)
    vp = jnp.pad(v, pad).reshape(B, nb + 2, W, Hk, D)
    kb = jnp.concatenate([kp[:, :-2], kp[:, 1:-1], kp[:, 2:]], axis=2)
    vb = jnp.concatenate([vp[:, :-2], vp[:, 1:-1], vp[:, 2:]], axis=2)
    qi = jnp.arange(W)[:, None]
    kj = jnp.arange(3 * W)[None, :]
    band = jnp.abs(kj - W - qi) <= WINDOW
    seg_blk = jnp.arange(nb)[:, None] + jnp.arange(3)[None, :] - 1
    valid = jnp.repeat((seg_blk >= 0) & (seg_blk < nb), W, axis=1)
    mask = band[None] & valid[:, None, :]
    s_lat = jnp.einsum('bnqhgd,bnkhd->bnhgqk', qb, kb, preferred_element_type=F32) * scale
    s_lat = jnp.where(mask[None, :, None, None], s_lat, NEG)
    s_ctx = jnp.einsum('bnqhgd,bkhd->bnhgqk', qb, kc, preferred_element_type=F32) * scale
    p = sink_softmax(jnp.concatenate([s_lat, s_ctx], axis=-1), sink)
    o = (jnp.einsum('bnhgqk,bnkhd->bnqhgd', p[..., :3 * W].astype(vb.dtype), vb)
         + jnp.einsum('bnhgqk,bkhd->bnqhgd', p[..., 3 * W:].astype(vc.dtype), vc))
    return o.reshape(B, T, Hk, G, D)

def centred_dwconv(x, w, b):
    y = lax.conv_general_dilated(x, w[:, None, :].astype(x.dtype), window_strides=(1,),
                                 padding=((D_CONV // 2, D_CONV // 2),),
                                 dimension_numbers=('NWC', 'WIO', 'NWC'),
                                 feature_group_count=x.shape[-1])
    return y + b.astype(x.dtype)

def masked_decay(diff, causal):
    return jnp.where(causal, jnp.exp(jnp.where(causal, diff, 0.0)), 0.0)

def ssd_scan(x, dt, a, bm, cm, d_skip, s0):
    B, T, H, P = x.shape
    Q = SSD_CHUNK
    nc = T // Q
    ch = lambda t: t.astype(F32).reshape(B, nc, Q, *t.shape[2:])
    xc, dtc, bc, cc = ch(x), ch(dt), ch(bm), ch(cm)
    cum = jnp.cumsum(dtc * a.astype(F32), axis=2)
    xdt = xc * dtc[..., None]
    causal = jnp.tril(jnp.ones((Q, Q), bool))[:, :, None]
    diff = cum[:, :, :, None] - cum[:, :, None, :]
    seg = masked_decay(diff, causal)
    scores = jnp.einsum('bcihn,bcjhn->bcijh', cc, bc) * seg
    y_intra = jnp.einsum('bcijh,bcjhp->bcihp', scores, xdt)
    last = cum[:, :, -1:]
    chunk_state = jnp.einsum('bcjhn,bcjhp->bchpn', bc * jnp.exp(last - cum)[..., None], xdt)
    chunk_decay = jnp.exp(last[:, :, 0])

    def step(s, inp):
        cs, cd = inp
        return cd[..., None, None] * s + cs, s

    s_fin, s_in = lax.scan(step, s0.astype(F32),
                           (jnp.moveaxis(chunk_state, 1, 0), jnp.moveaxis(chunk_decay, 1, 0)))
    s_in = jnp.moveaxis(s_in, 0, 1)
    y_inter = jnp.einsum('bcihn,bchpn->bcihp', cc * jnp.exp(cum)[..., None], s_in)
    y = (y_intra + y_inter).reshape(B, T, H, P) + x.astype(F32) * d_skip.astype(F32)[:, None]
    return y.astype(x.dtype), s_fin.astype(x.dtype)

def gla_scan(q, k, v, log_f, s0):
    B, T, H, K = q.shape
    Q = HGRN_CHUNK
    nc = T // Q
    ch = lambda t: t.astype(F32).reshape(B, nc, Q, *t.shape[2:])
    qc, kc, vc, lf = ch(q), ch(k), ch(v), ch(log_f)
    cum = jnp.cumsum(lf, axis=2)
    causal = jnp.tril(jnp.ones((Q, Q), bool))[:, :, None, None]
    diff = cum[:, :, :, None] - cum[:, :, None, :]
    dec = masked_decay(diff, causal)
    att = jnp.einsum('bcijhk,bcjhk->bcijh', dec * qc[:, :, :, None], kc)
    o_intra = jnp.einsum('bcijh,bcjhv->bcihv', att, vc)
    last = cum[:, :, -1:]
    chunk_state = jnp.einsum('bcjhk,bcjhv->bchkv', kc * jnp.exp(last - cum), vc)
    chunk_decay = jnp.exp(last[:, :, 0])

    def step(s, inp):
        cs, cd = inp
        return cd[..., None] * s + cs, s

    s_fin, s_in = lax.scan(step, s0.astype(F32),
                           (jnp.moveaxis(chunk_state, 1, 0), jnp.moveaxis(chunk_decay, 1, 0)))
    s_in = jnp.moveaxis(s_in, 0, 1)
    o_inter = jnp.einsum('bcihk,bchkv->bcihv', qc * jnp.exp(cum), s_in)
    o = (o_intra + o_inter).reshape(B, T, H, v.shape[-1])
    return o.astype(v.dtype), s_fin.astype(v.dtype)

def flip_t(t):
    return jnp.flip(t, axis=1)

def mla_expand(ckv_n, kr, w_ukv):
    B, T, _ = ckv_n.shape
    kv = (ckv_n @ w_ukv).reshape(B, T, H_A, NOPE_A + V_A)
    k = jnp.concatenate([kv[..., :NOPE_A], jnp.broadcast_to(kr, (B, T, H_A, ROPE_A)).astype(kv.dtype)], axis=-1)
    return k, kv[..., NOPE_A:]

def ssd_mixer(z, xbc, dt_raw, p, s0):
    B, T, _ = z.shape
    xbc = jax.nn.silu(centred_dwconv(xbc, p['ssd_conv_w'], p['ssd_conv_b']))
    xs, bm, cm = jnp.split(xbc, [D_B, D_B + G_B * N_B], axis=-1)
    xs = xs.reshape(B, T, H_B, P_B)
    rep = H_B // G_B
    bm = jnp.repeat(bm.reshape(B, T, G_B, N_B), rep, axis=2)
    cm = jnp.repeat(cm.reshape(B, T, G_B, N_B), rep, axis=2)
    dt = jax.nn.softplus(dt_raw.reshape(B, T, 2, H_B).astype(F32) + p['ssd_dt_bias'].astype(F32))
    a = -jnp.exp(p['ssd_a_log'].astype(F32))
    d = p['ssd_d']
    y_f, s_f = ssd_scan(xs, dt[:, :, 0], a[0], bm, cm, d[0], s0[:, 0])
    y_b, s_b = ssd_scan(flip_t(xs), flip_t(dt[:, :, 1]), a[1], flip_t(bm), flip_t(cm), d[1], s0[:, 1])
    y = (y_f + flip_t(y_b)) * jax.nn.silu(z.reshape(B, T, H_B, P_B))
    y = rms_norm(y, p['ssd_norm'].reshape(H_B, P_B))
    return y.reshape(B, T, D_B), jnp.stack([s_f, s_b], axis=1)

def hgrn_mixer(q, f_raw, i_in, g, p, s0):
    B, T, _ = q.shape
    fr = f_raw.reshape(B, T, 2, H_C, K_C).astype(F32)
    lb = p['hgrn_lb'].astype(F32).reshape(2, H_C, K_C)
    f = lb + (1.0 - lb) * jax.nn.sigmoid(fr)
    log_f = jnp.log(jnp.maximum(f, F_MIN))
    key = (1.0 - lb) * jax.nn.sigmoid(-fr)
    qh = q.reshape(B, T, H_C, K_C)
    vh = i_in.reshape(B, T, H_C, V_C)
    o_f, s_f = gla_scan(qh, key[:, :, 0], vh, log_f[:, :, 0], s0[:, 0])
    o_b, s_b = gla_scan(flip_t(qh), flip_t(key[:, :, 1]), flip_t(vh), flip_t(log_f[:, :, 1]), s0[:, 1])
    o = rms_norm(o_f + flip_t(o_b), p['hgrn_norm'].reshape(H_C, V_C)) * jax.nn.silu(g.reshape(B, T, H_C, V_C))
    return o.reshape(B, T, D_C), jnp.stack([s_f, s_b], axis=1)

def token_mixing(h, p, ctx):
    B, T, _ = h.shape
    latent = ctx is not None
    (a_cq, a_ckv, a_kr, b_z, b_xbc, b_dt, c_q, c_f, c_i, c_g, d_q, d_k, d_v) = jnp.split(
        h @ p['w_in'], IN_SPLITS, axis=-1)

    q_a = (rms_norm(a_cq, p['mla_q_norm']) @ p['mla_w_uq']).reshape(B, T, H_A, NOPE_A + ROPE_A)
    ckv_n = rms_norm(a_ckv, p['mla_kv_norm'])
    kr = a_kr[:, :, None, :]
    if latent:
        q_a = jnp.concatenate([q_a[..., :NOPE_A], axial_rope(q_a[..., NOPE_A:])], axis=-1)
        kr = axial_rope(kr)
    k_a, v_a = mla_expand(ckv_n, kr, p['mla_w_ukv'])
    if latent:
        k_c, v_c = mla_expand(ctx[0], ctx[1][:, :, None, :], p['mla_w_ukv'])
        k_a = jnp.concatenate([k_a, k_c], axis=1)
        v_a = jnp.concatenate([v_a, v_c], axis=1)
    o_a = dense_attention(q_a[:, :, :, None, :], k_a, v_a, None).reshape(B, T, H_A * V_A)

    s0_b = ctx[2] if latent else jnp.zeros((B, 2, H_B, P_B, N_B), h.dtype)
    o_b, st_b = ssd_mixer(b_z, b_xbc, b_dt, p, s0_b)

    s0_c = ctx[3] if latent else jnp.zeros((B, 2, H_C, K_C, V_C), h.dtype)
    o_c, st_c = hgrn_mixer(c_q, c_f, c_i, c_g, p, s0_c)

    q_d = d_q.reshape(B, T, H_D, HD_D)
    k_d = d_k.reshape(B, T, KV_D, HD_D)
    v_d = d_v.reshape(B, T, KV_D, HD_D)
    sink = p['gqa_sink'].reshape(KV_D, G_D)
    if latent:
        o_d = banded_attention(axial_rope(q_d).reshape(B, T, KV_D, G_D, HD_D), axial_rope(k_d), v_d,
                               ctx[4], ctx[5], sink)
    else:
        o_d = dense_attention(q_d.reshape(B, T, KV_D, G_D, HD_D), k_d, v_d, sink)
    o_d = o_d.reshape(B, T, H_D * HD_D)

    out = jnp.concatenate([o_a, o_b, o_c, o_d], axis=-1) @ p['w_out']
    state = None if latent else (ckv_n, a_kr, st_b, st_c, k_d, v_d)
    return out, state

def swiglu(h, w_gu, w_down):
    gate, up = jnp.split(h @ w_gu, 2, axis=-1)
    return (jax.nn.silu(gate) * up) @ w_down

def modulate(x, shift, scale):
    return x * (1 + scale) + shift

def trunk_layer(x, mod, p, ctx):
    shift, scale, gate = mod[:, :, :, 0], mod[:, :, :, 1], mod[:, :, :, 2]
    h = modulate(x, shift[:, :, 0], scale[:, :, 0])
    x = layer_norm(ALPHA * x + 0.5 * gate[:, :, 0] * swiglu(h, p['ffn_w_gu'][0], p['ffn_w_down'][0]),
                   p['ln_g'][0], p['ln_b'][0])
    h = modulate(x, shift[:, :, 1], scale[:, :, 1])
    u, state = token_mixing(h, p, ctx)
    x = layer_norm(ALPHA * x + gate[:, :, 1] * u, p['ln_g'][1], p['ln_b'][1])
    h = modulate(x, shift[:, :, 2], scale[:, :, 2])
    x = layer_norm(ALPHA * x + 0.5 * gate[:, :, 2] * swiglu(h, p['ffn_w_gu'][1], p['ffn_w_down'][1]),
                   p['ln_g'][2], p['ln_b'][2])
    return x, state

def setup_inputs(seed: int = 0) -> dict:
    key = jax.random.key(seed)
    ks = iter(jax.random.split(key, 48))

    def nrm(shape, scale):
        return scale * jax.random.normal(next(ks), shape, F32)

    dt0 = jnp.exp(jax.random.uniform(next(ks), (DEPTH, 2, H_B), F32, np.log(1e-3), np.log(1e-1)))
    dt_bias = dt0 + jnp.log(-jnp.expm1(-dt0))
    a_log = jnp.log(jax.random.uniform(next(ks), (DEPTH, 2, H_B), F32, 1.0, 16.0))
    return {
        'x_prompt': nrm((BATCH, SEQ, D_MODEL), 1.0),
        'x_sample': nrm((DEC_BATCH, DEC_SEQ, D_MODEL), 1.0),
        'cache_a_ckv': nrm((DEC_BATCH, DEPTH, PAST_LEN, KV_RANK), 1.0),
        'cache_a_krope': nrm((DEC_BATCH, DEPTH, PAST_LEN, ROPE_A), 1.0),
        'state_b_ssm': nrm((DEC_BATCH, DEPTH, 2, H_B, P_B, N_B), 0.5),
        'state_c_hgrn': nrm((DEC_BATCH, DEPTH, 2, H_C, K_C, V_C), 0.5),
        'cache_d_k': nrm((DEC_BATCH, DEPTH, PAST_LEN, KV_D, HD_D), 1.0),
        'cache_d_v': nrm((DEC_BATCH, DEPTH, PAST_LEN, KV_D, HD_D), 1.0),
        'c': nrm((DEC_BATCH, D_MODEL), 1.0),
        'c_ctx': nrm((D_MODEL,), 1.0),
        'w_mod': nrm((DEPTH, D_MODEL, N_SUB * 3 * D_MODEL), 0.5 * D_MODEL ** -0.5),
        'b_mod': nrm((DEPTH, N_SUB * 3 * D_MODEL), 0.02),
        'ln_g': 1.0 + nrm((DEPTH, N_SUB, D_MODEL), 0.02),
        'ln_b': nrm((DEPTH, N_SUB, D_MODEL), 0.02),
        'ffn_w_gu': nrm((DEPTH, 2, D_MODEL, 2 * D_FF), BETA * D_MODEL ** -0.5),
        'ffn_w_down': nrm((DEPTH, 2, D_FF, D_MODEL), BETA * D_FF ** -0.5),
        'w_in': nrm((DEPTH, D_MODEL, D_IN), D_MODEL ** -0.5),
        'w_out': nrm((DEPTH, D_MIX, D_MODEL), BETA * D_MIX ** -0.5),
        'mla_q_norm': 1.0 + nrm((DEPTH, Q_RANK), 0.02),
        'mla_kv_norm': 1.0 + nrm((DEPTH, KV_RANK), 0.02),
        'mla_w_uq': nrm((DEPTH, Q_RANK, H_A * (NOPE_A + ROPE_A)), Q_RANK ** -0.5),
        'mla_w_ukv': nrm((DEPTH, KV_RANK, H_A * (NOPE_A + V_A)), KV_RANK ** -0.5),
        'ssd_conv_w': nrm((DEPTH, D_CONV, CONV_CH), D_CONV ** -0.5),
        'ssd_conv_b': nrm((DEPTH, CONV_CH), 0.02),
        'ssd_a_log': a_log,
        'ssd_dt_bias': dt_bias,
        'ssd_d': 1.0 + nrm((DEPTH, 2, H_B), 0.02),
        'ssd_norm': 1.0 + nrm((DEPTH, D_B), 0.02),
        'hgrn_lb_logits': nrm((DEPTH, 2, H_C * K_C), 0.1),
        'hgrn_norm': 1.0 + nrm((DEPTH, D_C), 0.02),
        'gqa_sink': nrm((DEPTH, H_D), 0.5),
    }

def reference(x_prompt, x_sample, cache_a_ckv, cache_a_krope, state_b_ssm, state_c_hgrn,
              cache_d_k, cache_d_v, c, c_ctx, w_mod, b_mod, ln_g, ln_b, ffn_w_gu, ffn_w_down,
              w_in, w_out, mla_q_norm, mla_kv_norm, mla_w_uq, mla_w_ukv, ssd_conv_w, ssd_conv_b,
              ssd_a_log, ssd_dt_bias, ssd_d, ssd_norm, hgrn_lb_logits, hgrn_norm, gqa_sink):
    lb_p = jax.nn.softmax(hgrn_lb_logits.astype(F32), axis=0)
    hgrn_lb = jnp.cumsum(lb_p, axis=0) - lb_p[:1]
    y_p = x_prompt
    y_s = x_sample
    ctx_states = []
    for l in range(DEPTH):
        p = {'w_in': w_in[l], 'w_out': w_out[l], 'ln_g': ln_g[l], 'ln_b': ln_b[l],
             'ffn_w_gu': ffn_w_gu[l], 'ffn_w_down': ffn_w_down[l],
             'mla_q_norm': mla_q_norm[l], 'mla_kv_norm': mla_kv_norm[l],
             'mla_w_uq': mla_w_uq[l], 'mla_w_ukv': mla_w_ukv[l],
             'ssd_conv_w': ssd_conv_w[l], 'ssd_conv_b': ssd_conv_b[l], 'ssd_a_log': ssd_a_log[l],
             'ssd_dt_bias': ssd_dt_bias[l], 'ssd_d': ssd_d[l], 'ssd_norm': ssd_norm[l],
             'hgrn_lb': hgrn_lb[l], 'hgrn_norm': hgrn_norm[l], 'gqa_sink': gqa_sink[l]}
        mod_ctx = (jax.nn.silu(c_ctx) @ w_mod[l] + b_mod[l]).reshape(1, 1, N_SUB, 3, D_MODEL)
        mod_lat = (jax.nn.silu(c) @ w_mod[l] + b_mod[l]).reshape(c.shape[0], 1, N_SUB, 3, D_MODEL)
        y_p, st = trunk_layer(y_p, mod_ctx, p, None)
        ctx_states.append(st)
        ctx = (cache_a_ckv[:, l], cache_a_krope[:, l], state_b_ssm[:, l], state_c_hgrn[:, l],
               cache_d_k[:, l], cache_d_v[:, l])
        y_s, _ = trunk_layer(y_s, mod_lat, p, ctx)
    new_a_ckv = jnp.stack([s[0] for s in ctx_states], axis=1)
    new_a_krope = jnp.stack([s[1] for s in ctx_states], axis=1)
    new_b_ssm = jnp.stack([s[2] for s in ctx_states], axis=1)
    new_c_hgrn = jnp.stack([s[3] for s in ctx_states], axis=1)
    new_d_k = jnp.stack([s[4] for s in ctx_states], axis=1)
    new_d_v = jnp.stack([s[5] for s in ctx_states], axis=1)
    return (y_p, y_s, new_a_ckv, new_a_krope, new_b_ssm, new_c_hgrn, new_d_k, new_d_v)


_drawn_inputs = setup_inputs


def setup_inputs(seed=0):
    import zlib

    import numpy as np

    out = dict(_drawn_inputs(seed))
    spreads = {}
    factors = {'cache_a_ckv': 8.0,
     'cache_a_krope': 8.0,
     'state_c_hgrn': 8.0,
     'cache_d_k': 8.0,
     'cache_d_v': 8.0,
     'ffn_w_gu': 3.189,
     'ffn_w_down': 3.148,
     'mla_q_norm': 8.0,
     'mla_kv_norm': 2.886,
     'mla_w_uq': 6.054,
     'ssd_d': 8.0,
     'ssd_norm': 8.0,
     'hgrn_norm': 8.0,
     'gqa_sink': 8.0}
    for name, (base, spread) in spreads.items():
        noise = np.random.default_rng([zlib.crc32(name.encode()), seed]).standard_normal(out[name].shape)
        drawn = base * np.exp(spread * noise) if base else spread * noise
        out[name] = jnp.asarray(drawn.astype(out[name].dtype))
    for name, factor in factors.items():
        out[name] = (out[name] * factor).astype(out[name].dtype)
    return out
```

```python
from contextlib import ExitStack

import numpy as np
import concourse.bass as bass
from concourse import mybir
from concourse.alu_op_type import AluOpType as ALU

F32 = mybir.dt.float32
I32 = mybir.dt.int32
ACT = mybir.ActivationFunctionType
AX_X = mybir.AxisListType.X

P = 128
D_MODEL, DEPTH, LAT, CTX, PAST = 1024, 2, 512, 128, 128
TOK = LAT + CTX
EXT = TOK + PAST
KT_M = D_MODEL // P
D_FF = 2816
FT = D_FF // P
N_SUB = 3
ALPHA = (2 * DEPTH) ** 0.25
EPS = 1e-6
F_MIN = 1e-6
NEG = -1e30
GRID_W = 64
ROPE_BASE = 10000.0
H_A, NOPE, ROPE, V_A, Q_RANK, KV_RANK = 4, 64, 32, 64, 192, 128
QK_A = NOPE + ROPE
TAPS = 5
NCH = TOK // P
LEVELS = 7
SLOT = 8 * 512
SEGS = ((0, 0, LAT), (2, LAT, CTX))

C_CQ, C_CKV, C_Z, C_BC, C_DT = 0, 192, 352, 864, 1120
C_CQH, C_FB, C_G, C_DQ, C_DK = 1128, 1640, 2152, 2408, 2664

R_BMOD, R_LNG, R_LNB = 0, 72, 96
R_QN, R_KVN, R_CW, R_CB, R_SN, R_HN, R_C = 0, 2, 3, 33, 39, 41, 43
ROWS1, ROWS2 = 120, 59
N_SMALL = 48


def constants():
    parts, at, width = [], {}, 0

    def put(name, a):
        nonlocal width
        b = np.zeros((P, a.shape[1]), np.float32)
        b[:a.shape[0]] = a
        parts.append(b)
        at[name] = (width, a.shape[1])
        width += a.shape[1]

    t = np.arange(LAT)
    row, col = (t // GRID_W).astype(np.float32), (t % GRID_W).astype(np.float32)

    def rope(dim):
        r = dim // 2
        half = r // 2
        inv = (ROPE_BASE ** (-np.arange(half, dtype=np.float32) / half)).astype(np.float32)
        cos, sin, swap = np.zeros((dim, LAT)), np.zeros((dim, LAT)), np.zeros((dim, dim))
        for a, pos in enumerate((row, col)):
            ang = (pos[None, :] * inv[:, None]).astype(np.float32)
            lo, hi = a * r + np.arange(half), a * r + half + np.arange(half)
            cos[lo], cos[hi] = np.cos(ang), np.cos(ang)
            sin[lo], sin[hi] = -np.sin(ang), np.sin(ang)
            swap[hi, lo] = 1
            swap[lo, hi] = 1
        return cos, sin, swap

    i = np.arange(P)
    put("ident", np.eye(P))
    put("ones", np.ones((P, P)))
    put("block", (i[:, None] // 64 == i[None, :] // 64).astype(np.float32))
    cos, sin, swap = rope(ROPE)
    ca, sa, pa = np.ones((QK_A, LAT)), np.zeros((QK_A, LAT)), np.zeros((QK_A, QK_A))
    ca[NOPE:], sa[NOPE:], pa[NOPE:, NOPE:] = cos, sin, swap
    put("cos_a", ca), put("sin_a", sa), put("swap_a", pa)
    cos, sin, swap = rope(64)
    pd = np.zeros((P, P))
    pd[:64, :64], pd[64:, 64:] = swap, swap
    put("cos_d", np.tile(cos, (2, 1))), put("sin_d", np.tile(sin, (2, 1))), put("swap_d", pd)
    put("far_before", np.where(i[None, :] >= i[:, None], 0.0, NEG))
    put("far_after", np.where(i[None, :] <= i[:, None], 0.0, NEG))
    sel = np.zeros((8, 4, P))
    for d in range(2):
        for ct in range(2):
            for p in range(P):
                sel[d * 4 + ct * 2 + p // 64, d * 2 + ct, p] = 1
    put("sel", sel.reshape(8, 4 * P))
    masks = [np.eye(P)]
    for lev in range(1, LEVELS + 1):
        m = 2 ** (lev - 1)
        same = i[:, None] // (2 * m) == i[None, :] // (2 * m)
        masks.append(same & (i[:, None] // m != i[None, :] // m))
    put("masks", np.concatenate([np.asarray(m, np.float32) for m in masks], 1))
    put("eps", np.full((P, 1), EPS))
    return np.concatenate(parts, 1).astype(np.float32), at


def plan_layer():
    fills = [(f"mod{i}", 1) for i in range(18)]
    ffn = lambda s: [(f"gu{s}.{i}", 2) for i in range(FT // 2)] + [(f"dn{s}.{i}", 1) for i in range(KT_M)]
    fills += ffn(0)
    fills += [("zx", 1), ("bc", 8), ("qf", 1), ("fi", 1), ("g", 1), ("a", 1), ("d", 5), ("o0", 1), ("o1", 1)]
    fills += ffn(2)
    number, total, loaded = {}, [0, 0], []
    for n, (name, k) in enumerate(fills):
        number[name] = n
        total[n % 2] += 16 * k
        loaded.append(total[n % 2])
    jobs = [f"gu0.{f}" for f in range(FT)] + [f"dn0.{m}" for m in range(KT_M)]
    jobs += ["x0", "x1", "b0", "b1", "c0", "c1", "z0", "z1", "dt"] + [f"sel{d}" for d in range(4)] + ["y0", "ms0"]
    jobs += ["hq0", "hq1", "f0", "f1", "f2", "f3", "iv", "g0", "g1", "y1", "ms1"]
    jobs += ["cq0", "cq1", "ckv", "kr", "msq", "mskv"] + [f"q{h}" for h in range(4)] + [f"k{h}" for h in range(4)] + ["va"]
    jobs += ["qd0", "qd1", "kd", "vd"] + [f"o{m}" for m in range(KT_M)]
    jobs += [f"gu2.{f}" for f in range(FT)] + [f"dn2.{m}" for m in range(KT_M)]
    job = {n: i for i, n in enumerate(jobs)}
    units = []
    for kind in "AD":
        for h in range(4):
            for t in range(4):
                lo, hi = (0, 4) if kind == "A" else (max(t - 1, 0), min(t + 2, 4))
                units.append(dict(kind=kind, h=h, q=t * P, lo=lo, hi=hi, cache=True, t=t,
                                  tiles=list(range(lo, hi)) + [5]))
            units.append(dict(kind=kind, h=h, q=LAT, lo=4, hi=5, cache=False, t=None, tiles=[4]))
    return number, loaded, job, units


def trunk_kernel(nc, a, consts, const_at):
    number, loaded_at, job, units = plan_layer()
    with ExitStack() as ctx:
        def sb(name, cols, rows=P):
            return ctx.enter_context(nc.sbuf_tensor(name, [rows, cols], F32))

        def sem(name):
            return ctx.enter_context(nc.semaphore(name))

        banks = ctx.enter_context(nc.psum_tensor("banks", [P, 8, 512], F32))

        cst = sb("cst", consts.shape[1])
        X = sb("x_res", KT_M * TOK)[:].rearrange("p (k t) -> p k t", k=KT_M)
        H = sb("h_mod", KT_M * TOK)[:].rearrange("p (k t) -> p k t", k=KT_M)
        MIX = sb("mixed", KT_M * TOK)[:].rearrange("p (k t) -> p k t", k=KT_M)
        W = sb("w_slots", 2 * SLOT)[:].rearrange("p (s c) -> p s c", s=2)
        WU = sb("w_mla", 2 * 384 + 512)
        W_UQ = WU[:, 0:768].rearrange("p (k c) -> p k c", k=2)
        W_UKV = WU[:, 768:1280]
        PR1, PR2 = sb("par_rows1", P), sb("par_rows2", P)
        PT1, PT2 = sb("par1", ROWS1), sb("par2", ROWS2)
        SC = sb("cond", 16)[:].rearrange("p (k g) -> p k g", k=8)
        MOD = sb("mod", 144)[:].rearrange("p (s w m g) -> p s w m g", s=3, w=3, m=8)
        W_DT = sb("w_dt", 64)[:].rearrange("p (k c) -> p k c", k=8)
        LBT, LB, LBN, OML = sb("lb_t", 8), sb("lb", 4), sb("lb_next", 4), sb("one_minus_lb", 4)
        LBW = sb("lb_work", 4)
        DTP = sb("dt_par", 4, 8)
        SKIP, DS = sb("skip_par", 8), sb("skip", 2)
        SINK = sb("sink", 8)
        S0B, S0C = sb("s0_ssd", 512, 64), sb("s0_hgrn", 256)
        FIN, FINT = sb("fin", 256), S0B
        DEC = sb("chunk_decay", 20)[:].rearrange("p (d c h) -> p d c h", d=2, c=2)
        RS = sb("rstd", TOK)
        SM = sb("softmax_cols", 8 * 8)[:].rearrange("p (u c) -> p u c", u=8)
        CKT = sb("cache_rows", 3 * P)
        NEWROWS = sb("new_rows", P + P + QK_A + P)
        ARENA = 20480
        arena = sb("arena", ARENA)
        LBR = arena[0:8, 5120:5248]

        def view(first, k, n):
            return arena[:, first:first + k * n].rearrange("p (k n) -> p k n", k=k)

        HID, GATE, SQX = view(0, FT, TOK), view(FT * TOK, 2, TOK), view(0, KT_M, TOK)
        Q, KF, KB, PF, SE, SI, PB = (view(i * 1280, 2, TOK) for i in range(7))
        QL, KL = view(8960, 2, TOK), view(10240, 2, TOK)
        KTOK = arena[:, 8960:11520].rearrange("p (c d n) -> p c d n", c=5, d=4)
        CPAD = view(8960, 2, 648)
        CONV = arena[:, 8960 + 1296:8960 + 1296 + 644]
        V = view(11520, 5, 256)
        ATT = arena[:, 12800:15360].rearrange("p (c h n) -> p c h n", c=5, h=4)
        DTW = arena[0:8, 12800:15360].rearrange("p (k n) -> p k n", k=4)
        DT_B = arena[0:8, 5120:6400].rearrange("p (k n) -> p k n", k=2)
        SIN = arena[:, 15360:17920].rearrange("p (c d n) -> p c d n", c=5, d=4)
        XT, ZS = view(17920, 2, TOK), view(19200, 2, TOK)
        BB = PB
        Y, SQ, RB = SE, PB, KF
        CQ, CQN, SQA = view(0, 2, TOK), view(1280, 2, TOK), view(2560, 2, TOK)
        KVR, CKN, RA = arena[:, 3840:4480], arena[:, 4480:5248], arena[:, 5248:5888]
        KR = arena[:, 5888:6656]
        QA, KA = view(6656, 4, TOK), view(9216, 4, EXT)
        VA, VD = view(12288, 6, 256), view(13824, 6, P)
        QD, KD = view(14592, 2, TOK), arena[:, 15872:16640]
        ROT = arena[:, 16640:17152]
        PRB = view(17152, 2, 640)
        PTS = view(18432, 2, 640)
        XIN = view(0, 5, D_MODEL)

        def cc(name, rows=P):
            c0, n = const_at[name]
            return cst[0:rows, c0:c0 + n]

        ident, ones, block1 = cc("ident"), cc("ones"), cc("block")
        masks = cc("masks").bitcast(I32).rearrange("p (l n) -> p l n", l=LEVELS + 1)
        sel = cc("sel", 8).rearrange("p (d n) -> p d n", d=4)
        eps = cc("eps")

        init_load, init_turn, init_copy, init_lb, init_ready = (sem(n) for n in (
            "init_load", "init_turn", "init_copy", "init_lb", "init_ready"))
        fin_turn, fin_copy, fin_store = sem("fin_turn"), sem("fin_copy"), sem("fin_store")
        arrived, go = sem("arrived"), sem("go")
        names = ("par_load pool_load par_turned par_ready cond_ready mod_acc mod_ready modded scaled "
                 "w_used done gated mean_ready centred squared var_ready rstd affine "
                 "pads conv_in conv_out xt_turned v_ready dt_ready bc_ready gla_act "
                 "level_k att_done att_used exps prods sums fin_exp fin_prod k_turned k_copied "
                 "cs_done cs_used sin_zero s0_turned s0_ready sin_ready fin_out ft_turned ft_ready "
                 "y_ready ysq y_rstd excl_zero dt_step adt_copied f_raw f_ready mixed_ready "
                 "aq_sq aq_rstd aq_norm akv_norm cache_turned cache_ready rot_done rot_used roped kcopied attn_in_act "
                 "new_turned new_ready scored maxed expd normed_p p_turned p_copied pv_done pv_used "
                 "state_store small_store act_chain dve_chain pool_chain")
        s = {n: sem(n) for n in names.split()}
        w_loaded = [sem("w_loaded_even"), sem("w_loaded_odd")]
        freed = [sem("freed_even"), sem("freed_odd")]
        layer_sems = list(s.values()) + w_loaded + freed

        def slot(j):
            return 3 * (j % 2)

        def bank(n):
            return banks[:, n, :]

        def w_slot(name, k, c):
            return W[:, number[name] % 2, 0:k * c].rearrange("p (k c) -> p k c", k=k)

        def chain(eng, signal):
            count = [0]

            def link(ins):
                count[0] += 1
                ins.then_inc(signal, 1)
                eng.wait_ge(signal, count[0])
            return link

        def bc(ap, shape):
            return ap.broadcast_to(shape)

        rotated = [(QA[0:QK_A, h, 0:LAT], QK_A) for h in range(4)] + [(KR[0:QK_A, 0:LAT], QK_A)]
        rotated += [(QD[:, i, 0:LAT], P) for i in range(2)] + [(KD[:, 0:LAT], P)]

        blockctx = ctx.enter_context(nc.Block())

        @blockctx.sync
        def _(sp):
            sp.dma_start(cst[:], a["consts"]).then_inc(init_load, 16)
            for t in range(4):
                sp.dma_start(XIN[:, t, :], a["x_sample"][0, t * P:(t + 1) * P, :]).then_inc(init_load, 16)
            sp.dma_start(XIN[:, 4, :], a["x_prompt"][0]).then_inc(init_load, 16)
            sp.dma_start(LBR, a["hgrn_lb_logits"].rearrange("l d (t p) -> (l d t) p", p=P)).then_inc(init_load, 16)
            sp.wait_ge(init_load, 112)
            sp.wait_ge(init_ready, 1)

            with sp.Fori(0, DEPTH) as l:
                small = s["par_load"]
                sp.dma_start(PR1[0:72, :], a["b_mod"][l].rearrange("(r p) -> r p", p=P)).then_inc(small, 16)
                sp.dma_start(PR1[72:96, :], a["ln_g"][l].rearrange("s (r p) -> (s r) p", p=P)).then_inc(small, 16)
                sp.dma_start(PR1[96:120, :], a["ln_b"][l].rearrange("s (r p) -> (s r) p", p=P)).then_inc(small, 16)
                sp.dma_start(PR2[0:1, :], a["mla_q_norm"][bass.ds(l, 1), 0:P]).then_inc(small, 16)
                sp.dma_start(PR2[1:2, 0:64], a["mla_q_norm"][bass.ds(l, 1), P:Q_RANK]).then_inc(small, 16)
                sp.dma_start(PR2[1:2, 64:P], a["mla_q_norm"][bass.ds(l, 1), P:Q_RANK]).then_inc(small, 16)
                sp.dma_start(PR2[2:3, :], a["mla_kv_norm"][bass.ds(l, 1), :]).then_inc(small, 16)
                for tap in range(TAPS + 1):
                    r = R_CW + 6 * tap
                    src = a["ssd_conv_w"][l, tap] if tap < TAPS else a["ssd_conv_b"][l]
                    sp.dma_start(PR2[r:r + 2, :], src[0:256].rearrange("(r p) -> r p", p=P)).then_inc(small, 16)
                    for dup in range(2):
                        sp.dma_start(PR2[r + 2:r + 6, dup * 64:dup * 64 + 64],
                                     src[256:512].rearrange("(r p) -> r p", p=64)).then_inc(small, 16)
                sp.dma_start(PR2[R_SN:R_SN + 2, :], a["ssd_norm"][l].rearrange("(r p) -> r p", p=P)).then_inc(small, 16)
                sp.dma_start(PR2[R_HN:R_HN + 2, :], a["hgrn_norm"][l].rearrange("(r p) -> r p", p=P)).then_inc(small, 16)
                sp.dma_start(PR2[R_C:R_C + 8, :], a["c"][0].rearrange("(r p) -> r p", p=P)).then_inc(small, 16)
                sp.dma_start(PR2[R_C + 8:R_C + 16, :], a["c_ctx"].rearrange("(r p) -> r p", p=P)).then_inc(small, 16)
                sp.dma_start(DTP[:, 0:1], a["ssd_dt_bias"][l].rearrange("d (h o) -> (d h) o", o=1)).then_inc(small, 16)
                sp.dma_start(DTP[:, 1:2], a["ssd_a_log"][l].rearrange("d (h o) -> (d h) o", o=1)).then_inc(small, 16)
                sp.dma_start(SKIP[:], a["ssd_d"][bass.ds(l, 1)].rearrange("o d h -> o (d h)").partition_broadcast(P)).then_inc(small, 16)
                sp.dma_start(SINK[:, 0:4], a["gqa_sink"][bass.ds(l, 1)].partition_broadcast(P)).then_inc(small, 16)
                sp.dma_start(W_DT, a["w_in"][l].rearrange("(k p) c -> p k c", p=P)[:, :, C_DT:C_DT + 8]).then_inc(small, 16)
                sp.dma_start(W_UQ[:, 0, :], a["mla_w_uq"][l, 0:P, :]).then_inc(small, 16)
                sp.dma_start(W_UQ[0:64, 1, :], a["mla_w_uq"][l, P:Q_RANK, :]).then_inc(small, 16)
                sp.dma_start(W_UKV, a["mla_w_ukv"][l]).then_inc(small, 16)
                for d in range(2):
                    for ct in range(2):
                        at = (d * 2 + ct) * P
                        sp.dma_start(S0B[:, at:at + P].rearrange("p (h n) -> p h n", h=2),
                                     a["state_b_ssm"][0, l, d, 2 * ct:2 * ct + 2].rearrange("h p n -> p h n")).then_inc(small, 16)
                        at //= 2
                        sp.dma_start(S0C[:, at:at + 64],
                                     a["state_c_hgrn"][0, l, d, 2 * ct:2 * ct + 2].rearrange("h k v -> (h k) v")).then_inc(small, 16)
                sp.dma_start(CKT[:, 0:P], a["cache_a_ckv"][0, l]).then_inc(small, 16)
                sp.dma_start(CKT[:, P + NOPE:P + QK_A], a["cache_a_krope"][0, l]).then_inc(small, 16)
                sp.dma_start(CKT[:, 2 * P:3 * P], a["cache_d_k"][0, l].rearrange("t h d -> t (h d)")).then_inc(small, 16)

                def fill(name, pieces):
                    n = number[name]
                    if n >= 2:
                        sp.wait_ge(s["w_used"], n - 1)
                    for dst, src in pieces:
                        sp.dma_start(dst, src).then_inc(w_loaded[n % 2], 16)

                w_mod = a["w_mod"][l].rearrange("(k p) c -> p k c", p=P)
                w_in = a["w_in"][l].rearrange("(k p) c -> p k c", p=P)
                w_out = a["w_out"][l].rearrange("(k p) c -> p k c", p=P)
                for i in range(18):
                    fill(f"mod{i}", [(w_slot(f"mod{i}", 8, 512), w_mod[:, :, i * 512:(i + 1) * 512])])

                def fill_ffn(sub):
                    w_gu = a["ffn_w_gu"][l, sub // 2].rearrange("(k p) (w c) -> p k w c", p=P, w=2)
                    w_dn = a["ffn_w_down"][l, sub // 2].rearrange("(k p) c -> p k c", p=P)
                    base = number[f"gu{sub}.0"]

                    def pair(n_slot, col):
                        dst = W[:, n_slot, :].rearrange("p (w k c) -> p w k c", w=2, k=8)
                        for w in range(2):
                            sp.dma_start(dst[:, w], w_gu[:, :, w, bass.ds(col, 256)]).then_inc(w_loaded[n_slot], 16)

                    with sp.Fori(0, FT // 4) as i:
                        for c in range(2):
                            sp.wait_ge(s["w_used"], i * 2 + (base + c - 1))
                            pair((base + c) % 2, i * 512 + c * 256)
                    last = FT // 2 - 1
                    sp.wait_ge(s["w_used"], base + last - 1)
                    pair((base + last) % 2, last * 256)
                    for m in range(KT_M):
                        fill(f"dn{sub}.{m}", [(w_slot(f"dn{sub}.{m}", FT, P), w_dn[:, :, m * P:(m + 1) * P])])

                fill_ffn(0)
                fill("zx", [(w_slot("zx", 8, 512), w_in[:, :, C_Z:C_Z + 512])])
                pieces = []
                for g in range(4):
                    for dup in range(2):
                        at = (2 * g + dup) * 64
                        pieces.append((w_slot("bc", 8, 512)[:, :, at:at + 64], w_in[:, :, C_BC + g * 64:C_BC + g * 64 + 64]))
                fill("bc", pieces)
                fill("qf", [(w_slot("qf", 8, 512), w_in[:, :, C_CQH:C_CQH + 512])])
                fill("fi", [(w_slot("fi", 8, 512), w_in[:, :, C_FB:C_FB + 512])])
                fill("g", [(w_slot("g", 8, 256), w_in[:, :, C_G:C_G + 256])])
                fill("a", [(w_slot("a", 8, 352), w_in[:, :, 0:352])])
                pieces = []
                for h in range(4):
                    at = (2 * (h % 2) + h // 2) * 64
                    pieces.append((w_slot("d", 8, 512)[:, :, at:at + 64], w_in[:, :, C_DQ + h * 64:C_DQ + h * 64 + 64]))
                pieces.append((w_slot("d", 8, 512)[:, :, 256:512], w_in[:, :, C_DK:C_DK + 256]))
                fill("d", pieces)
                sp.wait_ge(s["mixed_ready"], 2)
                sp.dma_start(VD[:, 5, :], a["cache_d_v"][0, l].rearrange("t h d -> t (h d)")).then_inc(s["pool_load"], 16)
                for i in range(2):
                    fill(f"o{i}", [(w_slot(f"o{i}", 8, 512), w_out[:, :, i * 512:(i + 1) * 512])])
                fill_ffn(2)

                for d in range(2):
                    for ct in range(2):
                        at = (d * 2 + ct) * P
                        sp.wait_ge(s["ft_ready"], 1)
                        sp.dma_start(a["out_b"][0, l, d, 2 * ct:2 * ct + 2].rearrange("h p n -> p h n"),
                                     FINT[:, at:at + P].rearrange("p (h n) -> p h n", h=2)).then_inc(s["state_store"], 16)
                        at //= 2
                        sp.wait_ge(s["fin_out"], 2)
                        sp.dma_start(a["out_c"][0, l, d, 2 * ct:2 * ct + 2].rearrange("h k v -> (h k) v"),
                                     FIN[:, at:at + 64]).then_inc(s["state_store"], 16)
                sp.wait_ge(s["new_ready"], 1)
                sp.dma_start(a["out_ckv"][0, l], NEWROWS[:, 0:P]).then_inc(s["small_store"], 16)
                sp.dma_start(a["out_dk"][0, l].rearrange("t h d -> t (h d)"), NEWROWS[:, P:2 * P]).then_inc(s["small_store"], 16)
                sp.dma_start(a["out_krope"][0, l], NEWROWS[:, 2 * P + NOPE:2 * P + QK_A]).then_inc(s["small_store"], 16)
                sp.dma_start(a["out_dv"][0, l].rearrange("t h d -> t (h d)"), NEWROWS[:, 2 * P + QK_A:]).then_inc(s["small_store"], 16)
                sp.wait_ge(s["state_store"], 128)
                sp.wait_ge(s["small_store"], 64)
                sp.wait_ge(arrived, 4)
                for x in layer_sems:
                    sp.sem_clear(x)
                sp.sem_clear(arrived)
                sp.sem_inc(go, 1)

            for t in range(NCH):
                sp.wait_ge(fin_copy, 2 * t + 2)
                dst = a["y_s"][0, t * P:(t + 1) * P, :] if t < 4 else a["y_p"][0]
                sp.dma_start(dst, XIN[:, t, :]).then_inc(fin_store, 16)
            sp.wait_ge(fin_store, 16 * NCH)

        @blockctx.tensor
        def _(pe):
            mm = nc.tensor.matmul
            pe.wait_ge(init_load, 112)
            for n in range(2 * NCH):
                t, half = n // 2, n % 2
                if n >= 4:
                    pe.wait_ge(init_copy, n - 3)
                for k in range(4):
                    ins = nc.tensor.transpose(banks[:, n % 4, k * P:(k + 1) * P],
                                              XIN[:, t, (half * 4 + k) * P:(half * 4 + k + 1) * P], ident)
                ins.then_inc(init_turn, 1)
            nc.tensor.transpose(banks[:, 4, 0:8], LBR, ident[0:8, 0:8]).then_inc(init_turn, 1)
            pe.wait_ge(init_copy, 2 * NCH + 1)

            with pe.Fori(0, DEPTH) as l:
                def slot_free(j):
                    if j >= 2:
                        pe.wait_ge(freed[j % 2], j // 2)

                def weights(name):
                    pe.wait_ge(w_loaded[number[name] % 2], loaded_at[number[name]])

                def product(out, pairs):
                    for i, (lhs, rhs) in enumerate(pairs):
                        ins = mm(out, lhs, rhs, start=i == 0, stop=i == len(pairs) - 1)
                    return ins

                def dense(name, w, c0, m, src, kt, last=False):
                    j = job[name]
                    slot_free(j)
                    for b, t0, n in SEGS:
                        ins = product(banks[0:m, slot(j) + b, 0:n],
                                      [(w[:, k, c0:c0 + m], src[:, k, t0:t0 + n]) for k in range(kt)])
                    ins.then_inc(s["done"], 1)

                def used():
                    pe.wait_ge(s["done"], dense_count[0])
                    pe.sem_inc(s["w_used"], 1)

                dense_count = [0]

                def run(name, *args):
                    dense(name, *args)
                    dense_count[0] = job[name] + 1

                pe.wait_ge(s["par_load"], 16 * N_SMALL)
                nc.tensor.transpose(banks[:, 7, 0:ROWS1], PR1[0:ROWS1, :], ident[0:ROWS1, 0:ROWS1])
                nc.tensor.transpose(banks[:, 7, P:P + ROWS2], PR2[0:ROWS2, :], ident[0:ROWS2, 0:ROWS2]).then_inc(s["par_turned"], 1)
                pe.wait_ge(s["cond_ready"], 1)
                for i in range(18):
                    weights(f"mod{i}")
                    w = w_slot(f"mod{i}", 8, 512)
                    for m in range(4):
                        at = (4 * i + m) * 2
                        ins = product(banks[:, 6, at:at + 2], [(w[:, k, m * P:(m + 1) * P], SC[:, k, :]) for k in range(8)])
                    ins.then_inc(s["mod_acc"], 1)
                    pe.wait_ge(s["mod_acc"], i + 1)
                    pe.sem_inc(s["w_used"], 1)

                def ffn(sub):
                    base, fbase = job[f"gu{sub}.0"], number[f"gu{sub}.0"]
                    pe.wait_ge(s["modded"], 8 * (sub + 1))

                    def gate_up(n_slot, jslot, c, src):
                        w = W[:, n_slot, :].rearrange("p (w k c) -> p w k c", w=2, k=8)
                        for g in range(2):
                            for b, t0, n in SEGS:
                                out = banks[:, 3 * jslot + g, 0:n] if b == 0 else banks[:, 3 * jslot + 2, g * P:g * P + n]
                                ins = product(out, [(w[:, g, k, c * P:(c + 1) * P], H[:, k, t0:t0 + n]) for k in range(8)])
                        ins.then_inc(s["done"], 1)

                    per = 32
                    l0 = loaded_at[fbase] - per
                    with pe.Fori(0, FT // 2 - 1, 2) as i:
                        for c in range(2):
                            n = (fbase + c) % 2
                            first = loaded_at[fbase + c]
                            pe.wait_ge(w_loaded[n], i * (per // 2) + first)
                            for f in range(2):
                                jo = 2 * c + f
                                js = (base + jo) % 2
                                pe.wait_ge(freed[js], i + (base + jo) // 2)
                                gate_up(n, js, f, H)
                            pe.wait_ge(s["done"], i * 2 + (base + 2 * c + 2))
                            pe.sem_inc(s["w_used"], 1)
                    last = FT // 2 - 1
                    pe.wait_ge(w_loaded[(fbase + last) % 2], loaded_at[fbase + last])
                    for f in range(2):
                        j = base + 2 * last + f
                        slot_free(j)
                        gate_up((fbase + last) % 2, j % 2, f, H)
                    pe.wait_ge(s["done"], base + FT)
                    pe.sem_inc(s["w_used"], 1)
                    for p in range(2):
                        js = [j for j in range(base + FT) if j % 2 == p]
                        pe.wait_ge(freed[p], len(js))
                    for m in range(KT_M):
                        weights(f"dn{sub}.{m}")
                        run(f"dn{sub}.{m}", w_slot(f"dn{sub}.{m}", FT, P), 0, P, HID, FT)
                        used()

                def layer_norm(sub, last_job):
                    for p in range(2):
                        pe.wait_ge(freed[p], len([j for j in range(job[last_job] + 1) if j % 2 == p]))
                    for b, t0, n in SEGS:
                        ins = product(banks[:, 6 + b // 2, 0:n], [(ones, X[:, k, t0:t0 + n]) for k in range(8)])
                    ins.then_inc(s["mean_ready"], 1)
                    pe.wait_ge(s["squared"], 2 * sub + 2)
                    for b, t0, n in SEGS:
                        ins = product(banks[:, 6 + b // 2, 0:n], [(ones, SQX[:, k, t0:t0 + n]) for k in range(8)])
                    ins.then_inc(s["var_ready"], 1)

                ffn(0)
                layer_norm(0, "dn0.7")

                pe.wait_ge(s["modded"], 16)
                weights("zx")
                w = w_slot("zx", 8, 512)
                run("x0", w, 256, P, H, 8)
                run("x1", w, 384, P, H, 8)
                weights("bc")
                w2 = w_slot("bc", 8, 512)
                for g, name in enumerate(("b0", "b1", "c0", "c1")):
                    run(name, w2, g * P, P, H, 8)
                run("z0", w, 0, P, H, 8)
                run("z1", w, P, P, H, 8)
                used()
                pe.sem_inc(s["w_used"], 1)
                run("dt", W_DT, 0, 8, H, 8)
                pe.wait_ge(s["bc_ready"], 2)
                for c in range(NCH):
                    if c >= 2:
                        pe.wait_ge(s["v_ready"], c - 1)
                    for ct in range(2):
                        ins = nc.tensor.transpose(banks[:, 6 + c % 2, ct * P:(ct + 1) * P], XT[:, ct, c * P:(c + 1) * P], ident)
                    ins.then_inc(s["xt_turned"], 1)
                pe.wait_ge(s["dt_ready"], 1)
                for d in range(4):
                    j = job[f"sel{d}"]
                    slot_free(j)
                    mm(banks[:, slot(j), :], sel[:, d, :], DT_B[:, 0, 0:LAT], start=True, stop=True)
                    mm(banks[:, slot(j) + 1, :], sel[:, d, :], DT_B[:, 1, 0:LAT], start=True, stop=True)
                    mm(banks[:, slot(j) + 2, 0:P], sel[:, d, :], DT_B[:, 0, LAT:TOK], start=True, stop=True)
                    mm(banks[:, slot(j) + 2, P:2 * P], sel[:, d, :], DT_B[:, 1, LAT:TOK], start=True, stop=True).then_inc(s["done"], 1)

                def gla(mx):
                    pe.wait_ge(s["gla_act"], mx + 1)
                    for p in range(2):
                        pe.wait_ge(freed[p], len([j for j in range(job[f"y{mx}"]) if j % 2 == p]))
                    for lev in range(LEVELS + 1):
                        if lev == 0:
                            pe.wait_ge(s["level_k"], mx + 1)
                            q, k = Q, KL
                        else:
                            pe.wait_ge(s["prods"], 3 * (LEVELS * mx + lev))
                            q, k = QL, KL
                        for c in range(NCH):
                            n = (mx * (LEVELS + 1) + lev) * NCH + c
                            if n - mx * (LEVELS + 1) * NCH >= 3:
                                pe.wait_ge(s["att_used"], n - 2)
                            for h in (0, 2, 1, 3):
                                rows = slice(64 * (h % 2), 64 * (h % 2) + 64)
                                cols = slice(c * P, (c + 1) * P)
                                ins = mm(banks[:, 2 * (n % 3) + h % 2, (h // 2) * P:(h // 2 + 1) * P], k[rows, h // 2, cols],
                                         q[rows, h // 2, cols], start=True, stop=True)
                            ins.then_inc(s["att_done"], 1)
                    pe.wait_ge(s["fin_prod"], 4 * (mx + 1))
                    pe.wait_ge(s["att_used"], (mx + 1) * (LEVELS + 1) * NCH)
                    for c in range(NCH):
                        if c >= 4:
                            pe.wait_ge(s["k_copied"], NCH * mx + c - 3)
                        for d in range(4):
                            ins = nc.tensor.transpose(banks[:, c % 4, d * P:(d + 1) * P], (KF, KB)[d // 2][:, d % 2, c * P:(c + 1) * P], ident)
                        ins.then_inc(s["k_turned"], 1)
                    if mx == 0:
                        for d in range(4):
                            ins = nc.tensor.transpose(banks[:, 6, d * 64:(d + 1) * 64], S0B[:, d * P:(d + 1) * P], ident[0:64, 0:64])
                        ins.then_inc(s["s0_turned"], 1)
                    pe.wait_ge(s["k_copied"], NCH * (mx + 1))
                    for t in range(4):
                        if t >= 2:
                            pe.wait_ge(s["cs_used"], 4 * mx + t - 1)
                        for d in range(4):
                            c = 4 if t == 3 else (t, 3 - t)[d // 2]
                            ct = d % 2
                            ins = mm(banks[:, 4 + t % 2, d * P:(d + 1) * P], KTOK[:, c, d, :], V[:, c, ct * P:(ct + 1) * P], start=True, stop=True)
                        ins.then_inc(s["cs_done"], 1)
                    if mx == 0:
                        pe.wait_ge(s["fin_out"], 1)
                        pe.wait_ge(s["s0_ready"], 1)
                        for d in range(4):
                            ins = nc.tensor.transpose(banks[0:64, 6, d * P:(d + 1) * P], FIN[:, d * 64:(d + 1) * 64], ident)
                        ins.then_inc(s["ft_turned"], 1)
                    pe.wait_ge(s["sin_ready"], mx + 1)
                    j = job[f"y{mx}"]
                    b0 = slot(j)
                    for ct in range(2):
                        for c in range(NCH):
                            out = banks[:, b0 + ct, c * P:(c + 1) * P] if c < 4 else banks[:, b0 + 2, ct * P:(ct + 1) * P]
                            for hh in range(2):
                                h = 2 * ct + hh
                                ins = mm(out[64 * hh:64 * hh + 64], V[:, c, h * 64:(h + 1) * 64], ATT[:, c, 2 * hh + ct, :],
                                         start=True, stop=c == 4, skip_group_check=True)
                            if c < 4:
                                cols = slice(c * P, (c + 1) * P)
                                mm(out, SIN[:, c, ct, :], PF[:, ct, cols], start=False, stop=False, skip_group_check=True)
                                ins = mm(out, SIN[:, c, 2 + ct, :], SI[:, ct, cols], start=False, stop=True, skip_group_check=True)
                    ins.then_inc(s["done"], 1)
                    pe.wait_ge(s["ysq"], mx + 1)
                    j = job[f"ms{mx}"]
                    slot_free(j)
                    for ct in range(2):
                        mm(banks[:, slot(j) + ct, :], block1, SQ[:, ct, 0:LAT], start=True, stop=True)
                        ins = mm(banks[:, slot(j) + 2, ct * P:(ct + 1) * P], block1, SQ[:, ct, LAT:TOK], start=True, stop=True)
                    ins.then_inc(s["done"], 1)
                    pe.wait_ge(s["mixed_ready"], mx + 1)

                gla(0)
                weights("qf")
                w = w_slot("qf", 8, 512)
                for m, name in enumerate(("hq0", "hq1", "f0", "f1")):
                    run(name, w, m * P, P, H, 8)
                used()
                weights("fi")
                w = w_slot("fi", 8, 512)
                run("f2", w, 0, P, H, 8)
                run("f3", w, P, P, H, 8)
                j = job["iv"]
                slot_free(j)
                for c in range(NCH):
                    out = banks[:, slot(j) + c // 2, (c % 2) * 256:(c % 2) * 256 + 256]
                    ins = product(out, [(H[:, k, c * P:(c + 1) * P], w[:, k, 256:512]) for k in range(8)])
                ins.then_inc(s["done"], 1)
                dense_count[0] = j + 1
                used()
                weights("g")
                run("g0", w_slot("g", 8, 256), 0, P, H, 8)
                run("g1", w_slot("g", 8, 256), P, P, H, 8)
                used()
                gla(1)

                weights("a")
                w = w_slot("a", 8, 352)
                run("cq0", w, 0, P, H, 8)
                run("cq1", w, P, 64, H, 8)
                run("ckv", w, C_CKV, P, H, 8)
                run("kr", w, 256, QK_A, H, 8)
                used()
                j = job["msq"]
                slot_free(j)
                pe.wait_ge(s["aq_sq"], 2)
                for b, t0, n in SEGS:
                    mm(banks[:, slot(j) + b, 0:n], ones, SQA[:, 0, t0:t0 + n], start=True, stop=False)
                    ins = mm(banks[:, slot(j) + b, 0:n], ones[0:64, :], SQA[0:64, 1, t0:t0 + n], start=False, stop=True)
                ins.then_inc(s["done"], 1)
                j = job["mskv"]
                slot_free(j)
                pe.wait_ge(s["aq_sq"], 3)
                for b, t0, n in SEGS:
                    ins = mm(banks[:, slot(j) + b, 0:n], ones, SQA[:, 0, t0:t0 + n], start=True, stop=True)
                ins.then_inc(s["done"], 1)
                pe.wait_ge(s["akv_norm"], 1)
                nc.tensor.transpose(banks[:, 7, 0:P], CKT[:, 0:P], ident)
                nc.tensor.transpose(banks[0:QK_A, 7, P:2 * P], CKT[:, P:P + QK_A], ident)
                nc.tensor.transpose(banks[:, 7, 2 * P:3 * P], CKT[:, 2 * P:3 * P], ident).then_inc(s["cache_turned"], 1)
                pe.wait_ge(s["aq_norm"], 2)
                for h in range(4):
                    j = job[f"q{h}"]
                    slot_free(j)
                    cols = slice(h * QK_A, (h + 1) * QK_A)
                    for b, t0, n in SEGS:
                        out = banks[0:QK_A, slot(j) + b, 0:n]
                        mm(out, W_UQ[:, 0, cols], CQN[:, 0, t0:t0 + n], start=True, stop=False)
                        ins = mm(out, W_UQ[0:64, 1, cols], CQN[0:64, 1, t0:t0 + n], start=False, stop=True)
                    ins.then_inc(s["done"], 1)
                pe.wait_ge(s["cache_ready"], 1)
                for h in range(4):
                    j = job[f"k{h}"]
                    slot_free(j)
                    wk = W_UKV[:, h * P:h * P + NOPE]
                    mm(banks[0:NOPE, slot(j), :], wk, CKN[:, 0:LAT], start=True, stop=True)
                    mm(banks[0:NOPE, slot(j) + 2, 0:256], wk, CKN[:, LAT:EXT], start=True, stop=True).then_inc(s["done"], 1)
                j = job["va"]
                slot_free(j)
                wv = W_UKV.rearrange("p (h w c) -> p h w c", h=4, w=2)[:, :, 1, :]
                for c in range(6):
                    out = banks[:, slot(j) + c // 2, (c % 2) * 256:(c % 2) * 256 + 256]
                    ins = mm(out, CKN[:, c * P:(c + 1) * P], wv, start=True, stop=True)
                ins.then_inc(s["done"], 1)
                weights("d")
                w = w_slot("d", 8, 512)
                for m, name in enumerate(("qd0", "qd1", "kd")):
                    run(name, w, m * P, P, H, 8)
                j = job["vd"]
                slot_free(j)
                for c in range(NCH):
                    out = banks[:, slot(j) + c // 4, (c % 4) * P:(c % 4) * P + P]
                    ins = product(out, [(H[:, k, c * P:(c + 1) * P], w[:, k, 384:512]) for k in range(8)])
                ins.then_inc(s["done"], 1)
                dense_count[0] = j + 1
                used()
                pe.wait_ge(s["attn_in_act"], 1)
                nc.tensor.transpose(banks[:, 7, 0:P], CKN[:, LAT:TOK], ident)
                nc.tensor.transpose(banks[:, 7, P:2 * P], KD[:, LAT:TOK], ident)
                nc.tensor.transpose(banks[:, 7, 2 * P:2 * P + QK_A], KR[0:QK_A, LAT:TOK], ident[0:QK_A, 0:QK_A]).then_inc(s["new_turned"], 1)
                for n, (ap, rows) in enumerate(rotated):
                    if n >= 1:
                        pe.wait_ge(s["rot_used"], n)
                    mm(banks[0:rows, 6, :], (cc("swap_a", QK_A) if rows == QK_A else cc("swap_d")), ap, start=True, stop=True).then_inc(s["rot_done"], 1)

                def score(u):
                    un = units[u]
                    sl = 2 * (u % 2)
                    if u >= 2:
                        pe.wait_ge(s["expd"], u - 1)
                    if un["kind"] == "A":
                        q = QA[0:QK_A, un["h"], un["q"]:un["q"] + P]
                        key = KA[0:QK_A, un["h"], :]
                    else:
                        rows = slice(64 * (un["h"] // 2), 64 * (un["h"] // 2) + 64)
                        q = QD[rows, un["h"] % 2, un["q"]:un["q"] + P]
                        key = KD[rows, :]
                    n = (un["hi"] - un["lo"]) * P
                    flat = banks[:, sl:sl + 2, :].rearrange("p b n -> p (b n)")
                    if un["cache"]:
                        ins = mm(flat[:, n:n + P], q, key[:, TOK:EXT], start=True, stop=True)
                    masked = []
                    if un["kind"] == "D" and un["cache"]:
                        if un["t"] > 0:
                            masked.append((0, cc("far_before")))
                        if un["t"] < 3:
                            masked.append((n - P, cc("far_after")))
                    ins = mm(flat[:, 0:n], q, key[:, un["lo"] * P:un["hi"] * P], start=True, stop=not masked, skip_group_check=True)
                    for i, (at, m) in enumerate(masked):
                        ins = mm(flat[:, at:at + P], ident, m, start=False, stop=i == len(masked) - 1, skip_group_check=True)
                    ins.then_inc(s["scored"], 1)

                pe.wait_ge(s["roped"], 8)
                pe.wait_ge(s["kcopied"], 2)
                pe.wait_ge(s["new_ready"], 1)
                pe.wait_ge(s["pool_load"], 16)
                for p in range(2):
                    pe.wait_ge(freed[p], len([j for j in range(job["o0"]) if j % 2 == p]))
                score(0)
                score(1)
                for u, un in enumerate(units):
                    pe.wait_ge(s["normed_p"], u + 1)
                    if u >= 1:
                        pe.wait_ge(s["p_copied"], u)
                    pt = banks[:, 4:6, :].rearrange("p b n -> p (b n)")
                    for i in range(len(un["tiles"])):
                        ins = nc.tensor.transpose(pt[:, i * P:(i + 1) * P], PRB[:, u % 2, i * P:(i + 1) * P], ident)
                    ins.then_inc(s["p_turned"], 1)
                    if u + 2 < len(units):
                        score(u + 2)
                    pe.wait_ge(s["p_copied"], u + 1)
                    if u >= 2:
                        pe.wait_ge(s["pv_used"], u - 1)
                    h = un["h"]
                    rows = slice(64 * (h % 2), 64 * (h % 2) + 64)
                    v = [VA[:, t, h * 64:(h + 1) * 64] if un["kind"] == "A" else VD[:, t, (h // 2) * 64:(h // 2) * 64 + 64]
                         for t in un["tiles"]]
                    product(banks[rows, 6 + u % 2, 0:P],
                            [(vt, PTS[:, u % 2, i * P:(i + 1) * P]) for i, vt in enumerate(v)]).then_inc(s["pv_done"], 1)
                pe.wait_ge(s["pv_used"], len(units))

                for m in range(KT_M):
                    if m % 4 == 0:
                        weights(f"o{m // 4}")
                    run(f"o{m}", w_slot(f"o{m // 4}", 8, 512), (m % 4) * P, P, MIX, 8)
                    if m % 4 == 3:
                        used()
                layer_norm(1, "o7")
                ffn(2)
                layer_norm(2, "dn2.7")
                pe.wait_ge(s["affine"], 24)
                pe.sem_inc(arrived, 1)
                pe.wait_ge(go, l + 1)

            for n in range(2 * NCH):
                t, half = n // 2, n % 2
                if n >= 4:
                    pe.wait_ge(fin_copy, n - 3)
                for k in range(4):
                    ins = nc.tensor.transpose(banks[:, n % 4, k * P:(k + 1) * P], X[:, half * 4 + k, t * P:(t + 1) * P], ident)
                ins.then_inc(fin_turn, 1)


        def scale_of(un):
            return float((QK_A if un["kind"] == "A" else 64) ** -0.5)

        def flat(ap):
            return ap.rearrange("p k t -> p (k t)")

        def halves(ap, m):
            v = flat(ap).rearrange("p (b h m) -> p b h m", h=2, m=m)
            return v[:, :, 0, :], v[:, :, 1, :]

        def group_cols(j, b, n, rows=P):
            return banks[0:rows, slot(j) + b, 0:n]

        @blockctx.scalar
        def _(act):
            def f(out, in_, func=ACT.Copy, **kw):
                return nc.scalar.activation(out, in_, func, **kw)

            act.wait_ge(init_lb, 1)
            f(LBT[:], LBT[:], ACT.Exp).then_inc(init_lb, 1)

            with act.Fori(0, DEPTH) as l:
                link = chain(act, s["act_chain"])

                def finish(ins, signal, value):
                    ins.then_inc(signal, 1)
                    act.wait_ge(signal, value)

                def evacuate(name, dsts, func=ACT.Copy, rows=P, **kw):
                    j = job[name]
                    act.wait_ge(s["done"], j + 1)
                    for src, dst in dsts:
                        ins = f(dst, src, func, **kw)
                    ins.then_inc(freed[j % 2], 1)

                def both(name, dst, rows=P):
                    j = job[name]
                    return [(group_cols(j, b, n, rows), dst[:, t0:t0 + n]) for b, t0, n in SEGS]

                act.wait_ge(s["par_ready"], 1)
                f(SC, PT2[:, R_C:R_C + 16].rearrange("p (g k) -> p k g", g=2), ACT.Silu).then_inc(s["cond_ready"], 1)
                f(DTP[:, 2:3], DTP[:, 1:2], ACT.Exp).then_inc(s["dt_step"], 1)

                def modulate(sub):
                    act.wait_ge(s["mod_ready"], 1)
                    for m in range(KT_M):
                        if sub:
                            act.wait_ge(s["affine"], 8 * (sub - 1) + m + 1)
                        for g, (b, t0, n) in enumerate(SEGS):
                            ins = f(H[:, m, t0:t0 + n], X[:, m, t0:t0 + n], ACT.Identity,
                                    scale=MOD[:, sub, 1, m, g:g + 1], bias=MOD[:, sub, 0, m, g:g + 1])
                        ins.then_inc(s["modded"], 1)

                def ffn(sub):
                    base = job[f"gu{sub}.0"]
                    with act.Fori(0, FT, 2) as i:
                        for c in range(2):
                            b0 = 3 * ((base + c) % 2)
                            act.wait_ge(s["done"], i + (base + c + 1))
                            f(GATE[:, c, 0:LAT], banks[:, b0, :], ACT.Silu)
                            f(GATE[:, c, LAT:TOK], banks[:, b0 + 2, 0:P], ACT.Silu).then_inc(s["gated"], 1)

                def layer_norm(sub):
                    act.wait_ge(s["centred"], 2 * sub + 2)
                    for hf in range(2):
                        f(SQX[:, 4 * hf:4 * hf + 4, :], X[:, 4 * hf:4 * hf + 4, :], ACT.Square).then_inc(s["squared"], 1)
                    act.wait_ge(s["var_ready"], sub + 1)
                    for b, t0, n in SEGS:
                        link(f(RS[:, t0:t0 + n], banks[:, 6 + b // 2, 0:n], ACT.Ln, scale=1.0 / D_MODEL, bias=eps))
                    finish(f(RS[:], RS[:], ACT.Exp, scale=-0.5), s["rstd"], sub + 1)

                modulate(0)
                ffn(0)
                layer_norm(0)
                modulate(1)

                act.wait_ge(s["pads"], 1)
                conv_jobs = ("x0", "x1", "b0", "b1", "c0", "c1")
                conv_dst = (XT[:, 0], XT[:, 1], BB[:, 0], BB[:, 1], Q[:, 0], Q[:, 1])

                def conv_silu(i):
                    act.wait_ge(s["conv_out"], i + 1)
                    bias = PT2[:, R_CB + i:R_CB + i + 1]
                    f(conv_dst[i][:, 0:LAT], CONV[:, 0:LAT], ACT.Silu, bias=bias)
                    finish(f(conv_dst[i][:, LAT:TOK], CONV[:, LAT + 4:644], ACT.Silu, bias=bias), s["bc_ready"], i + 1)

                for i, name in enumerate(conv_jobs):
                    j = job[name]
                    act.wait_ge(s["done"], j + 1)
                    if i >= 2:
                        act.wait_ge(s["conv_out"], i - 1)
                    f(CPAD[:, i % 2, 2:2 + LAT], group_cols(j, 0, LAT))
                    finish(f(CPAD[:, i % 2, 6 + LAT:6 + TOK], group_cols(j, 2, CTX)), s["conv_in"], i + 1)
                    act.sem_inc(freed[j % 2], 1)
                    if i >= 1:
                        conv_silu(i - 1)
                conv_silu(5)
                for ct in range(2):
                    evacuate(f"z{ct}", both(f"z{ct}", ZS[:, ct]), ACT.Silu)
                r, e, w1, lg = (DTW[:, k, :] for k in range(4))
                act.wait_ge(s["dt_step"], 2)
                link(f(e, r, ACT.Abs))
                finish(f(e, e, ACT.Exp, scale=-1.0), s["dt_step"], 3)
                act.wait_ge(s["dt_step"], 4)
                finish(f(lg, w1, ACT.Ln), s["dt_step"], 5)
                for c in range(NCH):
                    act.wait_ge(s["xt_turned"], c + 1)
                    finish(f(V[:, c, :], banks[:, 6 + c % 2, 0:256]), s["v_ready"], c + 1)
                for d in range(4):
                    j = job[f"sel{d}"]
                    act.wait_ge(s["done"], j + 1)
                    dst = (PF, SI)[d // 2][:, d % 2]
                    f(dst[:, 0:LAT], banks[:, slot(j) + 1, :])
                    finish(f(dst[:, LAT:TOK], banks[:, slot(j) + 2, P:2 * P]), s["adt_copied"], d + 1)
                act.sem_inc(s["gla_act"], 1)

                def gla(mx):
                    act.wait_ge(s["excl_zero"], mx + 1)
                    for lev in range(1, LEVELS + 1):
                        m = 2 ** (lev - 1)
                        act.wait_ge(s["att_done"], (mx * (LEVELS + 1) + lev) * NCH)
                        if lev > 1:
                            act.wait_ge(s["sums"], 4 * (LEVELS * mx + lev - 1))
                        (q1, q2), (k1, k2) = halves(QL, m), halves(KL, m)
                        for dst, src in ((q1, halves(SI, m)[0]), (q2, halves(PF, m)[1]),
                                         (k1, halves(SE, m)[0]), (k2, halves(PB, m)[1])):
                            f(dst, src, ACT.Exp).then_inc(s["exps"], 1)
                    act.wait_ge(s["sums"], 4 * LEVELS * (mx + 1))
                    ends = lambda ap, i: ap.rearrange("p k (c i) -> p k c i", i=P)[:, :, :, i]
                    link(f(DEC[:, 0], ends(PF, P - 1), ACT.Exp))
                    link(f(DEC[:, 1], ends(SI, 0), ACT.Exp))
                    for ap in (PF, SI, SE, PB):
                        f(ap, ap, ACT.Exp).then_inc(s["fin_exp"], 1)
                    for c in range(NCH):
                        act.wait_ge(s["k_turned"], NCH * mx + c + 1)
                        f(KTOK[:, c], banks[:, c % 4, :].rearrange("p (d n) -> p d n", d=4)).then_inc(s["k_copied"], 1)
                    if mx == 0:
                        act.wait_ge(s["ft_turned"], 1)
                        f(FINT[:], banks[0:64, 6, :]).then_inc(s["ft_ready"], 1)
                    act.wait_ge(s["y_ready"], mx + 1)
                    f(SQ, Y, ACT.Square).then_inc(s["ysq"], 1)
                    j = job[f"ms{mx}"]
                    act.wait_ge(s["done"], j + 1)
                    b0 = slot(j)
                    link(f(RB[:, :, 0:LAT], banks[:, b0:b0 + 2, :], ACT.Ln, scale=1.0 / 64, bias=eps))
                    link(f(RB[:, :, LAT:TOK], banks[:, b0 + 2, 0:256].rearrange("p (k n) -> p k n", k=2), ACT.Ln, scale=1.0 / 64, bias=eps))
                    act.sem_inc(freed[j % 2], 1)
                    f(RB, RB, ACT.Exp, scale=-0.5).then_inc(s["y_rstd"], 1)

                gla(0)
                for ct in range(2):
                    evacuate(f"hq{ct}", both(f"hq{ct}", Q[:, ct]))
                for i in range(4):
                    j = job[f"f{i}"]
                    act.wait_ge(s["done"], j + 1)
                    for b, t0, n in SEGS:
                        f((PF, SI)[i // 2][:, i % 2, t0:t0 + n], group_cols(j, b, n), ACT.Sigmoid)
                        ins = f((KF, KB)[i // 2][:, i % 2, t0:t0 + n], group_cols(j, b, n), ACT.Sigmoid, scale=-1.0)
                    finish(ins, s["f_raw"], i + 1)
                    act.sem_inc(freed[j % 2], 1)
                j = job["iv"]
                b0 = slot(j)
                pair = lambda ap: ap.rearrange("p (c n) -> p c n", n=256)
                evacuate("iv", [(pair(banks[:, b0, :]), V[:, 0:2, :]), (pair(banks[:, b0 + 1, :]), V[:, 2:4, :]),
                                (banks[:, b0 + 2, 0:256], V[:, 4, :])])
                for ct in range(2):
                    evacuate(f"g{ct}", both(f"g{ct}", ZS[:, ct]), ACT.Silu)
                act.wait_ge(s["f_ready"], 4)
                link(f(PF, PF, ACT.Ln))
                link(f(SI, SI, ACT.Ln))
                act.sem_inc(s["gla_act"], 1)
                gla(1)

                evacuate("cq0", both("cq0", CQ[:, 0]))
                evacuate("cq1", both("cq1", CQ[0:64, 1], 64), rows=64)
                evacuate("ckv", both("ckv", KVR))
                evacuate("kr", both("kr", KR[0:QK_A, :], QK_A))
                for p in range(2):
                    act.wait_ge(freed[p], len([j for j in range(job["kr"] + 1) if j % 2 == p]))
                f(SQA[:, 0], CQ[:, 0], ACT.Square).then_inc(s["aq_sq"], 1)
                f(SQA[0:64, 1], CQ[0:64, 1], ACT.Square).then_inc(s["aq_sq"], 1)
                for n, (name, size) in enumerate((("msq", Q_RANK), ("mskv", KV_RANK))):
                    j = job[name]
                    act.wait_ge(s["done"], j + 1)
                    if n == 0:
                        f(SQA[:, 0], KVR, ACT.Square).then_inc(s["aq_sq"], 1)
                    else:
                        act.wait_ge(s["aq_norm"], 2)
                    for b, t0, k in SEGS:
                        link(f(RA[:, t0:t0 + k], group_cols(j, b, k), ACT.Ln, scale=1.0 / size, bias=eps))
                    act.sem_inc(freed[j % 2], 1)
                    finish(f(RA, RA, ACT.Exp, scale=-0.5), s["aq_rstd"], n + 1)
                act.wait_ge(s["cache_turned"], 1)
                link(f(CKN[:, TOK:EXT], banks[:, 7, 0:P]))
                link(f(KR[0:QK_A, TOK:EXT], banks[0:QK_A, 7, P:2 * P]))
                finish(f(KD[:, TOK:EXT], banks[:, 7, 2 * P:3 * P]), s["cache_ready"], 1)
                for h in range(4):
                    evacuate(f"q{h}", both(f"q{h}", QA[0:QK_A, h], QK_A))
                for h in range(4):
                    b0 = slot(job[f"k{h}"])
                    evacuate(f"k{h}", [(banks[0:NOPE, b0, :], KA[0:NOPE, h, 0:LAT]), (banks[0:NOPE, b0 + 2, 0:256], KA[0:NOPE, h, LAT:EXT])])
                b0 = slot(job["va"])
                evacuate("va", [(pair(banks[:, b0 + i, :]), VA[:, 2 * i:2 * i + 2, :]) for i in range(3)])
                evacuate("qd0", both("qd0", QD[:, 0]))
                evacuate("qd1", both("qd1", QD[:, 1]))
                evacuate("kd", both("kd", KD[:, 0:TOK]))
                b0 = slot(job["vd"])
                evacuate("vd", [(banks[:, b0, :].rearrange("p (c n) -> p c n", n=P), VD[:, 0:4, :]), (banks[:, b0 + 1, 0:P], VD[:, 4, :])])
                for p in range(2):
                    act.wait_ge(freed[p], len([j for j in range(job["vd"] + 1) if j % 2 == p]))
                act.sem_inc(s["attn_in_act"], 1)
                link(f(NEWROWS[:, 2 * P + QK_A:], VD[:, 4, :]))
                act.wait_ge(s["new_turned"], 1)
                finish(f(NEWROWS[:, 0:2 * P + QK_A], banks[:, 7, 0:2 * P + QK_A]), s["new_ready"], 1)
                act.wait_ge(s["roped"], 5)
                for i in range(2):
                    f(KA[NOPE:QK_A, 2 * i:2 * i + 2, :], bc(KR[NOPE:QK_A, :].unsqueeze(1), [ROPE, 2, EXT])).then_inc(s["kcopied"], 1)

                def probs(u):
                    un = units[u]
                    n = len(un["tiles"]) * P
                    sc = SM[:, u % 8, :]
                    act.wait_ge(s["maxed"], u + 1)
                    if u >= 2:
                        act.wait_ge(s["p_turned"], u - 1)
                    src = banks[:, 2 * (u % 2):2 * (u % 2) + 2, :].rearrange("p b n -> p (b n)")[:, 0:n]
                    if un["kind"] == "D":
                        f(sc[:, 3:4], SINK[:, un["h"]:un["h"] + 1], ACT.Exp, bias=sc[:, 1:2])
                    f(PRB[:, u % 2, 0:n], src, ACT.Exp, scale=scale_of(un), bias=sc[:, 1:2], accum_out=sc[:, 2:3]).then_inc(s["expd"], 1)

                probs(0)
                for u, un in enumerate(units):
                    if u + 1 < len(units):
                        probs(u + 1)
                    n = len(un["tiles"]) * P
                    act.wait_ge(s["p_turned"], u + 1)
                    if u >= 2:
                        act.wait_ge(s["pv_done"], u - 1)
                    f(PTS[:, u % 2, 0:n], banks[:, 4:6, :].rearrange("p b n -> p (b n)")[:, 0:n]).then_inc(s["p_copied"], 1)

                layer_norm(1)
                modulate(2)
                ffn(2)
                layer_norm(2)
                act.sem_inc(arrived, 1)
                act.wait_ge(go, l + 1)

        @blockctx.vector
        def _(dve):
            v = nc.vector
            for n in range(2 * NCH):
                t, half = n // 2, n % 2
                dve.wait_ge(init_turn, n + 1)
                v.tensor_copy(X[:, 4 * half:4 * half + 4, t * P:(t + 1) * P],
                              banks[:, n % 4, :].rearrange("p (k n) -> p k n", k=4)).then_inc(init_copy, 1)
            dve.wait_ge(init_turn, 2 * NCH + 1)
            v.tensor_copy(LBT[:], banks[:, 4, 0:8]).then_inc(init_copy, 1)
            dve.wait_ge(init_copy, 2 * NCH + 1)
            v.tensor_tensor(LBW[:], LBT[:, 0:4], LBT[:, 4:8], ALU.max).then_inc(init_copy, 1)
            dve.wait_ge(init_copy, 2 * NCH + 2)
            v.tensor_tensor(LBT[:].rearrange("p (l c) -> p l c", l=2), LBT[:].rearrange("p (l c) -> p l c", l=2),
                            bc(LBW[:].unsqueeze(1), [P, 2, 4]), ALU.subtract).then_inc(init_lb, 1)
            dve.wait_ge(init_lb, 2)
            v.tensor_tensor(LBW[:], LBT[:, 0:4], LBT[:, 4:8], ALU.add).then_inc(init_lb, 1)
            dve.wait_ge(init_lb, 3)
            v.reciprocal(LBW[:], LBW[:]).then_inc(init_lb, 1)
            dve.wait_ge(init_lb, 4)
            v.tensor_tensor(LBN[:], LBT[:, 4:8], LBW[:], ALU.mult).then_inc(init_lb, 1)
            v.memset(LB[:], 0.0).then_inc(init_lb, 1)
            dve.wait_ge(init_lb, 6)

            with dve.Fori(0, DEPTH) as l:
                link = chain(dve, s["dve_chain"])

                def finish(ins, signal, value):
                    ins.then_inc(signal, 1)
                    dve.wait_ge(signal, value)

                dve.wait_ge(s["par_turned"], 1)
                link(v.tensor_copy(PT1[:], banks[:, 7, 0:ROWS1]))
                finish(v.tensor_copy(PT2[:], banks[:, 7, P:P + ROWS2]), s["par_ready"], 1)
                link(v.tensor_scalar(OML[:], LB[:], -1.0, 1.0, ALU.mult, ALU.add))
                link(v.tensor_scalar(SINK[:, 4:8], SINK[:, 0:4], -1.0, None, ALU.mult))
                for hh in range(2):
                    rows = slice(64 * hh, 64 * hh + 64)
                    sk = SKIP[rows, :].rearrange("p (d c h) -> p d c h", d=2, c=2)
                    link(v.tensor_tensor(DS[rows, :], sk[:, 0, :, hh], sk[:, 1, :, hh], ALU.add))
                dve.wait_ge(s["dt_step"], 1)
                link(v.tensor_scalar(DTP[:, 3:4], DTP[:, 2:3], -1.0, None, ALU.mult))
                dve.wait_ge(s["mod_acc"], 18)
                mod = MOD.rearrange("p s w m g -> p (s w m) g")
                link(v.tensor_tensor(mod, banks[:, 6, 0:144].rearrange("p (r g) -> p r g", g=2),
                                     bc(PT1[:, 0:72].unsqueeze(2), [P, 72, 2]), ALU.add))
                for sub in range(3):
                    link(v.tensor_scalar(MOD[:, sub, 1], MOD[:, sub, 1], 1.0, None, ALU.add))
                    if sub != 1:
                        link(v.tensor_scalar(MOD[:, sub, 2], MOD[:, sub, 2], 0.5, None, ALU.mult))
                dve.sem_inc(s["mod_ready"], 1)

                def scale_residual(sub):
                    dve.wait_ge(s["modded"], 8 * (sub + 1))
                    link(v.tensor_scalar(X, X, float(ALPHA), None, ALU.mult))

                def residual(name, sub, m):
                    j = job[name]
                    dve.wait_ge(s["done"], j + 1)
                    for g, (b, t0, n) in enumerate(SEGS):
                        ins = v.scalar_tensor_tensor(out=X[:, m, t0:t0 + n], in0=group_cols(j, b, n), scalar=MOD[:, sub, 2, m, g:g + 1],
                                                     in1=X[:, m, t0:t0 + n], op0=ALU.mult, op1=ALU.add)
                    ins.then_inc(freed[j % 2], 1)

                def ffn(sub):
                    base, g0 = job[f"gu{sub}.0"], (FT if sub else 0)
                    with dve.Fori(0, FT // 2) as i:
                        for c in range(2):
                            b0 = 3 * ((base + c) % 2)
                            dve.wait_ge(s["gated"], i * 2 + (g0 + c + 1))
                            hid = HID.rearrange("p (i c) t -> p i c t", c=2)[:, bass.ds(i, 1), c, :]
                            v.tensor_tensor(hid[:, :, 0:LAT], GATE[:, c:c + 1, 0:LAT], banks[:, b0 + 1:b0 + 2, :], ALU.mult)
                            v.tensor_tensor(hid[:, :, LAT:TOK], GATE[:, c:c + 1, LAT:TOK], banks[:, b0 + 2:b0 + 3, P:2 * P],
                                            ALU.mult).then_inc(freed[(base + c) % 2], 1)
                    for m in range(KT_M):
                        residual(f"dn{sub}.{m}", sub, m)

                def layer_norm(sub):
                    dve.wait_ge(s["mean_ready"], sub + 1)
                    for b, t0, n in SEGS:
                        v.scalar_tensor_tensor(out=X[:, :, t0:t0 + n], in0=bc(banks[:, 6 + b // 2, 0:n].unsqueeze(1), [P, KT_M, n]),
                                               scalar=-1.0 / D_MODEL, in1=X[:, :, t0:t0 + n], op0=ALU.mult, op1=ALU.add).then_inc(s["centred"], 1)
                    dve.wait_ge(s["rstd"], sub + 1)
                    link(v.tensor_tensor(X, X, bc(RS[:].unsqueeze(1), [P, KT_M, TOK]), ALU.mult))
                    for m in range(KT_M):
                        v.tensor_scalar(X[:, m, :], X[:, m, :], PT1[:, R_LNG + 8 * sub + m:R_LNG + 8 * sub + m + 1],
                                        PT1[:, R_LNB + 8 * sub + m:R_LNB + 8 * sub + m + 1], ALU.mult, ALU.add).then_inc(s["affine"], 1)

                scale_residual(0)
                ffn(0)
                layer_norm(0)
                scale_residual(1)

                for i in range(6):
                    dve.wait_ge(s["conv_in"], i + 1)
                    if i >= 1:
                        dve.wait_ge(s["bc_ready"], i)
                    for tap in range(TAPS):
                        src = CPAD[:, i % 2, tap:tap + 644]
                        wt = PT2[:, R_CW + 6 * tap + i:R_CW + 6 * tap + i + 1]
                        if tap == 0:
                            link(v.tensor_scalar(CONV, src, wt, None, ALU.mult))
                        else:
                            ins = v.scalar_tensor_tensor(out=CONV, in0=src, scalar=wt, in1=CONV, op0=ALU.mult, op1=ALU.add)
                            if tap < TAPS - 1:
                                link(ins)
                            else:
                                finish(ins, s["conv_out"], i + 1)
                r, e, w1, lg = (DTW[:, k, :] for k in range(4))
                j = job["dt"]
                dve.wait_ge(s["done"], j + 1)
                for b, t0, n in SEGS:
                    link(v.tensor_scalar(r[:, t0:t0 + n], group_cols(j, b, n, 8), DTP[:, 0:1], None, ALU.add))
                dve.sem_inc(freed[j % 2], 1)
                dve.sem_inc(s["dt_step"], 1)
                dve.wait_ge(s["dt_step"], 3)
                finish(v.tensor_scalar(w1, e, 1.0, None, ALU.add), s["dt_step"], 4)
                dve.wait_ge(s["dt_step"], 5)
                t2 = DT_B[:, 0]
                link(v.tensor_scalar(t2, w1, -1.0, None, ALU.add))
                link(v.tensor_tensor(e, e, t2, ALU.subtract))
                link(v.reciprocal(w1, w1))
                link(v.tensor_tensor(e, e, w1, ALU.mult))
                link(v.tensor_tensor(lg, lg, e, ALU.add))
                link(v.scalar_tensor_tensor(out=DT_B[:, 0], in0=r, scalar=0.0, in1=lg, op0=ALU.max, op1=ALU.add))
                finish(v.tensor_scalar(DT_B[:, 1], DT_B[:, 0], DTP[:, 3:4], None, ALU.mult), s["dt_ready"], 1)
                dve.wait_ge(s["bc_ready"], 6)
                for d in range(4):
                    j = job[f"sel{d}"]
                    dve.wait_ge(s["adt_copied"], d + 1)
                    ct = d % 2
                    for b, t0, n in SEGS:
                        ins = v.tensor_tensor((KF, KB)[d // 2][:, ct, t0:t0 + n], group_cols(j, b, n), BB[:, ct, t0:t0 + n], ALU.mult)
                    ins.then_inc(freed[j % 2], 1)

                def gla(mx):
                    for p in range(2):
                        dve.wait_ge(freed[p], len([j for j in range(job[f"y{mx}"]) if j % 2 == p]))
                    finish(v.tensor_tensor(KL, KF, KB, ALU.add), s["level_k"], mx + 1)

                    def merge(lev):
                        mask = bc(masks[:, lev, :].unsqueeze(1).unsqueeze(1), [P, 2, 2, P])
                        for c in range(NCH):
                            n = (mx * (LEVELS + 1) + lev) * NCH + c
                            dve.wait_ge(s["att_done"], n + 1)
                            v.copy_predicated(ATT[:, c].rearrange("p (a b) n -> p a b n", a=2), mask,
                                              banks[:, 2 * (n % 3):2 * (n % 3) + 2, 0:256].rearrange("p a (b n) -> p a b n", b=2)).then_inc(s["att_used"], 1)

                    merge(0)
                    for lev in range(1, LEVELS + 1):
                        m = 2 ** (lev - 1)
                        at = LEVELS * mx + lev
                        dve.wait_ge(s["exps"], 4 * at)
                        v.tensor_tensor(QL, QL, Q, ALU.mult).then_inc(s["prods"], 1)
                        (k1, k2) = halves(KL, m)
                        v.tensor_tensor(k1, k1, halves(KF, m)[0], ALU.mult).then_inc(s["prods"], 1)
                        v.tensor_tensor(k2, k2, halves(KB, m)[1], ALU.mult).then_inc(s["prods"], 1)
                        merge(lev)
                    dve.wait_ge(s["fin_exp"], 4 * mx + 4)
                    for x, y in ((PF, Q), (SI, Q)):
                        v.tensor_tensor(x, x, y, ALU.mult).then_inc(s["fin_prod"], 1)
                    for x, y in ((KF, SE), (KB, PB)):
                        v.tensor_tensor(x, x, y, ALU.mult).then_inc(s["fin_prod"], 1)
                    dve.wait_ge(s["sin_zero"], mx + 1)
                    if mx == 0:
                        dve.wait_ge(s["s0_turned"], 1)
                        src = banks[:, 6, 0:256].rearrange("p (d n) -> p d n", d=4)
                    else:
                        src = S0C[:].rearrange("p (d n) -> p d n", d=4)
                    for d in range(2):
                        for hh in range(2):
                            rows = slice(64 * hh, 64 * hh + 64)
                            link(v.tensor_copy(SIN[rows, 3 * d, 2 * d:2 * d + 2, rows], src[rows, 2 * d:2 * d + 2, :]))
                    dve.sem_inc(s["s0_ready"], 1)
                    for t in range(4):
                        dve.wait_ge(s["cs_done"], 4 * mx + t + 1)
                        cs = banks[:, 4 + t % 2, :].rearrange("p (d n) -> p d n", d=4)
                        for hh in range(2):
                            rows = slice(64 * hh, 64 * hh + 64)
                            if t == 3:
                                link(v.tensor_copy(FIN[rows, :].rearrange("p (d n) -> p d n", d=4), cs[rows, :, rows]))
                                continue
                            for d in range(4):
                                src_c, dst_c = (t, t + 1) if d < 2 else (3 - t, 2 - t)
                                link(v.scalar_tensor_tensor(out=SIN[rows, dst_c, d, rows], in0=SIN[rows, src_c, d, rows],
                                                            scalar=DEC[rows, d // 2, d % 2, src_c:src_c + 1], in1=cs[rows, d, rows],
                                                            op0=ALU.mult, op1=ALU.add))
                        dve.sem_inc(s["cs_used"], 1)
                    dve.sem_inc(s["fin_out"], 1)
                    dve.sem_inc(s["sin_ready"], 1)
                    j = job[f"y{mx}"]
                    b0 = slot(j)
                    dve.wait_ge(s["done"], j + 1)
                    parts = ((banks[:, b0:b0 + 2, :], slice(0, LAT)), (banks[:, b0 + 2, 0:256].rearrange("p (k n) -> p k n", k=2), slice(LAT, TOK)))
                    for src, cols in parts:
                        if mx == 1:
                            link(v.tensor_copy(Y[:, :, cols], src))
                        else:
                            for ct in range(2):
                                link(v.scalar_tensor_tensor(out=Y[:, ct, cols], in0=XT[:, ct, cols], scalar=DS[:, ct:ct + 1],
                                                            in1=src[:, ct], op0=ALU.mult, op1=ALU.add))
                    dve.sem_inc(freed[j % 2], 1)
                    if mx == 0:
                        link(v.tensor_tensor(Y, Y, ZS, ALU.mult))
                    dve.sem_inc(s["y_ready"], 1)
                    dve.wait_ge(s["y_rstd"], mx + 1)
                    g0 = (R_SN, R_HN)[mx]
                    for ct in range(2):
                        dst = MIX[:, 2 + ct] if mx == 0 else Y[:, ct]
                        link(v.scalar_tensor_tensor(out=dst, in0=Y[:, ct], scalar=PT2[:, g0 + ct:g0 + ct + 1], in1=RB[:, ct],
                                                    op0=ALU.mult, op1=ALU.mult))
                    if mx == 1:
                        link(v.tensor_tensor(MIX[:, 4:6], Y, ZS, ALU.mult))
                    dve.sem_inc(s["mixed_ready"], 1)

                gla(0)
                for i in range(4):
                    dve.wait_ge(s["f_raw"], i + 1)
                    d, ct = i // 2, i % 2
                    lb, oml = LB[:, i:i + 1], OML[:, i:i + 1]
                    fg, key = (PF, SI)[d][:, ct], (KF, KB)[d][:, ct]
                    link(v.tensor_scalar(fg, fg, oml, lb, ALU.mult, ALU.add))
                    link(v.tensor_scalar(key, key, oml, None, ALU.mult))
                    finish(v.tensor_scalar(fg, fg, F_MIN, None, ALU.max), s["f_ready"], i + 1)
                gla(1)

                dve.wait_ge(s["aq_rstd"], 1)
                for ct, rows in ((0, P), (1, 64)):
                    v.scalar_tensor_tensor(out=CQN[0:rows, ct], in0=CQ[0:rows, ct], scalar=PT2[0:rows, R_QN + ct:R_QN + ct + 1],
                                           in1=RA[0:rows], op0=ALU.mult, op1=ALU.mult).then_inc(s["aq_norm"], 1)
                dve.wait_ge(s["aq_rstd"], 2)
                v.scalar_tensor_tensor(out=CKN[:, 0:TOK], in0=KVR, scalar=PT2[:, R_KVN:R_KVN + 1], in1=RA,
                                       op0=ALU.mult, op1=ALU.mult).then_inc(s["akv_norm"], 1)
                for n, (ap, rows) in enumerate(rotated):
                    cos, sin = (cc("cos_a", QK_A), cc("sin_a", QK_A)) if rows == QK_A else (cc("cos_d"), cc("sin_d"))
                    dve.wait_ge(s["rot_done"], n + 1)
                    finish(v.tensor_tensor(ROT[0:rows], banks[0:rows, 6, :], sin, ALU.mult), s["rot_used"], n + 1)
                    link(v.tensor_tensor(ap, ap, cos, ALU.mult))
                    finish(v.tensor_tensor(ap, ap, ROT[0:rows], ALU.add), s["roped"], n + 1)

                def row_max(u):
                    un, sc = units[u], SM[:, u % 8, :]
                    n = len(un["tiles"]) * P
                    src = banks[:, 2 * (u % 2):2 * (u % 2) + 2, :].rearrange("p b n -> p (b n)")[:, 0:n]
                    dve.wait_ge(s["scored"], u + 1)
                    link(v.reduce_max(sc[:, 0:1], src, AX_X))
                    if un["kind"] == "A":
                        ins = v.tensor_scalar(sc[:, 1:2], sc[:, 0:1], -scale_of(un), None, ALU.mult)
                    else:
                        ins = v.tensor_scalar(sc[:, 1:2], sc[:, 0:1], -scale_of(un), SINK[:, 4 + un["h"]:5 + un["h"]], ALU.mult, ALU.min)
                    ins.then_inc(s["maxed"], 1)

                row_max(0)
                for u in range(len(units) + 1):
                    if u + 1 < len(units):
                        row_max(u + 1)
                    if u < len(units):
                        un, sc = units[u], SM[:, u % 8, :]
                        n = len(un["tiles"]) * P
                        dve.wait_ge(s["expd"], u + 1)
                        total = sc[:, 2:3]
                        if un["kind"] == "D":
                            link(v.tensor_tensor(sc[:, 4:5], sc[:, 2:3], sc[:, 3:4], ALU.add))
                            total = sc[:, 4:5]
                        link(v.reciprocal(sc[:, 5:6], total))
                        v.tensor_scalar(PRB[:, u % 2, 0:n], PRB[:, u % 2, 0:n], sc[:, 5:6], None, ALU.mult).then_inc(s["normed_p"], 1)
                    if u >= 1:
                        un = units[u - 1]
                        h = un["h"]
                        rows = slice(64 * (h % 2), 64 * (h % 2) + 64)
                        tile = h // 2 + (0 if un["kind"] == "A" else 6)
                        dve.wait_ge(s["pv_done"], u)
                        v.tensor_copy(MIX[rows, tile, un["q"]:un["q"] + P], banks[rows, 6 + (u - 1) % 2, 0:P]).then_inc(s["pv_used"], 1)
                for m in range(KT_M):
                    residual(f"o{m}", 1, m)
                layer_norm(1)
                scale_residual(2)
                ffn(2)
                layer_norm(2)
                dve.wait_ge(s["affine"], 24)
                link(v.tensor_tensor(LB[:], LB[:], LBN[:], ALU.add))
                dve.sem_inc(arrived, 1)
                dve.wait_ge(go, l + 1)

            for n in range(2 * NCH):
                t, half = n // 2, n % 2
                dve.wait_ge(fin_turn, n + 1)
                v.tensor_copy(XIN[:, t, half * 512:(half + 1) * 512], banks[:, n % 4, :]).then_inc(fin_copy, 1)

        @blockctx.gpsimd
        def _(pool):
            g = nc.gpsimd
            g.memset(CKT[:, P:P + NOPE], 0.0).then_inc(init_ready, 1)
            pool.wait_ge(init_ready, 1)

            with pool.Fori(0, DEPTH) as l:
                link = chain(pool, s["pool_chain"])
                pool.wait_ge(s["modded"], 16)
                for c0, c1 in ((0, 2), (2 + LAT, 6 + LAT), (6 + TOK, 8 + TOK)):
                    link(g.memset(CPAD[:, :, c0:c1], 0.0))
                pool.sem_inc(s["pads"], 1)
                sums_done = [0]
                for mx in range(2):
                    if mx == 1:
                        pool.wait_ge(s["mixed_ready"], 1)
                    link(g.memset(SIN, 0.0))
                    pool.sem_inc(s["sin_zero"], 1)
                    pool.wait_ge(s["gla_act"], mx + 1)
                    pool.wait_ge(s["level_k"], mx + 1)
                    link(g.memset(SE, 0.0))
                    link(g.memset(PB, 0.0))
                    pool.sem_inc(s["excl_zero"], 1)
                    for lev in range(1, LEVELS + 1):
                        m = 2 ** (lev - 1)
                        nb = 2 * TOK // (2 * m)
                        pool.wait_ge(s["exps"], 4 * (LEVELS * mx + lev))
                        (p1, p2), (i1, i2), (e1, _), (_, b2) = (halves(x, m) for x in (PF, SI, SE, PB))
                        wide = lambda ap: bc(ap, [P, nb, m])
                        for dst, add in ((e1, p2[:, :, m - 1:m]), (b2, i1[:, :, 0:1]), (p2, p1[:, :, m - 1:m]), (i1, i2[:, :, 0:1])):
                            ins = g.tensor_tensor(dst, dst, wide(add), ALU.add)
                            ins.then_inc(s["sums"], 1)
                            sums_done[0] += 1
                            pool.wait_ge(s["sums"], sums_done[0])
                pool.sem_inc(arrived, 1)
                pool.wait_ge(go, l + 1)


_INS = ["x_prompt", "x_sample", "cache_a_ckv", "cache_a_krope", "state_b_ssm", "state_c_hgrn", "cache_d_k", "cache_d_v",
        "c", "c_ctx", "w_mod", "b_mod", "ln_g", "ln_b", "ffn_w_gu", "ffn_w_down", "w_in", "w_out", "mla_q_norm",
        "mla_kv_norm", "mla_w_uq", "mla_w_ukv", "ssd_conv_w", "ssd_conv_b", "ssd_a_log", "ssd_dt_bias", "ssd_d",
        "ssd_norm", "hgrn_lb_logits", "hgrn_norm", "gqa_sink"]
_OUTS = [("y_p", (1, CTX, D_MODEL)), ("y_s", (1, LAT, D_MODEL)), ("out_ckv", (1, DEPTH, CTX, KV_RANK)),
         ("out_krope", (1, DEPTH, CTX, ROPE)), ("out_b", (1, DEPTH, 2, 4, 64, 64)), ("out_c", (1, DEPTH, 2, 4, 64, 64)),
         ("out_dk", (1, DEPTH, CTX, 2, 64)), ("out_dv", (1, DEPTH, CTX, 2, 64))]


def kernel(**inputs):
    import concourse.bacc as bacc
    from concourse.bass_utils import run_bass_kernel_spmd

    nc = bacc.Bacc("TRN2", target_bir_lowering=False, num_devices=1)
    consts, const_at = constants()
    arrays, aps = {"in_consts": consts}, {}
    aps["consts"] = nc.dram_tensor("in_consts", consts.shape, F32, kind="ExternalInput").ap()
    for name in _INS:
        x = np.ascontiguousarray(inputs[name])
        arrays[f"in_{name}"] = x
        aps[name] = nc.dram_tensor(f"in_{name}", x.shape, mybir.dt.from_np(x.dtype), kind="ExternalInput").ap()
    for name, shape in _OUTS:
        aps[name] = nc.dram_tensor(name, shape, F32, kind="ExternalOutput").ap()
    trunk_kernel(nc, aps, consts, const_at)
    r = run_bass_kernel_spmd(nc, [arrays], core_ids=[0])
    return tuple(r.results[0][name] for name, _ in _OUTS)
```

```python
from contextlib import ExitStack

import numpy as np
import concourse.bass as bass
from concourse import mybir
from concourse.alu_op_type import AluOpType as ALU

F32 = mybir.dt.float32
F32R = mybir.dt.float32r
I32 = mybir.dt.int32
ACT = mybir.ActivationFunctionType
AX_X = mybir.AxisListType.X

P = 128
D_MODEL, DEPTH, LAT, CTX, PAST = 1024, 2, 512, 128, 128
TOK = LAT + CTX
EXT = TOK + PAST
KT_M = D_MODEL // P
D_FF = 2816
FT = D_FF // P
N_SUB = 3
ALPHA = (2 * DEPTH) ** 0.25
EPS = 1e-6
F_MIN = 1e-6
NEG = -1e30
GRID_W = 64
ROPE_BASE = 10000.0
H_A, NOPE, ROPE, V_A, Q_RANK, KV_RANK = 4, 64, 32, 64, 192, 128
QK_A = NOPE + ROPE
TAPS = 5
NCH = TOK // P
LEVELS = 7
SLOT = 8 * 512
SEGS = ((0, 0, LAT), (2, LAT, CTX))

C_CQ, C_CKV, C_Z, C_BC, C_DT = 0, 192, 352, 864, 1120
C_CQH, C_FB, C_G, C_DQ, C_DK = 1128, 1640, 2152, 2408, 2664

R_BMOD, R_LNG, R_LNB = 0, 72, 96
R_QN, R_KVN, R_CW, R_CB, R_SN, R_HN, R_C = 0, 2, 3, 33, 39, 41, 43
ROWS1, ROWS2 = 120, 59
FG = FT // 2
GROUP_JOBS = FG + KT_M
FFN_JOBS = 2 * GROUP_JOBS
HALF = TOK // 2
RAW = 2 * KT_M * P
MOD_FILLS, MOD_FIRST = 18, 10
N_SMALL = 48


def constants():
    parts, at, width = [], {}, 0

    def put(name, a):
        nonlocal width
        b = np.zeros((P, a.shape[1]), np.float32)
        b[:a.shape[0]] = a
        parts.append(b)
        at[name] = (width, a.shape[1])
        width += a.shape[1]

    t = np.arange(LAT)
    row, col = (t // GRID_W).astype(np.float32), (t % GRID_W).astype(np.float32)

    def rope(dim):
        r = dim // 2
        half = r // 2
        inv = (ROPE_BASE ** (-np.arange(half, dtype=np.float32) / half)).astype(np.float32)
        cos, sin, swap = np.zeros((dim, LAT)), np.zeros((dim, LAT)), np.zeros((dim, dim))
        for a, pos in enumerate((row, col)):
            ang = (pos[None, :] * inv[:, None]).astype(np.float32)
            lo, hi = a * r + np.arange(half), a * r + half + np.arange(half)
            cos[lo], cos[hi] = np.cos(ang), np.cos(ang)
            sin[lo], sin[hi] = -np.sin(ang), np.sin(ang)
            swap[hi, lo] = 1
            swap[lo, hi] = 1
        return cos, sin, swap

    i = np.arange(P)
    put("ident", np.eye(P))
    put("ones", np.ones((P, P)))
    put("block", (i[:, None] // 64 == i[None, :] // 64).astype(np.float32))
    cos, sin, swap = rope(ROPE)
    ca, sa, pa = np.ones((QK_A, LAT)), np.zeros((QK_A, LAT)), np.zeros((QK_A, QK_A))
    ca[NOPE:], sa[NOPE:], pa[NOPE:, NOPE:] = cos, sin, swap
    put("cos_a", ca), put("sin_a", sa), put("swap_a", pa)
    cos, sin, swap = rope(64)
    pd = np.zeros((P, P))
    pd[:64, :64], pd[64:, 64:] = swap, swap
    put("cos_d", np.tile(cos, (2, 1))), put("sin_d", np.tile(sin, (2, 1))), put("swap_d", pd)
    put("far_before", np.where(i[None, :] >= i[:, None], 0.0, NEG))
    put("far_after", np.where(i[None, :] <= i[:, None], 0.0, NEG))
    sel = np.zeros((8, 4, P))
    for d in range(2):
        for ct in range(2):
            for p in range(P):
                sel[d * 4 + ct * 2 + p // 64, d * 2 + ct, p] = 1
    put("sel", sel.reshape(8, 4 * P))
    masks = [np.eye(P)]
    for lev in range(1, LEVELS + 1):
        m = 2 ** (lev - 1)
        same = i[:, None] // (2 * m) == i[None, :] // (2 * m)
        masks.append(same & (i[:, None] // m != i[None, :] // m))
    put("masks", np.concatenate([np.asarray(m, np.float32) for m in masks], 1))
    put("eps", np.full((P, 1), EPS))
    return np.concatenate(parts, 1).astype(np.float32), at


def plan_layer():
    fills = [(f"mod{i}", 1) for i in range(MOD_FIRST)] + [("zx", 1), ("bc", 8)]
    fills += [(f"mod{i}", 1) for i in range(MOD_FIRST, MOD_FILLS)]
    fills += [("qf", 1), ("fi", 1), ("g", 1), ("a", 1), ("d", 5), ("o0", 1), ("o1", 1)]
    number, total, loaded = {}, [0, 0], []
    for n, (name, k) in enumerate(fills):
        number[name] = n
        total[n % 2] += 16 * k
        loaded.append(total[n % 2])
    jobs = ["x0", "x1", "b0", "b1", "c0", "c1", "z0", "z1", "dt"] + [f"sel{d}" for d in range(4)] + ["y0", "ms0"]
    jobs += ["hq0", "hq1", "f0", "f1", "f2", "f3", "iv", "g0", "g1", "y1", "ms1"]
    jobs += ["cq0", "cq1", "ckv", "kr", "msq", "mskv"] + [f"q{h}" for h in range(4)] + [f"k{h}" for h in range(4)] + ["va"]
    jobs += ["qd0", "qd1", "kd", "vd"] + [f"o{m}" for m in range(KT_M)]
    job = {n: i for i, n in enumerate(jobs)}
    units = []
    for kind in "AD":
        for t in (0, 1, 2, 3, None):
            for h in range(4):
                if t is None:
                    units.append(dict(kind=kind, h=h, q=LAT, lo=4, hi=5, cache=False, t=None, tiles=[4]))
                    continue
                lo, hi = (0, 4) if kind == "A" else (max(t - 1, 0), min(t + 2, 4))
                units.append(dict(kind=kind, h=h, q=t * P, lo=lo, hi=hi, cache=True, t=t,
                                  tiles=list(range(lo, hi)) + [5]))
    return number, loaded, job, units


def trunk_kernel(nc, a, consts, const_at):
    number, loaded_at, job, units = plan_layer()
    with ExitStack() as ctx:
        def sb(name, cols, rows=P):
            return ctx.enter_context(nc.sbuf_tensor(name, [rows, cols], F32))

        def sem(name):
            return ctx.enter_context(nc.semaphore(name))

        banks = ctx.enter_context(nc.psum_tensor("banks", [P, 8, 512], F32))

        cst = sb("cst", consts.shape[1])
        X = sb("x_res", KT_M * TOK)[:].rearrange("p (k t) -> p k t", k=KT_M)
        WU = sb("w_mla", 2 * 384 + 512)
        W_UQ = WU[:, 0:768].rearrange("p (k c) -> p k c", k=2)
        W_UKV = WU[:, 768:1280]
        PR1, PR2 = sb("par_rows1", P), sb("par_rows2", P)
        PT1, PT2 = sb("par1", ROWS1), sb("par2", ROWS2)
        SC = sb("cond", 16)[:].rearrange("p (k g) -> p k g", k=8)
        MOD = sb("mod", 144)[:].rearrange("p (s w m g) -> p s w m g", s=3, w=3, m=8)
        W_DT = sb("w_dt", 64)[:].rearrange("p (k c) -> p k c", k=8)
        LBT, LB, LBN, OML = sb("lb_t", 8), sb("lb", 4), sb("lb_next", 4), sb("one_minus_lb", 4)
        LBW = sb("lb_work", 4)
        DTP = sb("dt_par", 4, 8)
        SKIP, DS = sb("skip_par", 8), sb("skip", 2)
        SINK = sb("sink", 8)
        S0B, S0C = sb("s0_ssd", 512, 64), sb("s0_hgrn", 256)
        FIN, FINT = sb("fin", 256), S0B
        DEC = sb("chunk_decay", 20)[:].rearrange("p (d c h) -> p d c h", d=2, c=2)
        RS = sb("rstd", TOK)
        SM = sb("softmax_cols", 48)[:].rearrange("p (g c h) -> p g c h", g=2, c=6)
        CKT = sb("cache_rows", 3 * P)
        NEWROWS = sb("new_rows", 512)
        MROW = NEWROWS[0:2, :]
        ARENA = 20480
        with ExitStack() as mixers:
            def msb(name, cols):
                return mixers.enter_context(nc.sbuf_tensor(name, [P, cols], F32))
            H = msb("h_mod", KT_M * TOK)[:].rearrange("p (k t) -> p k t", k=KT_M)
            MIX = msb("mixed", KT_M * TOK)[:].rearrange("p (k t) -> p k t", k=KT_M)
            W = msb("w_slots", 2 * SLOT)[:].rearrange("p (s c) -> p s c", s=2)
            arena = msb("arena", ARENA)
        def rsb(name, cols):
            return ctx.enter_context(nc.sbuf_tensor(name, [P, cols], F32R))
        HHI = rsb("h_hi", KT_M * TOK)[:].rearrange("p (k t) -> p k t", k=KT_M)
        HLO = rsb("h_lo", KT_M * TOK)[:].rearrange("p (k t) -> p k t", k=KT_M)
        rsb("raw_gap", SLOT)
        w_split0 = rsb("w_split0", 2 * RAW)
        HIDHI = rsb("hid_hi", FG * TOK)[:].rearrange("p (k t) -> p k t", k=FG)
        HIDLO = rsb("hid_lo", FG * TOK)[:].rearrange("p (k t) -> p k t", k=FG)
        w_split1 = rsb("w_split1", 2 * RAW)
        WHI = [w[:, 0:RAW] for w in (w_split0, w_split1)]
        WLO = [w[:, RAW:2 * RAW] for w in (w_split0, w_split1)]
        WRAW = [W[:, 0, i * RAW:(i + 1) * RAW] for i in range(2)]

        def view(first, k, n):
            return arena[:, first:first + k * n].rearrange("p (k n) -> p k n", k=k)

        LBR = arena[0:8, 5120:5248]
        GATE, SQX = view(2 * FG * TOK + 2 * RAW, 2, TOK), view(0, KT_M, TOK)
        Q, KF, KB, PF, SE, SI, PB = (view(i * 1280, 2, TOK) for i in range(7))
        QL, KL = view(8960, 2, TOK), view(10240, 2, TOK)
        KTOK = arena[:, 8960:11520].rearrange("p (c d n) -> p c d n", c=5, d=4)
        CPAD = view(8960, 2, 648)
        CONV = arena[:, 8960 + 1296:8960 + 1296 + 644]
        V = view(11520, 5, 256)
        ATT = arena[:, 12800:15360].rearrange("p (c h n) -> p c h n", c=5, h=4)
        DTW = arena[0:8, 12800:15360].rearrange("p (k n) -> p k n", k=4)
        DT_B = arena[0:8, 5120:6400].rearrange("p (k n) -> p k n", k=2)
        SIN = arena[:, 15360:17920].rearrange("p (c d n) -> p c d n", c=5, d=4)
        XT, ZS = view(17920, 2, TOK), view(19200, 2, TOK)
        BB = PB
        Y, SQ, RB = SE, PB, KF
        CQ, CQN, SQA = view(0, 2, TOK), view(1280, 2, TOK), view(2560, 2, TOK)
        KVR, CKN, RA = arena[:, 3840:4480], arena[:, 4480:5248], arena[:, 5248:5888]
        KR = arena[:, 5888:6656]
        QA, KA = view(6656, 4, TOK), view(9216, 4, EXT)
        VA, VD = view(12288, 6, 256), view(13824, 6, P)
        QD, KD = view(14592, 2, TOK), arena[:, 15872:16640]
        ROT = arena[:, 16640:17152]
        ON = view(16640, 2, 256)
        PRB = view(17152, 2, 640)
        PTS = view(18432, 2, 640)
        XIN = view(0, 5, D_MODEL)

        def cc(name, rows=P):
            c0, n = const_at[name]
            return cst[0:rows, c0:c0 + n]

        ident, ones, block1 = cc("ident"), cc("ones"), cc("block")
        masks = cc("masks").bitcast(I32).rearrange("p (l n) -> p l n", l=LEVELS + 1)
        sel = cc("sel", 8).rearrange("p (d n) -> p d n", d=4)
        eps = cc("eps")

        init_load, init_turn, init_copy, init_lb, init_ready = (sem(n) for n in (
            "init_load", "init_turn", "init_copy", "init_lb", "init_ready"))
        fin_turn, fin_copy, fin_store = sem("fin_turn"), sem("fin_copy"), sem("fin_store")
        arrived, go = sem("arrived"), sem("go")
        names = ("par_load pool_load par_turned par_ready cond_ready mod_row mrow_copied mod_turned mod_ready w_hi w_lo f_done h_hi h_lo product hid_hi hid_lo modded scaled "
                 "w_used done gated mean_ready centred squared var_ready rstd affine "
                 "pads conv_in conv_out xt_turned v_ready dt_ready bc_ready gla_act "
                 "level_k att_done att_used exps prods sums fin_exp fin_prod k_turned k_copied "
                 "cs_done cs_used sin_zero s0_turned s0_ready sin_ready fin_out ft_turned ft_ready "
                 "y_ready ysq y_rstd excl_zero dt_step adt_copied f_raw f_ready mixed_ready "
                 "aq_sq aq_rstd aq_norm akv_norm cache_turned cache_ready rot_done rot_used roped kcopied attn_in_act "
                 "new_turned new_ready scored maxed expd p_turned p_copied pv_done on_ready on_turned on_used "
                 "state_store small_store act_chain dve_chain pool_chain")
        s = {n: sem(n) for n in names.split()}
        w_loaded = [sem("w_loaded_even"), sem("w_loaded_odd")]
        freed = [sem("freed_even"), sem("freed_odd")]
        raw_loaded = [sem("raw_loaded_even"), sem("raw_loaded_odd")]
        f_freed = [sem("ffn_freed_even"), sem("ffn_freed_odd")]
        layer_sems = list(s.values()) + w_loaded + freed + raw_loaded + f_freed

        def slot(j):
            return 3 * (j % 2)

        def bank(n):
            return banks[:, n, :]

        def w_slot(name, k, c):
            return W[:, number[name] % 2, 0:k * c].rearrange("p (k c) -> p k c", k=k)

        def chain(eng, signal):
            count = [0]

            def link(ins):
                count[0] += 1
                ins.then_inc(signal, 1)
                eng.wait_ge(signal, count[0])
            return link

        def bc(ap, shape):
            return ap.broadcast_to(shape)

        rotated = [(QA[0:QK_A, h, 0:LAT], QK_A) for h in range(4)] + [(KR[0:QK_A, 0:LAT], QK_A)]
        rotated += [(QD[:, i, 0:LAT], P) for i in range(2)] + [(KD[:, 0:LAT], P)]

        blockctx = ctx.enter_context(nc.Block())

        @blockctx.sync
        def _(sp):
            sp.dma_start(cst[:], a["consts"]).then_inc(init_load, 16)
            for t in range(4):
                sp.dma_start(XIN[:, t, :], a["x_sample"][0, t * P:(t + 1) * P, :]).then_inc(init_load, 16)
            sp.dma_start(XIN[:, 4, :], a["x_prompt"][0]).then_inc(init_load, 16)
            sp.dma_start(LBR, a["hgrn_lb_logits"].rearrange("l d (t p) -> (l d t) p", p=P)).then_inc(init_load, 16)
            sp.wait_ge(init_load, 112)
            sp.wait_ge(init_ready, 1)

            with sp.Fori(0, DEPTH) as l:
                small = s["par_load"]
                sp.dma_start(PR1[0:72, :], a["b_mod"][l].rearrange("(r p) -> r p", p=P)).then_inc(small, 16)
                sp.dma_start(PR1[72:96, :], a["ln_g"][l].rearrange("s (r p) -> (s r) p", p=P)).then_inc(small, 16)
                sp.dma_start(PR1[96:120, :], a["ln_b"][l].rearrange("s (r p) -> (s r) p", p=P)).then_inc(small, 16)
                sp.dma_start(PR2[0:1, :], a["mla_q_norm"][bass.ds(l, 1), 0:P]).then_inc(small, 16)
                sp.dma_start(PR2[1:2, 0:64], a["mla_q_norm"][bass.ds(l, 1), P:Q_RANK]).then_inc(small, 16)
                sp.dma_start(PR2[1:2, 64:P], a["mla_q_norm"][bass.ds(l, 1), P:Q_RANK]).then_inc(small, 16)
                sp.dma_start(PR2[2:3, :], a["mla_kv_norm"][bass.ds(l, 1), :]).then_inc(small, 16)
                for tap in range(TAPS + 1):
                    r = R_CW + 6 * tap
                    src = a["ssd_conv_w"][l, tap] if tap < TAPS else a["ssd_conv_b"][l]
                    sp.dma_start(PR2[r:r + 2, :], src[0:256].rearrange("(r p) -> r p", p=P)).then_inc(small, 16)
                    for dup in range(2):
                        sp.dma_start(PR2[r + 2:r + 6, dup * 64:dup * 64 + 64],
                                     src[256:512].rearrange("(r p) -> r p", p=64)).then_inc(small, 16)
                sp.dma_start(PR2[R_SN:R_SN + 2, :], a["ssd_norm"][l].rearrange("(r p) -> r p", p=P)).then_inc(small, 16)
                sp.dma_start(PR2[R_HN:R_HN + 2, :], a["hgrn_norm"][l].rearrange("(r p) -> r p", p=P)).then_inc(small, 16)
                sp.dma_start(PR2[R_C:R_C + 8, :], a["c"][0].rearrange("(r p) -> r p", p=P)).then_inc(small, 16)
                sp.dma_start(PR2[R_C + 8:R_C + 16, :], a["c_ctx"].rearrange("(r p) -> r p", p=P)).then_inc(small, 16)
                sp.dma_start(DTP[:, 0:1], a["ssd_dt_bias"][l].rearrange("d (h o) -> (d h) o", o=1)).then_inc(small, 16)
                sp.dma_start(DTP[:, 1:2], a["ssd_a_log"][l].rearrange("d (h o) -> (d h) o", o=1)).then_inc(small, 16)
                sp.dma_start(SKIP[:], a["ssd_d"][bass.ds(l, 1)].rearrange("o d h -> o (d h)").partition_broadcast(P)).then_inc(small, 16)
                sp.dma_start(SINK[:, 0:4], a["gqa_sink"][bass.ds(l, 1)].partition_broadcast(P)).then_inc(small, 16)
                sp.dma_start(W_DT, a["w_in"][l].rearrange("(k p) c -> p k c", p=P)[:, :, C_DT:C_DT + 8]).then_inc(small, 16)
                sp.dma_start(W_UQ[:, 0, :], a["mla_w_uq"][l, 0:P, :]).then_inc(small, 16)
                sp.dma_start(W_UQ[0:64, 1, :], a["mla_w_uq"][l, P:Q_RANK, :]).then_inc(small, 16)
                sp.dma_start(W_UKV, a["mla_w_ukv"][l]).then_inc(small, 16)
                for d in range(2):
                    for ct in range(2):
                        at = (d * 2 + ct) * P
                        sp.dma_start(S0B[:, at:at + P].rearrange("p (h n) -> p h n", h=2),
                                     a["state_b_ssm"][0, l, d, 2 * ct:2 * ct + 2].rearrange("h p n -> p h n")).then_inc(small, 16)
                        at //= 2
                        sp.dma_start(S0C[:, at:at + 64],
                                     a["state_c_hgrn"][0, l, d, 2 * ct:2 * ct + 2].rearrange("h k v -> (h k) v")).then_inc(small, 16)
                sp.dma_start(CKT[:, 0:P], a["cache_a_ckv"][0, l]).then_inc(small, 16)
                sp.dma_start(CKT[:, P + NOPE:P + QK_A], a["cache_a_krope"][0, l]).then_inc(small, 16)
                sp.dma_start(CKT[:, 2 * P:3 * P], a["cache_d_k"][0, l].rearrange("t h d -> t (h d)")).then_inc(small, 16)

                def fill(name, pieces):
                    n = number[name]
                    if n >= 2:
                        sp.wait_ge(s["w_used"], n - 1)
                    for dst, src in pieces:
                        sp.dma_start(dst, src).then_inc(w_loaded[n % 2], 16)

                w_mod = a["w_mod"][l].rearrange("(k p) c -> p k c", p=P)
                w_in = a["w_in"][l].rearrange("(k p) c -> p k c", p=P)
                w_out = a["w_out"][l].rearrange("(k p) c -> p k c", p=P)
                def fill_mod(i):
                    fill(f"mod{i}", [(w_slot(f"mod{i}", 8, 512), w_mod[:, :, i * 512:(i + 1) * 512])])

                for i in range(MOD_FIRST):
                    fill_mod(i)

                def fill_ffn(sub):
                    w_gu = a["ffn_w_gu"][l, sub // 2].rearrange("(k p) (w c) -> p w k c", p=P, w=2)
                    w_dn = a["ffn_w_down"][l, sub // 2].rearrange("(k p) c -> p k c", p=P)

                    def gate_up(par, col):
                        dst = WRAW[par].rearrange("p (w k c) -> p w k c", w=2, k=KT_M)
                        for w in range(2):
                            sp.dma_start(dst[:, w], w_gu[:, w, :, bass.ds(col, P)]).then_inc(raw_loaded[par], 16)

                    for g in range(2):
                        n0 = sub // 2 * FFN_JOBS + g * GROUP_JOBS
                        if g == 0:
                            for c in range(2):
                                gate_up((n0 + c) % 2, c * P)
                        with sp.Fori(1 if g == 0 else 0, FG // 2) as i:
                            for c in range(2):
                                sp.wait_ge(s["w_lo"], i * 2 + (n0 + c - 1))
                                gate_up((n0 + c) % 2, i * (2 * P) + (g * FG + c) * P)
                        sp.wait_ge(s["w_lo"], n0 + FG - 2)
                        gate_up((n0 + FG - 1) % 2, (g * FG + FG - 1) * P)
                        for m in range(KT_M):
                            n = n0 + FG + m
                            sp.wait_ge(s["w_lo"], n - 1)
                            dst = WRAW[n % 2][:, 0:FG * P].rearrange("p (k c) -> p k c", k=FG)
                            for k0, k1 in ((0, 6), (6, FG)):
                                sp.dma_start(dst[:, k0:k1], w_dn[:, g * FG + k0:g * FG + k1, m * P:(m + 1) * P])\
                                    .then_inc(raw_loaded[n % 2], 16)

                sp.wait_ge(s["w_used"], MOD_FIRST - 1)
                fill_ffn(0)
                sp.wait_ge(s["w_lo"], FFN_JOBS)
                if number["zx"] % 2 == 1:
                    sp.wait_ge(s["f_done"], FFN_JOBS)
                fill("zx", [(w_slot("zx", 8, 512), w_in[:, :, C_Z:C_Z + 512])])
                pieces = []
                for g in range(4):
                    for dup in range(2):
                        at = (2 * g + dup) * 64
                        pieces.append((w_slot("bc", 8, 512)[:, :, at:at + 64], w_in[:, :, C_BC + g * 64:C_BC + g * 64 + 64]))
                sp.wait_ge(s["f_done"], FFN_JOBS)
                fill("bc", pieces)
                for i in range(MOD_FIRST, MOD_FILLS):
                    fill_mod(i)
                fill("qf", [(w_slot("qf", 8, 512), w_in[:, :, C_CQH:C_CQH + 512])])
                fill("fi", [(w_slot("fi", 8, 512), w_in[:, :, C_FB:C_FB + 512])])
                fill("g", [(w_slot("g", 8, 256), w_in[:, :, C_G:C_G + 256])])
                fill("a", [(w_slot("a", 8, 352), w_in[:, :, 0:352])])
                pieces = []
                for h in range(4):
                    at = (2 * (h % 2) + h // 2) * 64
                    pieces.append((w_slot("d", 8, 512)[:, :, at:at + 64], w_in[:, :, C_DQ + h * 64:C_DQ + h * 64 + 64]))
                pieces.append((w_slot("d", 8, 512)[:, :, 256:512], w_in[:, :, C_DK:C_DK + 256]))
                fill("d", pieces)
                sp.wait_ge(s["mixed_ready"], 2)
                sp.dma_start(VD[:, 5, :], a["cache_d_v"][0, l].rearrange("t h d -> t (h d)")).then_inc(s["pool_load"], 16)
                for i in range(2):
                    fill(f"o{i}", [(w_slot(f"o{i}", 8, 512), w_out[:, :, i * 512:(i + 1) * 512])])
                sp.wait_ge(s["w_used"], number["o1"] + (1 if number["o1"] % 2 == 0 else 0))
                fill_ffn(2)

                for d in range(2):
                    for ct in range(2):
                        at = (d * 2 + ct) * P
                        sp.wait_ge(s["ft_ready"], 1)
                        sp.dma_start(a["out_b"][0, l, d, 2 * ct:2 * ct + 2].rearrange("h p n -> p h n"),
                                     FINT[:, at:at + P].rearrange("p (h n) -> p h n", h=2)).then_inc(s["state_store"], 16)
                        at //= 2
                        sp.wait_ge(s["fin_out"], 2)
                        sp.dma_start(a["out_c"][0, l, d, 2 * ct:2 * ct + 2].rearrange("h k v -> (h k) v"),
                                     FIN[:, at:at + 64]).then_inc(s["state_store"], 16)
                sp.wait_ge(s["new_ready"], 1)
                sp.dma_start(a["out_ckv"][0, l], NEWROWS[:, 0:P]).then_inc(s["small_store"], 16)
                sp.dma_start(a["out_dk"][0, l].rearrange("t h d -> t (h d)"), NEWROWS[:, P:2 * P]).then_inc(s["small_store"], 16)
                sp.dma_start(a["out_krope"][0, l], NEWROWS[:, 2 * P + NOPE:2 * P + QK_A]).then_inc(s["small_store"], 16)
                sp.dma_start(a["out_dv"][0, l].rearrange("t h d -> t (h d)"), NEWROWS[:, 2 * P + QK_A:3 * P + QK_A]).then_inc(s["small_store"], 16)
                sp.wait_ge(s["state_store"], 128)
                sp.wait_ge(s["small_store"], 64)
                sp.wait_ge(arrived, 4)
                for x in layer_sems:
                    sp.sem_clear(x)
                sp.sem_clear(arrived)
                sp.sem_inc(go, 1)

            for t in range(NCH):
                sp.wait_ge(fin_copy, 2 * t + 2)
                dst = a["y_s"][0, t * P:(t + 1) * P, :] if t < 4 else a["y_p"][0]
                sp.dma_start(dst, XIN[:, t, :]).then_inc(fin_store, 16)
            sp.wait_ge(fin_store, 16 * NCH)

        @blockctx.tensor
        def _(pe):
            mm = nc.tensor.matmul
            pe.wait_ge(init_load, 112)
            for n in range(2 * NCH):
                t, half = n // 2, n % 2
                if n >= 4:
                    pe.wait_ge(init_copy, n - 3)
                for k in range(4):
                    ins = nc.tensor.transpose(banks[:, n % 4, k * P:(k + 1) * P],
                                              XIN[:, t, (half * 4 + k) * P:(half * 4 + k + 1) * P], ident)
                ins.then_inc(init_turn, 1)
            nc.tensor.transpose(banks[:, 4, 0:8], LBR, ident[0:8, 0:8]).then_inc(init_turn, 1)
            pe.wait_ge(init_copy, 2 * NCH + 1)

            with pe.Fori(0, DEPTH) as l:
                def slot_free(j):
                    if j >= 2:
                        pe.wait_ge(freed[j % 2], j // 2)

                def weights(name):
                    pe.wait_ge(w_loaded[number[name] % 2], loaded_at[number[name]])

                def product(out, pairs):
                    for i, (lhs, rhs) in enumerate(pairs):
                        ins = mm(out, lhs, rhs, start=i == 0, stop=i == len(pairs) - 1)
                    return ins

                def dense(name, w, c0, m, src, kt, last=False):
                    j = job[name]
                    slot_free(j)
                    for b, t0, n in SEGS:
                        ins = product(banks[0:m, slot(j) + b, 0:n],
                                      [(w[:, k, c0:c0 + m], src[:, k, t0:t0 + n]) for k in range(kt)])
                    ins.then_inc(s["done"], 1)

                def used():
                    pe.wait_ge(s["done"], dense_count[0])
                    pe.sem_inc(s["w_used"], 1)

                dense_count = [0]

                def run(name, *args):
                    dense(name, *args)
                    dense_count[0] = job[name] + 1

                pe.wait_ge(s["par_load"], 16 * N_SMALL)
                nc.tensor.transpose(banks[:, 7, 0:ROWS1], PR1[0:ROWS1, :], ident[0:ROWS1, 0:ROWS1])
                nc.tensor.transpose(banks[:, 7, P:P + ROWS2], PR2[0:ROWS2, :], ident[0:ROWS2, 0:ROWS2]).then_inc(s["par_turned"], 1)
                pe.wait_ge(s["cond_ready"], 1)

                def mod_fill(i):
                    weights(f"mod{i}")
                    w = w_slot(f"mod{i}", 8, 512)
                    product(banks[0:2, 6, :], [(SC[:, k, :], w[:, k, :]) for k in range(8)]).then_inc(s["mod_row"], 1)
                    pe.wait_ge(s["mod_row"], i + 1)
                    pe.sem_inc(s["w_used"], 1)
                    pe.wait_ge(s["mrow_copied"], i + 1)
                    for m in range(4):
                        at = (4 * i + m) * 2
                        ins = nc.tensor.transpose(banks[:, 7, at:at + 2], MROW[:, m * P:(m + 1) * P], ident[0:2, 0:2])
                    ins.then_inc(s["mod_turned"], 1)

                for i in range(MOD_FIRST):
                    mod_fill(i)

                def ffn(sub):
                    def split_product(b0, par, c0, width, hi, lo, kt, tiles=False):
                        whi = WHI[par][:, 0:kt * width].rearrange("p (k c) -> p k c", k=kt) if c0 is None else WHI[par].rearrange("p (w k c) -> p w k c", w=2, k=kt)[:, c0]
                        wlo = WLO[par][:, 0:kt * width].rearrange("p (k c) -> p k c", k=kt) if c0 is None else WLO[par].rearrange("p (w k c) -> p w k c", w=2, k=kt)[:, c0]
                        for hf in range(2):
                            t = slice(hf * HALF, (hf + 1) * HALF)
                            pairs = []
                            for k in range(kt):
                                pairs += [(wlo[:, k, :], hi[:, k, t]), (whi[:, k, :], lo[:, k, t]), (whi[:, k, :], hi[:, k, t])]
                            for i, (w, x) in enumerate(pairs):
                                if tiles and hf == 0 and i % 3 == 0:
                                    pe.wait_ge(s["h_lo"], 8 * (sub // 2) + i // 3 + 1)
                                ins = mm(banks[:, b0 + hf, 0:HALF], w, x, start=i == 0, stop=i == len(pairs) - 1)
                        return ins

                    def gate_up(par, tiles=False):
                        for g in range(2):
                            ins = split_product(4 * par + 2 * g, par, g, P, HHI, HLO, KT_M, tiles and g == 0)
                        ins.then_inc(s["f_done"], 1)

                    for g in range(2):
                        n0 = sub // 2 * FFN_JOBS + g * GROUP_JOBS
                        if g == 0:
                            for c in range(2):
                                if n0 + c >= 2:
                                    pe.wait_ge(f_freed[(n0 + c) % 2], (n0 + c) // 2)
                                pe.wait_ge(s["w_lo"], n0 + c + 1)
                                gate_up((n0 + c) % 2, c == 0)
                        with pe.Fori(1 if g == 0 else 0, FG // 2) as i:
                            for c in range(2):
                                par = (n0 + c) % 2
                                pe.wait_ge(f_freed[par], i + (n0 + c) // 2)
                                pe.wait_ge(s["w_lo"], i * 2 + (n0 + c + 1))
                                gate_up(par)
                        n = n0 + FG - 1
                        pe.wait_ge(f_freed[n % 2], n // 2)
                        pe.wait_ge(s["w_lo"], n + 1)
                        gate_up(n % 2)
                        for m in range(KT_M):
                            n = n0 + FG + m
                            pe.wait_ge(f_freed[n % 2], n // 2)
                            if m == 0:
                                pe.wait_ge(s["hid_lo"], (sub + g + 1) * FG)
                            pe.wait_ge(s["w_lo"], n + 1)
                            split_product(4 * (n % 2), n % 2, None, P, HIDHI, HIDLO, FG).then_inc(s["f_done"], 1)
                            if g == 1 and m >= 2:
                                mean_product(m - 2)
                    for k in (KT_M - 2, KT_M - 1):
                        n = n0 + FG + k
                        pe.wait_ge(f_freed[n % 2], n // 2 + 1)
                        ins = mean_product(k)
                    ins.then_inc(s["mean_ready"], 1)

                def mean_product(k):
                    for b, t0, n in SEGS:
                        ins = mm(banks[:, 6 + b // 2, 0:n], ones, X[:, k, t0:t0 + n], start=k == 0, stop=k == KT_M - 1, skip_group_check=True)
                    return ins

                def layer_norm(sub):
                    for k in range(KT_M):
                        if k % 2 == 0:
                            pe.wait_ge(s["squared"], 4 * sub + k // 2 + 1)
                        for b, t0, n in SEGS:
                            ins = mm(banks[:, 4 + b // 2, 0:n], ones, SQX[:, k, t0:t0 + n], start=k == 0, stop=k == KT_M - 1, skip_group_check=True)
                    ins.then_inc(s["var_ready"], 1)

                ffn(0)
                layer_norm(0)

                pe.wait_ge(s["modded"], 16)
                weights("zx")
                w = w_slot("zx", 8, 512)
                run("x0", w, 256, P, H, 8)
                run("x1", w, 384, P, H, 8)
                weights("bc")
                w2 = w_slot("bc", 8, 512)
                for g, name in enumerate(("b0", "b1", "c0", "c1")):
                    run(name, w2, g * P, P, H, 8)
                run("z0", w, 0, P, H, 8)
                run("z1", w, P, P, H, 8)
                used()
                pe.sem_inc(s["w_used"], 1)
                run("dt", W_DT, 0, 8, H, 8)
                pe.wait_ge(s["bc_ready"], 2)
                for c in range(NCH):
                    if c >= 2:
                        pe.wait_ge(s["v_ready"], c - 1)
                    for ct in range(2):
                        ins = nc.tensor.transpose(banks[:, 6 + c % 2, ct * P:(ct + 1) * P], XT[:, ct, c * P:(c + 1) * P], ident)
                    ins.then_inc(s["xt_turned"], 1)
                pe.wait_ge(s["dt_ready"], 1)
                for d in range(4):
                    j = job[f"sel{d}"]
                    slot_free(j)
                    mm(banks[:, slot(j), :], sel[:, d, :], DT_B[:, 0, 0:LAT], start=True, stop=True)
                    mm(banks[:, slot(j) + 1, :], sel[:, d, :], DT_B[:, 1, 0:LAT], start=True, stop=True)
                    mm(banks[:, slot(j) + 2, 0:P], sel[:, d, :], DT_B[:, 0, LAT:TOK], start=True, stop=True)
                    mm(banks[:, slot(j) + 2, P:2 * P], sel[:, d, :], DT_B[:, 1, LAT:TOK], start=True, stop=True).then_inc(s["done"], 1)

                def gla(mx):
                    pe.wait_ge(s["gla_act"], mx + 1)
                    for p in range(2):
                        pe.wait_ge(freed[p], len([j for j in range(job[f"y{mx}"]) if j % 2 == p]))
                    for lev in range(LEVELS + 1):
                        if lev == 0:
                            pe.wait_ge(s["level_k"], mx + 1)
                            q, k = Q, KL
                        else:
                            pe.wait_ge(s["prods"], 3 * (LEVELS * mx + lev))
                            q, k = QL, KL
                        for c in range(NCH):
                            n = (mx * (LEVELS + 1) + lev) * NCH + c
                            if n - mx * (LEVELS + 1) * NCH >= 3:
                                pe.wait_ge(s["att_used"], n - 2)
                            for h in (0, 2, 1, 3):
                                rows = slice(64 * (h % 2), 64 * (h % 2) + 64)
                                cols = slice(c * P, (c + 1) * P)
                                ins = mm(banks[:, 2 * (n % 3) + h % 2, (h // 2) * P:(h // 2 + 1) * P], k[rows, h // 2, cols],
                                         q[rows, h // 2, cols], start=True, stop=True)
                            ins.then_inc(s["att_done"], 1)
                        if mx == 0:
                            mod_fill(MOD_FIRST + lev)
                    pe.wait_ge(s["fin_prod"], 4 * (mx + 1))
                    pe.wait_ge(s["att_used"], (mx + 1) * (LEVELS + 1) * NCH)
                    for c in range(NCH):
                        if c >= 4:
                            pe.wait_ge(s["k_copied"], NCH * mx + c - 3)
                        for d in range(4):
                            ins = nc.tensor.transpose(banks[:, c % 4, d * P:(d + 1) * P], (KF, KB)[d // 2][:, d % 2, c * P:(c + 1) * P], ident)
                        ins.then_inc(s["k_turned"], 1)
                    if mx == 0:
                        for d in range(4):
                            ins = nc.tensor.transpose(banks[:, 6, d * 64:(d + 1) * 64], S0B[:, d * P:(d + 1) * P], ident[0:64, 0:64])
                        ins.then_inc(s["s0_turned"], 1)
                    pe.wait_ge(s["k_copied"], NCH * (mx + 1))
                    for t in range(4):
                        if t >= 2:
                            pe.wait_ge(s["cs_used"], 4 * mx + t - 1)
                        for d in range(4):
                            c = 4 if t == 3 else (t, 3 - t)[d // 2]
                            ct = d % 2
                            ins = mm(banks[:, 4 + t % 2, d * P:(d + 1) * P], KTOK[:, c, d, :], V[:, c, ct * P:(ct + 1) * P], start=True, stop=True)
                        ins.then_inc(s["cs_done"], 1)
                    if mx == 0:
                        pe.wait_ge(s["fin_out"], 1)
                        pe.wait_ge(s["s0_ready"], 1)
                        for d in range(4):
                            ins = nc.tensor.transpose(banks[0:64, 6, d * P:(d + 1) * P], FIN[:, d * 64:(d + 1) * 64], ident)
                        ins.then_inc(s["ft_turned"], 1)
                    pe.wait_ge(s["sin_ready"], mx + 1)
                    j = job[f"y{mx}"]
                    b0 = slot(j)
                    for ct in range(2):
                        for c in range(NCH):
                            out = banks[:, b0 + ct, c * P:(c + 1) * P] if c < 4 else banks[:, b0 + 2, ct * P:(ct + 1) * P]
                            for hh in range(2):
                                h = 2 * ct + hh
                                ins = mm(out[64 * hh:64 * hh + 64], V[:, c, h * 64:(h + 1) * 64], ATT[:, c, 2 * hh + ct, :],
                                         start=True, stop=c == 4, skip_group_check=True)
                            if c < 4:
                                cols = slice(c * P, (c + 1) * P)
                                mm(out, SIN[:, c, ct, :], PF[:, ct, cols], start=False, stop=False, skip_group_check=True)
                                ins = mm(out, SIN[:, c, 2 + ct, :], SI[:, ct, cols], start=False, stop=True, skip_group_check=True)
                    ins.then_inc(s["done"], 1)
                    pe.wait_ge(s["ysq"], mx + 1)
                    j = job[f"ms{mx}"]
                    slot_free(j)
                    for ct in range(2):
                        mm(banks[:, slot(j) + ct, :], block1, SQ[:, ct, 0:LAT], start=True, stop=True)
                        ins = mm(banks[:, slot(j) + 2, ct * P:(ct + 1) * P], block1, SQ[:, ct, LAT:TOK], start=True, stop=True)
                    ins.then_inc(s["done"], 1)
                    pe.wait_ge(s["mixed_ready"], mx + 1)

                gla(0)
                weights("qf")
                w = w_slot("qf", 8, 512)
                for m, name in enumerate(("hq0", "hq1", "f0", "f1")):
                    run(name, w, m * P, P, H, 8)
                used()
                weights("fi")
                w = w_slot("fi", 8, 512)
                run("f2", w, 0, P, H, 8)
                run("f3", w, P, P, H, 8)
                j = job["iv"]
                slot_free(j)
                for c in range(NCH):
                    out = banks[:, slot(j) + c // 2, (c % 2) * 256:(c % 2) * 256 + 256]
                    ins = product(out, [(H[:, k, c * P:(c + 1) * P], w[:, k, 256:512]) for k in range(8)])
                ins.then_inc(s["done"], 1)
                dense_count[0] = j + 1
                used()
                weights("g")
                run("g0", w_slot("g", 8, 256), 0, P, H, 8)
                run("g1", w_slot("g", 8, 256), P, P, H, 8)
                used()
                gla(1)

                weights("a")
                w = w_slot("a", 8, 352)
                run("cq0", w, 0, P, H, 8)
                run("cq1", w, P, 64, H, 8)
                run("ckv", w, C_CKV, P, H, 8)
                run("kr", w, 256, QK_A, H, 8)
                used()
                j = job["msq"]
                slot_free(j)
                pe.wait_ge(s["aq_sq"], 2)
                for b, t0, n in SEGS:
                    mm(banks[:, slot(j) + b, 0:n], ones, SQA[:, 0, t0:t0 + n], start=True, stop=False)
                    ins = mm(banks[:, slot(j) + b, 0:n], ones[0:64, :], SQA[0:64, 1, t0:t0 + n], start=False, stop=True)
                ins.then_inc(s["done"], 1)
                j = job["mskv"]
                slot_free(j)
                pe.wait_ge(s["aq_sq"], 3)
                for b, t0, n in SEGS:
                    ins = mm(banks[:, slot(j) + b, 0:n], ones, SQA[:, 0, t0:t0 + n], start=True, stop=True)
                ins.then_inc(s["done"], 1)
                pe.wait_ge(s["akv_norm"], 1)
                nc.tensor.transpose(banks[:, 7, 0:P], CKT[:, 0:P], ident)
                nc.tensor.transpose(banks[0:QK_A, 7, P:2 * P], CKT[:, P:P + QK_A], ident)
                nc.tensor.transpose(banks[:, 7, 2 * P:3 * P], CKT[:, 2 * P:3 * P], ident).then_inc(s["cache_turned"], 1)
                pe.wait_ge(s["aq_norm"], 2)
                for h in range(4):
                    j = job[f"q{h}"]
                    slot_free(j)
                    cols = slice(h * QK_A, (h + 1) * QK_A)
                    for b, t0, n in SEGS:
                        out = banks[0:QK_A, slot(j) + b, 0:n]
                        mm(out, W_UQ[:, 0, cols], CQN[:, 0, t0:t0 + n], start=True, stop=False)
                        ins = mm(out, W_UQ[0:64, 1, cols], CQN[0:64, 1, t0:t0 + n], start=False, stop=True)
                    ins.then_inc(s["done"], 1)
                pe.wait_ge(s["cache_ready"], 1)
                for h in range(4):
                    j = job[f"k{h}"]
                    slot_free(j)
                    wk = W_UKV[:, h * P:h * P + NOPE]
                    mm(banks[0:NOPE, slot(j), :], wk, CKN[:, 0:LAT], start=True, stop=True)
                    mm(banks[0:NOPE, slot(j) + 2, 0:256], wk, CKN[:, LAT:EXT], start=True, stop=True).then_inc(s["done"], 1)
                j = job["va"]
                slot_free(j)
                wv = W_UKV.rearrange("p (h w c) -> p h w c", h=4, w=2)[:, :, 1, :]
                for c in range(6):
                    out = banks[:, slot(j) + c // 2, (c % 2) * 256:(c % 2) * 256 + 256]
                    ins = mm(out, CKN[:, c * P:(c + 1) * P], wv, start=True, stop=True)
                ins.then_inc(s["done"], 1)
                weights("d")
                w = w_slot("d", 8, 512)
                for m, name in enumerate(("qd0", "qd1", "kd")):
                    run(name, w, m * P, P, H, 8)
                j = job["vd"]
                slot_free(j)
                for c in range(NCH):
                    out = banks[:, slot(j) + c // 4, (c % 4) * P:(c % 4) * P + P]
                    ins = product(out, [(H[:, k, c * P:(c + 1) * P], w[:, k, 384:512]) for k in range(8)])
                ins.then_inc(s["done"], 1)
                dense_count[0] = j + 1
                used()
                pe.wait_ge(s["attn_in_act"], 1)
                nc.tensor.transpose(banks[:, 7, 0:P], CKN[:, LAT:TOK], ident)
                nc.tensor.transpose(banks[:, 7, P:2 * P], KD[:, LAT:TOK], ident)
                nc.tensor.transpose(banks[:, 7, 2 * P:2 * P + QK_A], KR[0:QK_A, LAT:TOK], ident[0:QK_A, 0:QK_A]).then_inc(s["new_turned"], 1)
                for n, (ap, rows) in enumerate(rotated):
                    if n >= 1:
                        pe.wait_ge(s["rot_used"], n)
                    mm(banks[0:rows, 6, :], (cc("swap_a", QK_A) if rows == QK_A else cc("swap_d")), ap, start=True, stop=True).then_inc(s["rot_done"], 1)

                def score(u):
                    un = units[u]
                    sl = 2 * (u % 2)
                    if u >= 2:
                        pe.wait_ge(s["expd"], u - 1)
                    if un["kind"] == "A":
                        q = QA[0:QK_A, un["h"], un["q"]:un["q"] + P]
                        key = KA[0:QK_A, un["h"], :]
                    else:
                        rows = slice(64 * (un["h"] // 2), 64 * (un["h"] // 2) + 64)
                        q = QD[rows, un["h"] % 2, un["q"]:un["q"] + P]
                        key = KD[rows, :]
                    n = (un["hi"] - un["lo"]) * P
                    flat = banks[:, sl:sl + 2, :].rearrange("p b n -> p (b n)")
                    if un["cache"]:
                        ins = mm(flat[:, n:n + P], q, key[:, TOK:EXT], start=True, stop=True)
                    masked = []
                    if un["kind"] == "D" and un["cache"]:
                        if un["t"] > 0:
                            masked.append((0, cc("far_before")))
                        if un["t"] < 3:
                            masked.append((n - P, cc("far_after")))
                    ins = mm(flat[:, 0:n], q, key[:, un["lo"] * P:un["hi"] * P], start=True, stop=not masked, skip_group_check=True)
                    for i, (at, m) in enumerate(masked):
                        ins = mm(flat[:, at:at + P], ident, m, start=False, stop=i == len(masked) - 1, skip_group_check=True)
                    ins.then_inc(s["scored"], 1)

                pe.wait_ge(s["roped"], 8)
                pe.wait_ge(s["kcopied"], 2)
                pe.wait_ge(s["new_ready"], 1)
                pe.wait_ge(s["pool_load"], 16)
                for p in range(2):
                    pe.wait_ge(freed[p], len([j for j in range(job["o0"]) if j % 2 == p]))
                score(0)
                score(1)
                for u in range(len(units) + 4):
                    if u < len(units):
                        un = units[u]
                        pe.wait_ge(s["expd"], u + 1)
                        if u >= 1:
                            pe.wait_ge(s["p_copied"], u)
                        pt = banks[:, 4:6, :].rearrange("p b n -> p (b n)")
                        for i in range(len(un["tiles"])):
                            ins = nc.tensor.transpose(pt[:, i * P:(i + 1) * P], PRB[:, u % 2, i * P:(i + 1) * P], ident)
                        ins.then_inc(s["p_turned"], 1)
                        if u + 2 < len(units):
                            score(u + 2)
                        pe.wait_ge(s["p_copied"], u + 1)
                        g, h = u // 4, un["h"]
                        if h == 0 and g >= 2:
                            pe.wait_ge(s["on_used"], g - 1)
                        v = [VA[:, t, h * 64:(h + 1) * 64] if un["kind"] == "A" else VD[:, t, (h // 2) * 64:(h // 2) * 64 + 64]
                             for t in un["tiles"]]
                        product(banks[:, 6 + g % 2, h * 64:(h + 1) * 64],
                                [(PTS[:, u % 2, i * P:(i + 1) * P], vt) for i, vt in enumerate(v)]).then_inc(s["pv_done"], 1)
                    if u >= 6 and u % 4 == 2:
                        g = u // 4 - 1
                        pe.wait_ge(s["on_ready"], g + 1)
                        for i in range(2):
                            ins = nc.tensor.transpose(banks[:, 6 + g % 2, (2 + i) * P:(3 + i) * P], ON[:, g % 2, i * P:(i + 1) * P], ident)
                        ins.then_inc(s["on_turned"], 1)
                pe.wait_ge(s["on_used"], len(units) // 4)

                for m in range(KT_M):
                    if m % 4 == 0:
                        weights(f"o{m // 4}")
                    run(f"o{m}", w_slot(f"o{m // 4}", 8, 512), (m % 4) * P, P, MIX, 8)
                    if m % 4 == 3:
                        used()
                    if m >= 2:
                        mean_product(m - 2)
                for k in (KT_M - 2, KT_M - 1):
                    j = job[f"o{k}"]
                    pe.wait_ge(freed[j % 2], j // 2 + 1)
                    ins = mean_product(k)
                ins.then_inc(s["mean_ready"], 1)
                layer_norm(1)
                ffn(2)
                layer_norm(2)
                pe.wait_ge(s["affine"], 24)
                pe.sem_inc(arrived, 1)
                pe.wait_ge(go, l + 1)

            for n in range(2 * NCH):
                t, half = n // 2, n % 2
                if n >= 4:
                    pe.wait_ge(fin_copy, n - 3)
                for k in range(4):
                    ins = nc.tensor.transpose(banks[:, n % 4, k * P:(k + 1) * P], X[:, half * 4 + k, t * P:(t + 1) * P], ident)
                ins.then_inc(fin_turn, 1)


        def scale_of(un):
            return float((QK_A if un["kind"] == "A" else 64) ** -0.5)

        def flat(ap):
            return ap.rearrange("p k t -> p (k t)")

        def halves(ap, m):
            v = flat(ap).rearrange("p (b h m) -> p b h m", h=2, m=m)
            return v[:, :, 0, :], v[:, :, 1, :]

        def group_cols(j, b, n, rows=P):
            return banks[0:rows, slot(j) + b, 0:n]

        @blockctx.scalar
        def _(act):
            def f(out, in_, func=ACT.Copy, **kw):
                return nc.scalar.activation(out, in_, func, **kw)

            act.wait_ge(init_lb, 1)
            f(LBT[:], LBT[:], ACT.Exp).then_inc(init_lb, 1)

            with act.Fori(0, DEPTH) as l:
                link = chain(act, s["act_chain"])

                def finish(ins, signal, value):
                    ins.then_inc(signal, 1)
                    act.wait_ge(signal, value)

                def evacuate(name, dsts, func=ACT.Copy, rows=P, **kw):
                    j = job[name]
                    act.wait_ge(s["done"], j + 1)
                    for src, dst in dsts:
                        ins = f(dst, src, func, **kw)
                    ins.then_inc(freed[j % 2], 1)

                def both(name, dst, rows=P):
                    j = job[name]
                    return [(group_cols(j, b, n, rows), dst[:, t0:t0 + n]) for b, t0, n in SEGS]

                act.wait_ge(s["par_ready"], 1)
                f(SC, PT2[:, R_C:R_C + 16].rearrange("p (g k) -> p k g", g=2), ACT.Silu).then_inc(s["cond_ready"], 1)
                f(DTP[:, 2:3], DTP[:, 1:2], ACT.Exp).then_inc(s["dt_step"], 1)

                def mod_row(i):
                    act.wait_ge(s["mod_row"], i + 1)
                    if i:
                        act.wait_ge(s["mod_turned"], i)
                    f(MROW, banks[0:2, 6, :]).then_inc(s["mrow_copied"], 1)

                def weights_hi(n, i=None):
                    act.wait_ge(raw_loaded[n % 2], 32 * (n // 2 + 1) if i is None else i * 32 + 32 * (n // 2 + 1))
                    if n >= 2:
                        act.wait_ge(s["f_done"], n - 1 if i is None else i * 2 + (n - 1))
                    f(WHI[n % 2], WRAW[n % 2]).then_inc(s["w_hi"], 1)

                def modulate(sub):
                    act.wait_ge(s["mod_ready"], 1 + (sub == 2))
                    for m in range(KT_M):
                        if sub:
                            act.wait_ge(s["affine"], 8 * (sub - 1) + m + 1)
                        at = 8 * (sub // 2) + m
                        if sub != 1 and m >= 2:
                            act.wait_ge(s["h_lo"], at - 1)
                        dst = H[:, m] if sub == 1 else GATE[:, m % 2]
                        for g, (b, t0, n) in enumerate(SEGS):
                            ins = f(dst[:, t0:t0 + n], X[:, m, t0:t0 + n], ACT.Identity,
                                    scale=MOD[:, sub, 1, m, g:g + 1], bias=MOD[:, sub, 0, m, g:g + 1])
                        ins.then_inc(s["modded"], 1)
                        if sub != 1:
                            act.wait_ge(s["modded"], 8 * sub + m + 1)
                            f(HHI[:, m], GATE[:, m % 2]).then_inc(s["h_hi"], 1)

                def ffn(sub):
                    def gate(par, c, n, hid, dst, split_next):
                        act.wait_ge(s["f_done"], n + 1)
                        act.wait_ge(s["hid_lo"], hid)
                        f(GATE[:, c], banks[:, 4 * par:4 * par + 2, 0:HALF], ACT.Silu).then_inc(s["gated"], 1)
                        split_next()
                        act.wait_ge(s["product"], hid + 1)
                        f(dst, GATE[:, c:c + 1]).then_inc(s["hid_hi"], 1)

                    for g in range(2):
                        n0 = sub // 2 * FFN_JOBS + g * GROUP_JOBS
                        h0 = (sub + g) * FG
                        pairs = HIDHI[:, 0:FG - 1].rearrange("p (i c) t -> p i c t", c=2)
                        with act.Fori(0, FG // 2) as i:
                            for c in range(2):
                                n = n0 + c
                                gate(n % 2, c, i * 2 + n, i * 2 + (h0 + c), pairs[:, bass.ds(i, 1), c, :],
                                     lambda: weights_hi(n + 2, i))
                        n = n0 + FG - 1
                        gate(n % 2, 0, n, h0 + FG - 1, HIDHI[:, FG - 1:FG, :], lambda: weights_hi(n + 2))
                        for m in range(KT_M):
                            n = n0 + FG + m
                            if n + 2 < (sub // 2 + 1) * FFN_JOBS:
                                weights_hi(n + 2)

                def layer_norm(sub, meanwhile=None):
                    for i in range(4):
                        act.wait_ge(s["centred"], 4 * sub + i + 1)
                        f(SQX[:, 2 * i:2 * i + 2, :], X[:, 2 * i:2 * i + 2, :], ACT.Square).then_inc(s["squared"], 1)
                    if meanwhile:
                        meanwhile()
                    act.wait_ge(s["var_ready"], sub + 1)
                    for b, t0, n in SEGS:
                        link(f(RS[:, t0:t0 + n], banks[:, 4 + b // 2, 0:n], ACT.Ln, scale=1.0 / D_MODEL, bias=eps))
                    finish(f(RS[:], RS[:], ACT.Exp, scale=-0.5), s["rstd"], sub + 1)

                for i in range(MOD_FIRST):
                    mod_row(i)
                act.wait_ge(s["w_used"], MOD_FIRST)
                weights_hi(0)
                weights_hi(1)
                modulate(0)
                ffn(0)
                layer_norm(0)
                modulate(1)

                act.wait_ge(s["pads"], 1)
                conv_jobs = ("x0", "x1", "b0", "b1", "c0", "c1")
                conv_dst = (XT[:, 0], XT[:, 1], BB[:, 0], BB[:, 1], Q[:, 0], Q[:, 1])

                def conv_silu(i):
                    act.wait_ge(s["conv_out"], i + 1)
                    bias = PT2[:, R_CB + i:R_CB + i + 1]
                    f(conv_dst[i][:, 0:LAT], CONV[:, 0:LAT], ACT.Silu, bias=bias)
                    finish(f(conv_dst[i][:, LAT:TOK], CONV[:, LAT + 4:644], ACT.Silu, bias=bias), s["bc_ready"], i + 1)

                for i, name in enumerate(conv_jobs):
                    j = job[name]
                    act.wait_ge(s["done"], j + 1)
                    if i >= 2:
                        act.wait_ge(s["conv_out"], i - 1)
                    f(CPAD[:, i % 2, 2:2 + LAT], group_cols(j, 0, LAT))
                    finish(f(CPAD[:, i % 2, 6 + LAT:6 + TOK], group_cols(j, 2, CTX)), s["conv_in"], i + 1)
                    act.sem_inc(freed[j % 2], 1)
                    if i >= 1:
                        conv_silu(i - 1)
                conv_silu(5)
                for ct in range(2):
                    evacuate(f"z{ct}", both(f"z{ct}", ZS[:, ct]), ACT.Silu)
                r, e, w1, lg = (DTW[:, k, :] for k in range(4))
                act.wait_ge(s["dt_step"], 2)
                link(f(e, r, ACT.Abs))
                finish(f(e, e, ACT.Exp, scale=-1.0), s["dt_step"], 3)
                act.wait_ge(s["dt_step"], 4)
                finish(f(lg, w1, ACT.Ln), s["dt_step"], 5)
                for c in range(NCH):
                    act.wait_ge(s["xt_turned"], c + 1)
                    finish(f(V[:, c, :], banks[:, 6 + c % 2, 0:256]), s["v_ready"], c + 1)
                for d in range(4):
                    j = job[f"sel{d}"]
                    act.wait_ge(s["done"], j + 1)
                    dst = (PF, SI)[d // 2][:, d % 2]
                    f(dst[:, 0:LAT], banks[:, slot(j) + 1, :])
                    finish(f(dst[:, LAT:TOK], banks[:, slot(j) + 2, P:2 * P]), s["adt_copied"], d + 1)
                act.sem_inc(s["gla_act"], 1)

                def gla(mx):
                    act.wait_ge(s["excl_zero"], mx + 1)
                    for lev in range(1, LEVELS + 1):
                        m = 2 ** (lev - 1)
                        act.wait_ge(s["att_done"], (mx * (LEVELS + 1) + lev) * NCH)
                        if lev > 1:
                            act.wait_ge(s["sums"], 4 * (LEVELS * mx + lev - 1))
                        (q1, q2), (k1, k2) = halves(QL, m), halves(KL, m)
                        for dst, src in ((q1, halves(SI, m)[0]), (q2, halves(PF, m)[1]),
                                         (k1, halves(SE, m)[0]), (k2, halves(PB, m)[1])):
                            f(dst, src, ACT.Exp).then_inc(s["exps"], 1)
                        if mx == 0:
                            mod_row(MOD_FIRST + lev - 1)
                    if mx == 0:
                        mod_row(MOD_FIRST + LEVELS)
                    act.wait_ge(s["sums"], 4 * LEVELS * (mx + 1))
                    ends = lambda ap, i: ap.rearrange("p k (c i) -> p k c i", i=P)[:, :, :, i]
                    link(f(DEC[:, 0], ends(PF, P - 1), ACT.Exp))
                    link(f(DEC[:, 1], ends(SI, 0), ACT.Exp))
                    for ap in (PF, SI, SE, PB):
                        f(ap, ap, ACT.Exp).then_inc(s["fin_exp"], 1)
                    for c in range(NCH):
                        act.wait_ge(s["k_turned"], NCH * mx + c + 1)
                        f(KTOK[:, c], banks[:, c % 4, :].rearrange("p (d n) -> p d n", d=4)).then_inc(s["k_copied"], 1)
                    if mx == 0:
                        act.wait_ge(s["ft_turned"], 1)
                        f(FINT[:], banks[0:64, 6, :]).then_inc(s["ft_ready"], 1)
                    act.wait_ge(s["y_ready"], mx + 1)
                    f(SQ, Y, ACT.Square).then_inc(s["ysq"], 1)
                    j = job[f"ms{mx}"]
                    act.wait_ge(s["done"], j + 1)
                    b0 = slot(j)
                    link(f(RB[:, :, 0:LAT], banks[:, b0:b0 + 2, :], ACT.Ln, scale=1.0 / 64, bias=eps))
                    link(f(RB[:, :, LAT:TOK], banks[:, b0 + 2, 0:256].rearrange("p (k n) -> p k n", k=2), ACT.Ln, scale=1.0 / 64, bias=eps))
                    act.sem_inc(freed[j % 2], 1)
                    f(RB, RB, ACT.Exp, scale=-0.5).then_inc(s["y_rstd"], 1)

                gla(0)
                for ct in range(2):
                    evacuate(f"hq{ct}", both(f"hq{ct}", Q[:, ct]))
                for i in range(4):
                    j = job[f"f{i}"]
                    act.wait_ge(s["done"], j + 1)
                    for b, t0, n in SEGS:
                        f((PF, SI)[i // 2][:, i % 2, t0:t0 + n], group_cols(j, b, n), ACT.Sigmoid)
                        ins = f((KF, KB)[i // 2][:, i % 2, t0:t0 + n], group_cols(j, b, n), ACT.Sigmoid, scale=-1.0)
                    finish(ins, s["f_raw"], i + 1)
                    act.sem_inc(freed[j % 2], 1)
                j = job["iv"]
                b0 = slot(j)
                pair = lambda ap: ap.rearrange("p (c n) -> p c n", n=256)
                evacuate("iv", [(pair(banks[:, b0, :]), V[:, 0:2, :]), (pair(banks[:, b0 + 1, :]), V[:, 2:4, :]),
                                (banks[:, b0 + 2, 0:256], V[:, 4, :])])
                for ct in range(2):
                    evacuate(f"g{ct}", both(f"g{ct}", ZS[:, ct]), ACT.Silu)
                act.wait_ge(s["f_ready"], 4)
                link(f(PF, PF, ACT.Ln))
                link(f(SI, SI, ACT.Ln))
                act.sem_inc(s["gla_act"], 1)
                gla(1)

                evacuate("cq0", both("cq0", CQ[:, 0]))
                evacuate("cq1", both("cq1", CQ[0:64, 1], 64), rows=64)
                evacuate("ckv", both("ckv", KVR))
                evacuate("kr", both("kr", KR[0:QK_A, :], QK_A))
                for p in range(2):
                    act.wait_ge(freed[p], len([j for j in range(job["kr"] + 1) if j % 2 == p]))
                f(SQA[:, 0], CQ[:, 0], ACT.Square).then_inc(s["aq_sq"], 1)
                f(SQA[0:64, 1], CQ[0:64, 1], ACT.Square).then_inc(s["aq_sq"], 1)
                for n, (name, size) in enumerate((("msq", Q_RANK), ("mskv", KV_RANK))):
                    j = job[name]
                    act.wait_ge(s["done"], j + 1)
                    if n == 0:
                        f(SQA[:, 0], KVR, ACT.Square).then_inc(s["aq_sq"], 1)
                    else:
                        act.wait_ge(s["aq_norm"], 2)
                    for b, t0, k in SEGS:
                        link(f(RA[:, t0:t0 + k], group_cols(j, b, k), ACT.Ln, scale=1.0 / size, bias=eps))
                    act.sem_inc(freed[j % 2], 1)
                    finish(f(RA, RA, ACT.Exp, scale=-0.5), s["aq_rstd"], n + 1)
                act.wait_ge(s["cache_turned"], 1)
                link(f(CKN[:, TOK:EXT], banks[:, 7, 0:P]))
                link(f(KR[0:QK_A, TOK:EXT], banks[0:QK_A, 7, P:2 * P]))
                finish(f(KD[:, TOK:EXT], banks[:, 7, 2 * P:3 * P]), s["cache_ready"], 1)
                for h in range(4):
                    evacuate(f"q{h}", both(f"q{h}", QA[0:QK_A, h], QK_A))
                for h in range(4):
                    b0 = slot(job[f"k{h}"])
                    evacuate(f"k{h}", [(banks[0:NOPE, b0, :], KA[0:NOPE, h, 0:LAT]), (banks[0:NOPE, b0 + 2, 0:256], KA[0:NOPE, h, LAT:EXT])])
                b0 = slot(job["va"])
                evacuate("va", [(pair(banks[:, b0 + i, :]), VA[:, 2 * i:2 * i + 2, :]) for i in range(3)])
                evacuate("qd0", both("qd0", QD[:, 0]))
                evacuate("qd1", both("qd1", QD[:, 1]))
                evacuate("kd", both("kd", KD[:, 0:TOK]))
                b0 = slot(job["vd"])
                evacuate("vd", [(banks[:, b0, :].rearrange("p (c n) -> p c n", n=P), VD[:, 0:4, :]), (banks[:, b0 + 1, 0:P], VD[:, 4, :])])
                for p in range(2):
                    act.wait_ge(freed[p], len([j for j in range(job["vd"] + 1) if j % 2 == p]))
                act.sem_inc(s["attn_in_act"], 1)
                link(f(NEWROWS[:, 2 * P + QK_A:3 * P + QK_A], VD[:, 4, :]))
                act.wait_ge(s["new_turned"], 1)
                finish(f(NEWROWS[:, 0:2 * P + QK_A], banks[:, 7, 0:2 * P + QK_A]), s["new_ready"], 1)
                act.wait_ge(s["roped"], 5)
                for i in range(2):
                    f(KA[NOPE:QK_A, 2 * i:2 * i + 2, :], bc(KR[NOPE:QK_A, :].unsqueeze(1), [ROPE, 2, EXT])).then_inc(s["kcopied"], 1)

                def probs(u):
                    un = units[u]
                    n = len(un["tiles"]) * P
                    sc = SM[:, u // 4 % 2, :, un["h"]]
                    act.wait_ge(s["maxed"], u + 1)
                    if u >= 2:
                        act.wait_ge(s["p_turned"], u - 1)
                    src = banks[:, 2 * (u % 2):2 * (u % 2) + 2, :].rearrange("p b n -> p (b n)")[:, 0:n]
                    if un["kind"] == "D":
                        f(sc[:, 3:4], SINK[:, un["h"]:un["h"] + 1], ACT.Exp, bias=sc[:, 1:2])
                    f(PRB[:, u % 2, 0:n], src, ACT.Exp, scale=scale_of(un), bias=sc[:, 1:2], accum_out=sc[:, 2:3]).then_inc(s["expd"], 1)

                probs(0)
                for u, un in enumerate(units):
                    if u + 1 < len(units):
                        probs(u + 1)
                    n = len(un["tiles"]) * P
                    act.wait_ge(s["p_turned"], u + 1)
                    if u >= 2:
                        act.wait_ge(s["pv_done"], u - 1)
                    f(PTS[:, u % 2, 0:n], banks[:, 4:6, :].rearrange("p b n -> p (b n)")[:, 0:n]).then_inc(s["p_copied"], 1)

                layer_norm(1, lambda: (weights_hi(FFN_JOBS), weights_hi(FFN_JOBS + 1)))
                modulate(2)
                ffn(2)
                layer_norm(2)
                act.sem_inc(arrived, 1)
                act.wait_ge(go, l + 1)

        @blockctx.vector
        def _(dve):
            v = nc.vector
            for n in range(2 * NCH):
                t, half = n // 2, n % 2
                dve.wait_ge(init_turn, n + 1)
                v.tensor_copy(X[:, 4 * half:4 * half + 4, t * P:(t + 1) * P],
                              banks[:, n % 4, :].rearrange("p (k n) -> p k n", k=4)).then_inc(init_copy, 1)
            dve.wait_ge(init_turn, 2 * NCH + 1)
            v.tensor_copy(LBT[:], banks[:, 4, 0:8]).then_inc(init_copy, 1)
            dve.wait_ge(init_copy, 2 * NCH + 1)
            v.tensor_tensor(LBW[:], LBT[:, 0:4], LBT[:, 4:8], ALU.max).then_inc(init_copy, 1)
            dve.wait_ge(init_copy, 2 * NCH + 2)
            v.tensor_tensor(LBT[:].rearrange("p (l c) -> p l c", l=2), LBT[:].rearrange("p (l c) -> p l c", l=2),
                            bc(LBW[:].unsqueeze(1), [P, 2, 4]), ALU.subtract).then_inc(init_lb, 1)
            dve.wait_ge(init_lb, 2)
            v.tensor_tensor(LBW[:], LBT[:, 0:4], LBT[:, 4:8], ALU.add).then_inc(init_lb, 1)
            dve.wait_ge(init_lb, 3)
            v.reciprocal(LBW[:], LBW[:]).then_inc(init_lb, 1)
            dve.wait_ge(init_lb, 4)
            v.tensor_tensor(LBN[:], LBT[:, 4:8], LBW[:], ALU.mult).then_inc(init_lb, 1)
            v.memset(LB[:], 0.0).then_inc(init_lb, 1)
            dve.wait_ge(init_lb, 6)

            with dve.Fori(0, DEPTH) as l:
                link = chain(dve, s["dve_chain"])

                def finish(ins, signal, value):
                    ins.then_inc(signal, 1)
                    dve.wait_ge(signal, value)

                dve.wait_ge(s["par_turned"], 1)
                link(v.tensor_copy(PT1[:], banks[:, 7, 0:ROWS1]))
                finish(v.tensor_copy(PT2[:], banks[:, 7, P:P + ROWS2]), s["par_ready"], 1)
                link(v.tensor_scalar(OML[:], LB[:], -1.0, 1.0, ALU.mult, ALU.add))
                link(v.tensor_scalar(SINK[:, 4:8], SINK[:, 0:4], -1.0, None, ALU.mult))
                for hh in range(2):
                    rows = slice(64 * hh, 64 * hh + 64)
                    sk = SKIP[rows, :].rearrange("p (d c h) -> p d c h", d=2, c=2)
                    link(v.tensor_tensor(DS[rows, :], sk[:, 0, :, hh], sk[:, 1, :, hh], ALU.add))
                dve.wait_ge(s["dt_step"], 1)
                link(v.tensor_scalar(DTP[:, 3:4], DTP[:, 2:3], -1.0, None, ALU.mult))

                def modulation(r0, r1, turned):
                    dve.wait_ge(s["mod_turned"], turned)
                    rows = MOD.rearrange("p s w m g -> p (s w m) g")[:, r0:r1]
                    link(v.tensor_tensor(rows, banks[:, 7, 2 * r0:2 * r1].rearrange("p (r g) -> p r g", g=2),
                                         bc(PT1[:, r0:r1].unsqueeze(2), [P, r1 - r0, 2]), ALU.add))

                modulation(0, 4 * MOD_FIRST, MOD_FIRST)
                for sub in range(2):
                    link(v.tensor_scalar(MOD[:, sub, 1], MOD[:, sub, 1], 1.0, None, ALU.add))
                link(v.tensor_scalar(MOD[:, 0, 2], MOD[:, 0, 2], 0.5, None, ALU.mult))
                dve.sem_inc(s["mod_ready"], 1)

                def weights_lo(n, i=None):
                    dve.wait_ge(s["w_hi"], n + 1 if i is None else i * 2 + (n + 1))
                    v.tensor_tensor(WLO[n % 2], WRAW[n % 2], WHI[n % 2].bitcast(F32), ALU.subtract).then_inc(s["w_lo"], 1)

                def input_lo_tile(sub, m):
                    dve.wait_ge(s["h_hi"], 8 * (sub // 2) + m + 1)
                    v.tensor_tensor(HLO[:, m], GATE[:, m % 2], HHI[:, m].bitcast(F32), ALU.subtract).then_inc(s["h_lo"], 1)

                def scale_residual(sub):
                    dve.wait_ge(s["modded"], 8 * (sub + 1))
                    link(v.tensor_scalar(X, X, float(ALPHA), None, ALU.mult))

                def residual(name, sub, m):
                    j = job[name]
                    dve.wait_ge(s["done"], j + 1)
                    for g, (b, t0, n) in enumerate(SEGS):
                        ins = v.scalar_tensor_tensor(out=X[:, m, t0:t0 + n], in0=group_cols(j, b, n), scalar=MOD[:, sub, 2, m, g:g + 1],
                                                     in1=X[:, m, t0:t0 + n], op0=ALU.mult, op1=ALU.add)
                    ins.then_inc(freed[j % 2], 1)

                def ffn(sub):
                    def hidden(par, c, hid, hi, lo, split_next):
                        dve.wait_ge(s["gated"], hid + 1)
                        v.tensor_tensor(GATE[:, c].rearrange("p (h t) -> p h t", h=2), GATE[:, c].rearrange("p (h t) -> p h t", h=2),
                                        banks[:, 4 * par + 2:4 * par + 4, 0:HALF], ALU.mult).then_inc(s["product"], 1)
                        dve.wait_ge(s["product"], hid + 1)
                        dve.sem_inc(f_freed[par], 1)
                        split_next()
                        dve.wait_ge(s["hid_hi"], hid + 1)
                        v.tensor_tensor(lo, GATE[:, c:c + 1], hi.bitcast(F32), ALU.subtract).then_inc(s["hid_lo"], 1)

                    for g in range(2):
                        n0 = sub // 2 * FFN_JOBS + g * GROUP_JOBS
                        h0 = (sub + g) * FG
                        hi2, lo2 = (x[:, 0:FG - 1].rearrange("p (i c) t -> p i c t", c=2) for x in (HIDHI, HIDLO))
                        with dve.Fori(0, FG // 2) as i:
                            for c in range(2):
                                n = n0 + c
                                hidden(n % 2, c, i * 2 + (h0 + c), hi2[:, bass.ds(i, 1), c, :], lo2[:, bass.ds(i, 1), c, :],
                                       lambda: weights_lo(n + 2, i))
                        n = n0 + FG - 1
                        hidden(n % 2, 0, h0 + FG - 1, HIDHI[:, FG - 1:FG, :], HIDLO[:, FG - 1:FG, :], lambda: weights_lo(n + 2))
                        for m in range(KT_M):
                            n = n0 + FG + m
                            if n + 2 < (sub // 2 + 1) * FFN_JOBS:
                                weights_lo(n + 2)
                            dve.wait_ge(s["f_done"], n + 1)
                            b = 4 * (n % 2)
                            for src, t0, cols, grp in ((banks[:, b, 0:HALF], 0, HALF, 0), (banks[:, b + 1, 0:LAT - HALF], HALF, LAT - HALF, 0),
                                                       (banks[:, b + 1, LAT - HALF:HALF], LAT, CTX, 1)):
                                ins = v.scalar_tensor_tensor(out=X[:, m, t0:t0 + cols], in0=src, scalar=MOD[:, sub, 2, m, grp:grp + 1],
                                                             in1=X[:, m, t0:t0 + cols], op0=ALU.mult, op1=ALU.add)
                            ins.then_inc(f_freed[n % 2], 1)

                def layer_norm(sub, meanwhile=None):
                    dve.wait_ge(s["mean_ready"], sub + 1)
                    for i in range(4):
                        for b, t0, n in SEGS:
                            x2 = X[:, 2 * i:2 * i + 2, t0:t0 + n]
                            ins = v.scalar_tensor_tensor(out=x2, in0=bc(banks[:, 6 + b // 2, 0:n].unsqueeze(1), [P, 2, n]),
                                                         scalar=-1.0 / D_MODEL, in1=x2, op0=ALU.mult, op1=ALU.add)
                        ins.then_inc(s["centred"], 1)
                    if meanwhile:
                        meanwhile()
                    dve.wait_ge(s["rstd"], sub + 1)
                    dve.wait_ge(s["centred"], 4 * sub + 4)
                    for m in range(KT_M):
                        link(v.tensor_tensor(X[:, m, :], X[:, m, :], RS[:], ALU.mult))
                        v.tensor_scalar(X[:, m, :], X[:, m, :], PT1[:, R_LNG + 8 * sub + m:R_LNG + 8 * sub + m + 1],
                                        PT1[:, R_LNB + 8 * sub + m:R_LNB + 8 * sub + m + 1], ALU.mult, ALU.add).then_inc(s["affine"], 1)
                        if sub == 1:
                            if m >= 2:
                                input_lo_tile(2, m - 2)
                    if sub == 1:
                        input_lo_tile(2, 6)
                        input_lo_tile(2, 7)

                weights_lo(0)
                weights_lo(1)
                for m in range(KT_M):
                    input_lo_tile(0, m)
                scale_residual(0)
                ffn(0)
                layer_norm(0)
                scale_residual(1)

                for i in range(6):
                    dve.wait_ge(s["conv_in"], i + 1)
                    if i >= 1:
                        dve.wait_ge(s["bc_ready"], i)
                    for tap in range(TAPS):
                        src = CPAD[:, i % 2, tap:tap + 644]
                        wt = PT2[:, R_CW + 6 * tap + i:R_CW + 6 * tap + i + 1]
                        if tap == 0:
                            link(v.tensor_scalar(CONV, src, wt, None, ALU.mult))
                        else:
                            ins = v.scalar_tensor_tensor(out=CONV, in0=src, scalar=wt, in1=CONV, op0=ALU.mult, op1=ALU.add)
                            if tap < TAPS - 1:
                                link(ins)
                            else:
                                finish(ins, s["conv_out"], i + 1)
                r, e, w1, lg = (DTW[:, k, :] for k in range(4))
                j = job["dt"]
                dve.wait_ge(s["done"], j + 1)
                for b, t0, n in SEGS:
                    link(v.tensor_scalar(r[:, t0:t0 + n], group_cols(j, b, n, 8), DTP[:, 0:1], None, ALU.add))
                dve.sem_inc(freed[j % 2], 1)
                dve.sem_inc(s["dt_step"], 1)
                dve.wait_ge(s["dt_step"], 3)
                finish(v.tensor_scalar(w1, e, 1.0, None, ALU.add), s["dt_step"], 4)
                dve.wait_ge(s["dt_step"], 5)
                t2 = DT_B[:, 0]
                link(v.tensor_scalar(t2, w1, -1.0, None, ALU.add))
                link(v.tensor_tensor(e, e, t2, ALU.subtract))
                link(v.reciprocal(w1, w1))
                link(v.tensor_tensor(e, e, w1, ALU.mult))
                link(v.tensor_tensor(lg, lg, e, ALU.add))
                link(v.scalar_tensor_tensor(out=DT_B[:, 0], in0=r, scalar=0.0, in1=lg, op0=ALU.max, op1=ALU.add))
                finish(v.tensor_scalar(DT_B[:, 1], DT_B[:, 0], DTP[:, 3:4], None, ALU.mult), s["dt_ready"], 1)
                dve.wait_ge(s["bc_ready"], 6)
                for d in range(4):
                    j = job[f"sel{d}"]
                    dve.wait_ge(s["adt_copied"], d + 1)
                    ct = d % 2
                    for b, t0, n in SEGS:
                        ins = v.tensor_tensor((KF, KB)[d // 2][:, ct, t0:t0 + n], group_cols(j, b, n), BB[:, ct, t0:t0 + n], ALU.mult)
                    ins.then_inc(freed[j % 2], 1)

                def gla(mx):
                    for p in range(2):
                        dve.wait_ge(freed[p], len([j for j in range(job[f"y{mx}"]) if j % 2 == p]))
                    finish(v.tensor_tensor(KL, KF, KB, ALU.add), s["level_k"], mx + 1)

                    def merge(lev):
                        mask = bc(masks[:, lev, :].unsqueeze(1).unsqueeze(1), [P, 2, 2, P])
                        for c in range(NCH):
                            n = (mx * (LEVELS + 1) + lev) * NCH + c
                            dve.wait_ge(s["att_done"], n + 1)
                            v.copy_predicated(ATT[:, c].rearrange("p (a b) n -> p a b n", a=2), mask,
                                              banks[:, 2 * (n % 3):2 * (n % 3) + 2, 0:256].rearrange("p a (b n) -> p a b n", b=2)).then_inc(s["att_used"], 1)

                    merge(0)
                    for lev in range(1, LEVELS + 1):
                        m = 2 ** (lev - 1)
                        at = LEVELS * mx + lev
                        dve.wait_ge(s["exps"], 4 * at)
                        v.tensor_tensor(QL, QL, Q, ALU.mult).then_inc(s["prods"], 1)
                        (k1, k2) = halves(KL, m)
                        v.tensor_tensor(k1, k1, halves(KF, m)[0], ALU.mult).then_inc(s["prods"], 1)
                        v.tensor_tensor(k2, k2, halves(KB, m)[1], ALU.mult).then_inc(s["prods"], 1)
                        merge(lev)
                    if mx == 0:
                        modulation(4 * MOD_FIRST, 72, MOD_FILLS)
                        link(v.tensor_scalar(MOD[:, 2, 1], MOD[:, 2, 1], 1.0, None, ALU.add))
                        link(v.tensor_scalar(MOD[:, 2, 2], MOD[:, 2, 2], 0.5, None, ALU.mult))
                        dve.sem_inc(s["mod_ready"], 1)
                    dve.wait_ge(s["fin_exp"], 4 * mx + 4)
                    for x, y in ((PF, Q), (SI, Q)):
                        v.tensor_tensor(x, x, y, ALU.mult).then_inc(s["fin_prod"], 1)
                    for x, y in ((KF, SE), (KB, PB)):
                        v.tensor_tensor(x, x, y, ALU.mult).then_inc(s["fin_prod"], 1)
                    dve.wait_ge(s["sin_zero"], mx + 1)
                    if mx == 0:
                        dve.wait_ge(s["s0_turned"], 1)
                        src = banks[:, 6, 0:256].rearrange("p (d n) -> p d n", d=4)
                    else:
                        src = S0C[:].rearrange("p (d n) -> p d n", d=4)
                    for d in range(2):
                        for hh in range(2):
                            rows = slice(64 * hh, 64 * hh + 64)
                            link(v.tensor_copy(SIN[rows, 3 * d, 2 * d:2 * d + 2, rows], src[rows, 2 * d:2 * d + 2, :]))
                    dve.sem_inc(s["s0_ready"], 1)
                    for t in range(4):
                        dve.wait_ge(s["cs_done"], 4 * mx + t + 1)
                        cs = banks[:, 4 + t % 2, :].rearrange("p (d n) -> p d n", d=4)
                        for hh in range(2):
                            rows = slice(64 * hh, 64 * hh + 64)
                            if t == 3:
                                link(v.tensor_copy(FIN[rows, :].rearrange("p (d n) -> p d n", d=4), cs[rows, :, rows]))
                                continue
                            for d in range(4):
                                src_c, dst_c = (t, t + 1) if d < 2 else (3 - t, 2 - t)
                                link(v.scalar_tensor_tensor(out=SIN[rows, dst_c, d, rows], in0=SIN[rows, src_c, d, rows],
                                                            scalar=DEC[rows, d // 2, d % 2, src_c:src_c + 1], in1=cs[rows, d, rows],
                                                            op0=ALU.mult, op1=ALU.add))
                        dve.sem_inc(s["cs_used"], 1)
                    dve.sem_inc(s["fin_out"], 1)
                    dve.sem_inc(s["sin_ready"], 1)
                    j = job[f"y{mx}"]
                    b0 = slot(j)
                    dve.wait_ge(s["done"], j + 1)
                    parts = ((banks[:, b0:b0 + 2, :], slice(0, LAT)), (banks[:, b0 + 2, 0:256].rearrange("p (k n) -> p k n", k=2), slice(LAT, TOK)))
                    for src, cols in parts:
                        if mx == 1:
                            link(v.tensor_copy(Y[:, :, cols], src))
                        else:
                            for ct in range(2):
                                link(v.scalar_tensor_tensor(out=Y[:, ct, cols], in0=XT[:, ct, cols], scalar=DS[:, ct:ct + 1],
                                                            in1=src[:, ct], op0=ALU.mult, op1=ALU.add))
                    dve.sem_inc(freed[j % 2], 1)
                    if mx == 0:
                        link(v.tensor_tensor(Y, Y, ZS, ALU.mult))
                    dve.sem_inc(s["y_ready"], 1)
                    dve.wait_ge(s["y_rstd"], mx + 1)
                    g0 = (R_SN, R_HN)[mx]
                    for ct in range(2):
                        dst = MIX[:, 2 + ct] if mx == 0 else Y[:, ct]
                        link(v.scalar_tensor_tensor(out=dst, in0=Y[:, ct], scalar=PT2[:, g0 + ct:g0 + ct + 1], in1=RB[:, ct],
                                                    op0=ALU.mult, op1=ALU.mult))
                    if mx == 1:
                        link(v.tensor_tensor(MIX[:, 4:6], Y, ZS, ALU.mult))
                    dve.sem_inc(s["mixed_ready"], 1)

                gla(0)
                for i in range(4):
                    dve.wait_ge(s["f_raw"], i + 1)
                    d, ct = i // 2, i % 2
                    lb, oml = LB[:, i:i + 1], OML[:, i:i + 1]
                    fg, key = (PF, SI)[d][:, ct], (KF, KB)[d][:, ct]
                    link(v.tensor_scalar(fg, fg, oml, lb, ALU.mult, ALU.add))
                    link(v.tensor_scalar(key, key, oml, None, ALU.mult))
                    finish(v.tensor_scalar(fg, fg, F_MIN, None, ALU.max), s["f_ready"], i + 1)
                gla(1)

                dve.wait_ge(s["aq_rstd"], 1)
                for ct, rows in ((0, P), (1, 64)):
                    v.scalar_tensor_tensor(out=CQN[0:rows, ct], in0=CQ[0:rows, ct], scalar=PT2[0:rows, R_QN + ct:R_QN + ct + 1],
                                           in1=RA[0:rows], op0=ALU.mult, op1=ALU.mult).then_inc(s["aq_norm"], 1)
                dve.wait_ge(s["aq_rstd"], 2)
                v.scalar_tensor_tensor(out=CKN[:, 0:TOK], in0=KVR, scalar=PT2[:, R_KVN:R_KVN + 1], in1=RA,
                                       op0=ALU.mult, op1=ALU.mult).then_inc(s["akv_norm"], 1)
                for n, (ap, rows) in enumerate(rotated):
                    cos, sin = (cc("cos_a", QK_A), cc("sin_a", QK_A)) if rows == QK_A else (cc("cos_d"), cc("sin_d"))
                    dve.wait_ge(s["rot_done"], n + 1)
                    finish(v.tensor_tensor(ROT[0:rows], banks[0:rows, 6, :], sin, ALU.mult), s["rot_used"], n + 1)
                    link(v.tensor_tensor(ap, ap, cos, ALU.mult))
                    finish(v.tensor_tensor(ap, ap, ROT[0:rows], ALU.add), s["roped"], n + 1)

                def row_max(u):
                    un = units[u]
                    sc = SM[:, u // 4 % 2, :, un["h"]]
                    n = len(un["tiles"]) * P
                    src = banks[:, 2 * (u % 2):2 * (u % 2) + 2, :].rearrange("p b n -> p (b n)")[:, 0:n]
                    dve.wait_ge(s["scored"], u + 1)
                    link(v.reduce_max(sc[:, 0:1], src, AX_X))
                    if un["kind"] == "A":
                        ins = v.tensor_scalar(sc[:, 1:2], sc[:, 0:1], -scale_of(un), None, ALU.mult)
                    else:
                        ins = v.tensor_scalar(sc[:, 1:2], sc[:, 0:1], -scale_of(un), SINK[:, 4 + un["h"]:5 + un["h"]], ALU.mult, ALU.min)
                    ins.then_inc(s["maxed"], 1)

                row_max(0)
                for u in range(len(units) + 4):
                    if u + 1 < len(units):
                        row_max(u + 1)
                    g = u // 4 - 1
                    if g < 0:
                        continue
                    un, sc = units[4 * g], SM[:, g % 2]
                    if u % 4 == 1:
                        dve.wait_ge(s["pv_done"], 4 * g + 4)
                        total = sc[:, 2]
                        if un["kind"] == "D":
                            link(v.tensor_tensor(sc[:, 4], sc[:, 2], sc[:, 3], ALU.add))
                            total = sc[:, 4]
                        link(v.reciprocal(sc[:, 5], total))
                        v.tensor_tensor(ON[:, g % 2].rearrange("p (h n) -> p h n", h=4),
                                        banks[:, 6 + g % 2, 0:256].rearrange("p (h n) -> p h n", h=4),
                                        bc(sc[:, 5].unsqueeze(2), [P, 4, 64]), ALU.mult).then_inc(s["on_ready"], 1)
                    if u % 4 == 3:
                        tile = 0 if un["kind"] == "A" else 6
                        dve.wait_ge(s["on_turned"], g + 1)
                        v.tensor_copy(MIX[:, tile:tile + 2, un["q"]:un["q"] + P],
                                      banks[:, 6 + g % 2, 256:512].rearrange("p (k n) -> p k n", k=2)).then_inc(s["on_used"], 1)
                for m in range(KT_M):
                    residual(f"o{m}", 1, m)
                layer_norm(1, lambda: (weights_lo(FFN_JOBS), weights_lo(FFN_JOBS + 1)))
                scale_residual(2)
                ffn(2)
                layer_norm(2)
                dve.wait_ge(s["affine"], 24)
                link(v.tensor_tensor(LB[:], LB[:], LBN[:], ALU.add))
                dve.sem_inc(arrived, 1)
                dve.wait_ge(go, l + 1)

            for n in range(2 * NCH):
                t, half = n // 2, n % 2
                dve.wait_ge(fin_turn, n + 1)
                v.tensor_copy(XIN[:, t, half * 512:(half + 1) * 512], banks[:, n % 4, :]).then_inc(fin_copy, 1)

        @blockctx.gpsimd
        def _(pool):
            g = nc.gpsimd
            g.memset(CKT[:, P:P + NOPE], 0.0).then_inc(init_ready, 1)
            pool.wait_ge(init_ready, 1)

            with pool.Fori(0, DEPTH) as l:
                link = chain(pool, s["pool_chain"])
                pool.wait_ge(s["modded"], 16)
                for c0, c1 in ((0, 2), (2 + LAT, 6 + LAT), (6 + TOK, 8 + TOK)):
                    link(g.memset(CPAD[:, :, c0:c1], 0.0))
                pool.sem_inc(s["pads"], 1)
                sums_done = [0]
                for mx in range(2):
                    if mx == 1:
                        pool.wait_ge(s["mixed_ready"], 1)
                    link(g.memset(SIN, 0.0))
                    pool.sem_inc(s["sin_zero"], 1)
                    pool.wait_ge(s["gla_act"], mx + 1)
                    pool.wait_ge(s["level_k"], mx + 1)
                    link(g.memset(SE, 0.0))
                    link(g.memset(PB, 0.0))
                    pool.sem_inc(s["excl_zero"], 1)
                    for lev in range(1, LEVELS + 1):
                        m = 2 ** (lev - 1)
                        nb = 2 * TOK // (2 * m)
                        pool.wait_ge(s["exps"], 4 * (LEVELS * mx + lev))
                        (p1, p2), (i1, i2), (e1, _), (_, b2) = (halves(x, m) for x in (PF, SI, SE, PB))
                        wide = lambda ap: bc(ap, [P, nb, m])
                        for dst, add in ((e1, p2[:, :, m - 1:m]), (b2, i1[:, :, 0:1]), (p2, p1[:, :, m - 1:m]), (i1, i2[:, :, 0:1])):
                            ins = g.tensor_tensor(dst, dst, wide(add), ALU.add)
                            ins.then_inc(s["sums"], 1)
                            sums_done[0] += 1
                            pool.wait_ge(s["sums"], sums_done[0])
                pool.sem_inc(arrived, 1)
                pool.wait_ge(go, l + 1)


_INS = ["x_prompt", "x_sample", "cache_a_ckv", "cache_a_krope", "state_b_ssm", "state_c_hgrn", "cache_d_k", "cache_d_v",
        "c", "c_ctx", "w_mod", "b_mod", "ln_g", "ln_b", "ffn_w_gu", "ffn_w_down", "w_in", "w_out", "mla_q_norm",
        "mla_kv_norm", "mla_w_uq", "mla_w_ukv", "ssd_conv_w", "ssd_conv_b", "ssd_a_log", "ssd_dt_bias", "ssd_d",
        "ssd_norm", "hgrn_lb_logits", "hgrn_norm", "gqa_sink"]
_OUTS = [("y_p", (1, CTX, D_MODEL)), ("y_s", (1, LAT, D_MODEL)), ("out_ckv", (1, DEPTH, CTX, KV_RANK)),
         ("out_krope", (1, DEPTH, CTX, ROPE)), ("out_b", (1, DEPTH, 2, 4, 64, 64)), ("out_c", (1, DEPTH, 2, 4, 64, 64)),
         ("out_dk", (1, DEPTH, CTX, 2, 64)), ("out_dv", (1, DEPTH, CTX, 2, 64))]


def kernel(**inputs):
    import concourse.bacc as bacc
    from concourse.bass_utils import run_bass_kernel_spmd

    nc = bacc.Bacc("TRN2", target_bir_lowering=False, num_devices=1)
    consts, const_at = constants()
    arrays, aps = {"in_consts": consts}, {}
    aps["consts"] = nc.dram_tensor("in_consts", consts.shape, F32, kind="ExternalInput").ap()
    for name in _INS:
        x = np.ascontiguousarray(inputs[name])
        arrays[f"in_{name}"] = x
        aps[name] = nc.dram_tensor(f"in_{name}", x.shape, mybir.dt.from_np(x.dtype), kind="ExternalInput").ap()
    for name, shape in _OUTS:
        aps[name] = nc.dram_tensor(name, shape, F32, kind="ExternalOutput").ap()
    trunk_kernel(nc, aps, consts, const_at)
    r = run_bass_kernel_spmd(nc, [arrays], core_ids=[0])
    return tuple(r.results[0][name] for name, _ in _OUTS)
```

```python
from contextlib import ExitStack

import numpy as np
import concourse.bass as bass
from concourse import mybir
from concourse.alu_op_type import AluOpType as ALU

F32 = mybir.dt.float32
F32R = mybir.dt.float32r
I32 = mybir.dt.int32
ACT = mybir.ActivationFunctionType
AX_X = mybir.AxisListType.X

P = 128
D_MODEL, DEPTH, LAT, CTX, PAST = 1024, 2, 512, 128, 128
TOK = LAT + CTX
EXT = TOK + PAST
KT_M = D_MODEL // P
D_FF = 2816
FT = D_FF // P
N_SUB = 3
ALPHA = (2 * DEPTH) ** 0.25
EPS = 1e-6
F_MIN = 1e-6
NEG = -1e30
GRID_W = 64
ROPE_BASE = 10000.0
H_A, NOPE, ROPE, V_A, Q_RANK, KV_RANK = 4, 64, 32, 64, 192, 128
QK_A = NOPE + ROPE
TAPS = 5
NCH = TOK // P
LEVELS = 7
SLOT = 8 * 512
SEGS = ((0, 0, LAT), (2, LAT, CTX))

C_CQ, C_CKV, C_Z, C_BC, C_DT = 0, 192, 352, 864, 1120
C_CQH, C_FB, C_G, C_DQ, C_DK = 1128, 1640, 2152, 2408, 2664

R_BMOD, R_LNG, R_LNB = 0, 72, 96
R_QN, R_KVN, R_CW, R_CB, R_SN, R_HN = 0, 2, 3, 33, 39, 41
ROWS1, ROWS2 = 120, 43
FG = FT // 2
GROUP_JOBS = FG + KT_M
FFN_JOBS = 2 * GROUP_JOBS
HALF = TOK // 2
RAW = 2 * KT_M * P
MOD_FILLS, MOD_FIRST, MOD_NORM = 18, 10, 12
SIDE = ("g0", "g1", "hq0", "f0", "hq1", "cq0", "cq1", "ckv", "kr", "qd0", "qd1", "kd", "vd")
N_SMALL = 46


def constants():
    parts, at, width = [], {}, 0

    def put(name, a):
        nonlocal width
        b = np.zeros((P, a.shape[1]), np.float32)
        b[:a.shape[0]] = a
        parts.append(b)
        at[name] = (width, a.shape[1])
        width += a.shape[1]

    t = np.arange(LAT)
    row, col = (t // GRID_W).astype(np.float32), (t % GRID_W).astype(np.float32)

    def rope(dim):
        r = dim // 2
        half = r // 2
        inv = (ROPE_BASE ** (-np.arange(half, dtype=np.float32) / half)).astype(np.float32)
        cos, sin, swap = np.zeros((dim, LAT)), np.zeros((dim, LAT)), np.zeros((dim, dim))
        for a, pos in enumerate((row, col)):
            ang = (pos[None, :] * inv[:, None]).astype(np.float32)
            lo, hi = a * r + np.arange(half), a * r + half + np.arange(half)
            cos[lo], cos[hi] = np.cos(ang), np.cos(ang)
            sin[lo], sin[hi] = -np.sin(ang), np.sin(ang)
            swap[hi, lo] = 1
            swap[lo, hi] = 1
        return cos, sin, swap

    i = np.arange(P)
    put("ident", np.eye(P))
    put("ones", np.ones((P, P)))
    put("block", (i[:, None] // 64 == i[None, :] // 64).astype(np.float32))
    cos, sin, swap = rope(ROPE)
    ca, sa, pa = np.ones((QK_A, LAT)), np.zeros((QK_A, LAT)), np.zeros((QK_A, QK_A))
    ca[NOPE:], sa[NOPE:], pa[NOPE:, NOPE:] = cos, sin, swap
    put("cos_a", ca), put("sin_a", sa), put("swap_a", pa)
    cos, sin, swap = rope(64)
    pd = np.zeros((P, P))
    pd[:64, :64], pd[64:, 64:] = swap, swap
    put("cos_d", np.tile(cos, (2, 1))), put("sin_d", np.tile(sin, (2, 1))), put("swap_d", pd)
    put("far_before", np.where(i[None, :] >= i[:, None], 0.0, NEG))
    put("far_after", np.where(i[None, :] <= i[:, None], 0.0, NEG))
    sel = np.zeros((8, 4, P))
    for d in range(2):
        for ct in range(2):
            for p in range(P):
                sel[d * 4 + ct * 2 + p // 64, d * 2 + ct, p] = 1
    put("sel", sel.reshape(8, 4 * P))
    masks = [np.eye(P)]
    for lev in range(1, LEVELS + 1):
        m = 2 ** (lev - 1)
        same = i[:, None] // (2 * m) == i[None, :] // (2 * m)
        masks.append(same & (i[:, None] // m != i[None, :] // m))
    put("masks", np.concatenate([np.asarray(m, np.float32) for m in masks], 1))
    put("eps", np.full((P, 1), EPS))
    return np.concatenate(parts, 1).astype(np.float32), at


def plan_layer():
    fills = [(f"mod{i}", 1) for i in range(MOD_NORM)] + [("zx", 1), ("bc", 8)]
    fills += [(f"mod{i}", 1) for i in range(MOD_NORM, MOD_FILLS)]
    fills += [("g", 1), ("qf", 1), ("fi", 1), ("a", 1), ("d", 5), ("o0", 1), ("o1", 1)]
    number, total, loaded = {}, [0, 0], []
    for n, (name, k) in enumerate(fills):
        number[name] = n
        total[n % 2] += 16 * k
        loaded.append(total[n % 2])
    jobs = ["x0", "x1", "dt", "b0", "b1", "c0", "c1", "z0", "sel0", "sel1", "z1", "sel2", "sel3", "y0", "ms0"]
    jobs += ["f1", "f2", "f3", "iv", "y1", "ms1"]
    jobs += ["msq", "mskv"] + [f"q{h}" for h in range(4)] + [f"k{h}" for h in range(4)] + ["va"]
    jobs += [f"o{m}" for m in range(KT_M)]
    job = {n: i for i, n in enumerate(jobs)}
    units = []
    for kind in "AD":
        for t in (0, 1, 2, 3, None):
            for h in range(4):
                if t is None:
                    units.append(dict(kind=kind, h=h, q=LAT, lo=4, hi=5, cache=False, t=None, tiles=[4]))
                    continue
                lo, hi = (0, 4) if kind == "A" else (max(t - 1, 0), min(t + 2, 4))
                units.append(dict(kind=kind, h=h, q=t * P, lo=lo, hi=hi, cache=True, t=t,
                                  tiles=list(range(lo, hi)) + [5]))
    return number, loaded, job, units


def trunk_kernel(nc, a, consts, const_at):
    number, loaded_at, job, units = plan_layer()
    with ExitStack() as ctx:
        def sb(name, cols, rows=P):
            return ctx.enter_context(nc.sbuf_tensor(name, [rows, cols], F32))

        def sem(name):
            return ctx.enter_context(nc.semaphore(name))

        banks = ctx.enter_context(nc.psum_tensor("banks", [P, 8, 512], F32))

        cst = sb("cst", consts.shape[1])
        X = sb("x_res", KT_M * TOK)[:].rearrange("p (k t) -> p k t", k=KT_M)
        WU = sb("w_mla", 2 * 384 + 512)
        W_UQ = WU[:, 0:768].rearrange("p (k c) -> p k c", k=2)
        W_UKV = WU[:, 768:1280]
        PR1, PR2 = sb("par_rows1", P), sb("par_rows2", P)
        PT1, PT2 = sb("par1", ROWS1), sb("par2", ROWS2)
        SC = sb("cond", 16)[:].rearrange("p (k g) -> p k g", k=8)
        MOD = sb("mod", 144)[:].rearrange("p (s w m g) -> p s w m g", s=3, w=3, m=8)
        W_DT = sb("w_dt", 64)[:].rearrange("p (k c) -> p k c", k=8)
        LBT, LB, LBN, OML = sb("lb_t", 24), sb("lb", 4), sb("lb_next", 4), sb("one_minus_lb", 4)
        LBW = sb("lb_work", 4)
        DTP = sb("dt_par", 4, 8)
        SKIP, DS = sb("skip_par", 8), sb("skip", 2)
        SINK = sb("sink", 8)
        S0B, S0C = sb("s0_ssd", 512, 64), sb("s0_hgrn", 256)
        FIN, FINT = sb("fin", 256), S0B
        DEC = sb("chunk_decay", 20)[:].rearrange("p (d c h) -> p d c h", d=2, c=2)
        RS = sb("rstd", TOK)
        SM = sb("softmax_cols", 48)[:].rearrange("p (g c h) -> p g c h", g=2, c=6)
        CKT = sb("cache_rows", 3 * P)
        NEWROWS = sb("new_rows", 512)
        MROW = NEWROWS[0:2, :]
        ARENA = 20480
        with ExitStack() as mixers:
            def msb(name, cols):
                return mixers.enter_context(nc.sbuf_tensor(name, [P, cols], F32))
            H = msb("h_mod", KT_M * TOK)[:].rearrange("p (k t) -> p k t", k=KT_M)
            mixed = msb("mixed", KT_M * TOK)
            MIX = mixed[:].rearrange("p (k t) -> p k t", k=KT_M)
            W = msb("w_slots", 2 * SLOT)[:].rearrange("p (s c) -> p s c", s=2)
            arena = msb("arena", ARENA)
        def rsb(name, cols):
            return ctx.enter_context(nc.sbuf_tensor(name, [P, cols], F32R))
        HHI = rsb("h_hi", KT_M * TOK)[:].rearrange("p (k t) -> p k t", k=KT_M)
        HLO = rsb("h_lo", KT_M * TOK)[:].rearrange("p (k t) -> p k t", k=KT_M)
        rsb("raw_gap", SLOT)
        w_split0 = rsb("w_split0", 2 * RAW)
        HIDHI = rsb("hid_hi", FG * TOK)[:].rearrange("p (k t) -> p k t", k=FG)
        HIDLO = rsb("hid_lo", FG * TOK)[:].rearrange("p (k t) -> p k t", k=FG)
        w_split1 = rsb("w_split1", 2 * RAW)
        WHI = [w[:, 0:RAW] for w in (w_split0, w_split1)]
        WLO = [w[:, RAW:2 * RAW] for w in (w_split0, w_split1)]
        WRAW = [W[:, 0, i * RAW:(i + 1) * RAW] for i in range(2)]

        def view(first, k, n):
            return arena[:, first:first + k * n].rearrange("p (k n) -> p k n", k=k)

        LBR = arena[0:24, 5120:5248]
        GATE, SQX = view(2 * FG * TOK + 2 * RAW, 2, TOK), view(0, KT_M, TOK)
        Q, KF, KB, PF, SE, SI, PB = (view(i * 1280, 2, TOK) for i in range(7))
        QL, KL = view(8960, 2, TOK), view(10240, 2, TOK)
        KTOK = arena[:, 8960:11520].rearrange("p (c d n) -> p c d n", c=5, d=4)
        CPAD = view(8960, 2, 648)
        CONV = arena[:, 8960 + 1296:8960 + 1296 + 644]
        V = view(11520, 5, 256)
        ATT = arena[:, 12800:15360].rearrange("p (c h n) -> p c h n", c=5, h=4)
        DTW = arena[0:8, 12800:15360].rearrange("p (k n) -> p k n", k=4)
        DT_B = arena[0:8, 5120:6400].rearrange("p (k n) -> p k n", k=2)
        SIN = arena[:, 15360:17920].rearrange("p (c d n) -> p c d n", c=5, d=4)
        XT, ZS = view(17920, 2, TOK), view(19200, 2, TOK)
        BB = PB
        Y, SQ, RB = SE, PB, KF
        CQ, CQN, SQA = MIX[:, 6:8], view(1280, 2, TOK), view(0, 2, TOK)
        KVR, CKN, RA = RS[:], arena[:, 4480:5248], arena[:, 12800:12800 + TOK]
        KR = mixed[:, 0:EXT]
        QA, KA = view(6656, 4, TOK), view(9216, 4, EXT)
        VA, VD_CACHE = view(12288, 6, 256), arena[:, 13824:13824 + P]
        ROT = arena[:, 14592:14592 + LAT]
        ON = view(14592, 2, 256)
        PRB = view(15104, 2, 640)
        PTS = view(16384, 2, 640)
        QD, KD = view(17920, 2, TOK), arena[:, 19200:19200 + EXT]
        VD_LAT = view(19200 + EXT, 4, P)
        VD_CTX = NEWROWS[:, 2 * P + QK_A:3 * P + QK_A]
        VD = [VD_LAT[:, i] for i in range(4)] + [VD_CTX, VD_CACHE]
        XIN = view(0, 5, D_MODEL)

        def cc(name, rows=P):
            c0, n = const_at[name]
            return cst[0:rows, c0:c0 + n]

        ident, ones, block1 = cc("ident"), cc("ones"), cc("block")
        masks = cc("masks").bitcast(I32).rearrange("p (l n) -> p l n", l=LEVELS + 1)
        sel = cc("sel", 8).rearrange("p (d n) -> p d n", d=4)
        eps = cc("eps")

        init_load, init_turn, init_copy, init_lb, init_ready = (sem(n) for n in (
            "init_load", "init_turn", "init_copy", "init_lb", "init_ready"))
        init_cond = sem("init_cond")
        fin_turn, fin_copy, fin_store = sem("fin_turn"), sem("fin_copy"), sem("fin_store")
        arrived, pool_arrived, go = sem("arrived"), sem("pool_arrived"), sem("go")
        names = ("par_load pool_load par_turned par_ready mod_row mrow_copied mod_turned mod_ready "
                 "w_hi w_lo f_done h_hi h_lo product hid_hi hid_lo modded "
                 "w_used done gated centred squared var_ready rstd affine "
                 "pads conv_in conv_out xt_turned v_ready dt_ready bc_ready gla_act "
                 "level_k att_done att_used exps prods sums fin_exp fin_prod k_turned k_copied "
                 "cs_done cs_used sin_zero s0_turned s0_ready sin_ready fin_out ft_turned ft_ready "
                 "y_ready ysq y_rstd excl_zero dt_step adt_copied f_raw f_ready mixed_ready "
                 "aq_sq aq_rstd aq_norm akv_norm cache_turned cache_ready rot_done rot_used roped kcopied attn_in_act "
                 "new_turned new_ready scored maxed expd p_turned p_copied pv_done on_ready on_turned on_used "
                 "side_done side_freed sq_summed x_summed mean_ready normed "
                 "state_store small_store act_chain dve_chain pool_chain")
        s = {n: sem(n) for n in names.split()}
        w_loaded = [sem("w_loaded_even"), sem("w_loaded_odd")]
        freed = [sem("freed_even"), sem("freed_odd")]
        raw_loaded = [sem("raw_loaded_even"), sem("raw_loaded_odd")]
        f_freed = [sem("ffn_freed_even"), sem("ffn_freed_odd")]
        late = ("w_hi w_lo f_done h_hi h_lo product hid_hi hid_lo modded gated mean_ready centred squared sq_summed "
                "x_summed normed var_ready rstd affine act_chain dve_chain").split()
        early_sems = [x for n, x in s.items() if n not in late] + w_loaded + freed
        late_sems = [s[n] for n in late] + raw_loaded + f_freed

        def slot(j):
            return 3 * (j % 2)

        def w_slot(name, k, c):
            return W[:, number[name] % 2, 0:k * c].rearrange("p (k c) -> p k c", k=k)

        def chain(eng, signal):
            count = [0]

            def link(ins):
                count[0] += 1
                ins.then_inc(signal, 1)
                eng.wait_ge(signal, count[0])
            return link

        def bc(ap, shape):
            return ap.broadcast_to(shape)

        rotated = [(KR[0:QK_A, 0:LAT], QK_A)] + [(QD[:, i, 0:LAT], P) for i in range(2)] + [(KD[:, 0:LAT], P)]
        rotated += [(QA[0:QK_A, h, 0:LAT], QK_A) for h in range(4)]

        blockctx = ctx.enter_context(nc.Block())

        @blockctx.sync
        def _(sp):
            sp.dma_start(cst[:], a["consts"]).then_inc(init_load, 16)
            for t in range(4):
                sp.dma_start(XIN[:, t, :], a["x_sample"][0, t * P:(t + 1) * P, :]).then_inc(init_load, 16)
            sp.dma_start(XIN[:, 4, :], a["x_prompt"][0]).then_inc(init_load, 16)
            sp.dma_start(LBR[0:8], a["hgrn_lb_logits"].rearrange("l d (t p) -> (l d t) p", p=P)).then_inc(init_load, 16)
            sp.dma_start(LBR[8:16], a["c"][0].rearrange("(r p) -> r p", p=P)).then_inc(init_load, 16)
            sp.dma_start(LBR[16:24], a["c_ctx"].rearrange("(r p) -> r p", p=P)).then_inc(init_load, 16)
            sp.wait_ge(init_load, 144)
            sp.wait_ge(init_ready, 1)

            with sp.Fori(0, DEPTH) as l:
                def fill(name, pieces):
                    n = number[name]
                    if n >= 2:
                        sp.wait_ge(s["w_used"], n - 1)
                    for dst, src in pieces:
                        sp.dma_start(dst, src).then_inc(w_loaded[n % 2], 16)

                w_mod = a["w_mod"][l].rearrange("(k p) c -> p k c", p=P)
                w_in = a["w_in"][l].rearrange("(k p) c -> p k c", p=P)
                w_out = a["w_out"][l].rearrange("(k p) c -> p k c", p=P)
                def fill_mod(i):
                    fill(f"mod{i}", [(w_slot(f"mod{i}", 8, 512), w_mod[:, :, i * 512:(i + 1) * 512])])

                small = s["par_load"]
                fill_mod(0)
                fill_mod(1)
                sp.dma_start(PR1[0:72, :], a["b_mod"][l].rearrange("(r p) -> r p", p=P)).then_inc(small, 16)
                sp.dma_start(PR1[72:96, :], a["ln_g"][l].rearrange("s (r p) -> (s r) p", p=P)).then_inc(small, 16)
                sp.dma_start(PR1[96:120, :], a["ln_b"][l].rearrange("s (r p) -> (s r) p", p=P)).then_inc(small, 16)
                sp.dma_start(PR2[0:1, :], a["mla_q_norm"][bass.ds(l, 1), 0:P]).then_inc(small, 16)
                sp.dma_start(PR2[1:2, 0:64], a["mla_q_norm"][bass.ds(l, 1), P:Q_RANK]).then_inc(small, 16)
                sp.dma_start(PR2[1:2, 64:P], a["mla_q_norm"][bass.ds(l, 1), P:Q_RANK]).then_inc(small, 16)
                sp.dma_start(PR2[2:3, :], a["mla_kv_norm"][bass.ds(l, 1), :]).then_inc(small, 16)
                fill_mod(2)
                for tap in range(TAPS + 1):
                    r = R_CW + 6 * tap
                    src = a["ssd_conv_w"][l, tap] if tap < TAPS else a["ssd_conv_b"][l]
                    sp.dma_start(PR2[r:r + 2, :], src[0:256].rearrange("(r p) -> r p", p=P)).then_inc(small, 16)
                    for dup in range(2):
                        sp.dma_start(PR2[r + 2:r + 6, dup * 64:dup * 64 + 64],
                                     src[256:512].rearrange("(r p) -> r p", p=64)).then_inc(small, 16)
                fill_mod(3)
                sp.dma_start(PR2[R_SN:R_SN + 2, :], a["ssd_norm"][l].rearrange("(r p) -> r p", p=P)).then_inc(small, 16)
                sp.dma_start(PR2[R_HN:R_HN + 2, :], a["hgrn_norm"][l].rearrange("(r p) -> r p", p=P)).then_inc(small, 16)
                sp.dma_start(DTP[:, 0:1], a["ssd_dt_bias"][l].rearrange("d (h o) -> (d h) o", o=1)).then_inc(small, 16)
                sp.dma_start(DTP[:, 1:2], a["ssd_a_log"][l].rearrange("d (h o) -> (d h) o", o=1)).then_inc(small, 16)
                sp.dma_start(SKIP[:], a["ssd_d"][bass.ds(l, 1)].rearrange("o d h -> o (d h)").partition_broadcast(P)).then_inc(small, 16)
                sp.dma_start(SINK[:, 0:4], a["gqa_sink"][bass.ds(l, 1)].partition_broadcast(P)).then_inc(small, 16)
                sp.dma_start(W_DT, a["w_in"][l].rearrange("(k p) c -> p k c", p=P)[:, :, C_DT:C_DT + 8]).then_inc(small, 16)
                sp.dma_start(W_UQ[:, 0, :], a["mla_w_uq"][l, 0:P, :]).then_inc(small, 16)
                sp.dma_start(W_UQ[0:64, 1, :], a["mla_w_uq"][l, P:Q_RANK, :]).then_inc(small, 16)
                sp.dma_start(W_UKV, a["mla_w_ukv"][l]).then_inc(small, 16)
                fill_mod(4)
                for d in range(2):
                    for ct in range(2):
                        at = (d * 2 + ct) * P
                        sp.dma_start(S0B[:, at:at + P].rearrange("p (h n) -> p h n", h=2),
                                     a["state_b_ssm"][0, l, d, 2 * ct:2 * ct + 2].rearrange("h p n -> p h n")).then_inc(small, 16)
                        at //= 2
                        sp.dma_start(S0C[:, at:at + 64],
                                     a["state_c_hgrn"][0, l, d, 2 * ct:2 * ct + 2].rearrange("h k v -> (h k) v")).then_inc(small, 16)
                sp.dma_start(CKT[:, 0:P], a["cache_a_ckv"][0, l]).then_inc(small, 16)
                sp.dma_start(CKT[:, P + NOPE:P + QK_A], a["cache_a_krope"][0, l]).then_inc(small, 16)
                sp.dma_start(CKT[:, 2 * P:3 * P], a["cache_d_k"][0, l].rearrange("t h d -> t (h d)")).then_inc(small, 16)
                for i in range(5, MOD_FIRST):
                    fill_mod(i)

                def fill_ffn(sub):
                    w_gu = a["ffn_w_gu"][l, sub // 2].rearrange("(k p) (w c) -> p w k c", p=P, w=2)
                    w_dn = a["ffn_w_down"][l, sub // 2].rearrange("(k p) c -> p k c", p=P)

                    def gate_up(par, col):
                        dst = WRAW[par].rearrange("p (w k c) -> p w k c", w=2, k=KT_M)
                        for w in range(2):
                            sp.dma_start(dst[:, w], w_gu[:, w, :, bass.ds(col, P)]).then_inc(raw_loaded[par], 16)

                    for g in range(2):
                        n0 = sub // 2 * FFN_JOBS + g * GROUP_JOBS
                        if g == 0:
                            for c in range(2):
                                gate_up((n0 + c) % 2, c * P)
                        with sp.Fori(1 if g == 0 else 0, FG // 2) as i:
                            for c in range(2):
                                sp.wait_ge(s["w_lo"], i * 2 + (n0 + c - 1))
                                gate_up((n0 + c) % 2, i * (2 * P) + (g * FG + c) * P)
                        sp.wait_ge(s["w_lo"], n0 + FG - 2)
                        gate_up((n0 + FG - 1) % 2, (g * FG + FG - 1) * P)
                        for m in range(KT_M):
                            n = n0 + FG + m
                            sp.wait_ge(s["w_lo"], n - 1)
                            dst = WRAW[n % 2][:, 0:FG * P].rearrange("p (k c) -> p k c", k=FG)
                            for k0, k1 in ((0, 6), (6, FG)):
                                sp.dma_start(dst[:, k0:k1], w_dn[:, g * FG + k0:g * FG + k1, m * P:(m + 1) * P])\
                                    .then_inc(raw_loaded[n % 2], 16)

                sp.wait_ge(s["w_used"], MOD_FIRST - 1)
                fill_ffn(0)
                sp.wait_ge(s["w_lo"], FFN_JOBS)
                fill_mod(MOD_FIRST)
                sp.wait_ge(s["f_done"], FFN_JOBS)
                fill_mod(MOD_FIRST + 1)
                fill("zx", [(w_slot("zx", 8, 512), w_in[:, :, C_Z:C_Z + 512])])
                pieces = []
                for g in range(4):
                    for dup in range(2):
                        at = (2 * g + dup) * 64
                        pieces.append((w_slot("bc", 8, 512)[:, :, at:at + 64], w_in[:, :, C_BC + g * 64:C_BC + g * 64 + 64]))
                fill("bc", pieces)
                for i in range(MOD_NORM, MOD_FILLS):
                    fill_mod(i)
                fill("g", [(w_slot("g", 8, 256), w_in[:, :, C_G:C_G + 256])])
                fill("qf", [(w_slot("qf", 8, 512), w_in[:, :, C_CQH:C_CQH + 512])])
                fill("fi", [(w_slot("fi", 8, 512), w_in[:, :, C_FB:C_FB + 512])])
                fill("a", [(w_slot("a", 8, 352), w_in[:, :, 0:352])])
                pieces = []
                for h in range(4):
                    at = (2 * (h % 2) + h // 2) * 64
                    pieces.append((w_slot("d", 8, 512)[:, :, at:at + 64], w_in[:, :, C_DQ + h * 64:C_DQ + h * 64 + 64]))
                pieces.append((w_slot("d", 8, 512)[:, :, 256:512], w_in[:, :, C_DK:C_DK + 256]))
                fill("d", pieces)
                sp.wait_ge(s["mixed_ready"], 2)
                sp.dma_start(VD_CACHE, a["cache_d_v"][0, l].rearrange("t h d -> t (h d)")).then_inc(s["pool_load"], 16)
                for i in range(2):
                    fill(f"o{i}", [(w_slot(f"o{i}", 8, 512), w_out[:, :, i * 512:(i + 1) * 512])])
                sp.wait_ge(s["w_used"], number["o1"] + (1 if number["o1"] % 2 == 0 else 0))
                fill_ffn(2)

                for d in range(2):
                    for ct in range(2):
                        at = (d * 2 + ct) * P
                        sp.wait_ge(s["ft_ready"], 1)
                        sp.dma_start(a["out_b"][0, l, d, 2 * ct:2 * ct + 2].rearrange("h p n -> p h n"),
                                     FINT[:, at:at + P].rearrange("p (h n) -> p h n", h=2)).then_inc(s["state_store"], 16)
                        at //= 2
                        sp.wait_ge(s["fin_out"], 2)
                        sp.dma_start(a["out_c"][0, l, d, 2 * ct:2 * ct + 2].rearrange("h k v -> (h k) v"),
                                     FIN[:, at:at + 64]).then_inc(s["state_store"], 16)
                sp.wait_ge(s["new_ready"], 1)
                sp.dma_start(a["out_ckv"][0, l], NEWROWS[:, 0:P]).then_inc(s["small_store"], 16)
                sp.dma_start(a["out_dk"][0, l].rearrange("t h d -> t (h d)"), NEWROWS[:, P:2 * P]).then_inc(s["small_store"], 16)
                sp.dma_start(a["out_krope"][0, l], NEWROWS[:, 2 * P + NOPE:2 * P + QK_A]).then_inc(s["small_store"], 16)
                sp.dma_start(a["out_dv"][0, l].rearrange("t h d -> t (h d)"), VD_CTX).then_inc(s["small_store"], 16)
                sp.wait_ge(s["state_store"], 128)
                sp.wait_ge(s["small_store"], 64)
                sp.wait_ge(pool_arrived, 1)
                for x in early_sems:
                    sp.sem_clear(x)
                sp.sem_clear(pool_arrived)
                sp.wait_ge(arrived, 3)
                for x in late_sems:
                    sp.sem_clear(x)
                sp.sem_clear(arrived)
                sp.sem_inc(go, 1)

            for t in range(NCH):
                sp.wait_ge(fin_copy, 2 * t + 2)
                dst = a["y_s"][0, t * P:(t + 1) * P, :] if t < 4 else a["y_p"][0]
                sp.dma_start(dst, XIN[:, t, :]).then_inc(fin_store, 16)
            sp.wait_ge(fin_store, 16 * NCH)

        @blockctx.tensor
        def _(pe):
            mm = nc.tensor.matmul
            pe.wait_ge(init_load, 144)
            for n in range(2 * NCH):
                t, half = n // 2, n % 2
                if n >= 4:
                    pe.wait_ge(init_copy, n - 3)
                for k in range(4):
                    ins = nc.tensor.transpose(banks[:, n % 4, k * P:(k + 1) * P],
                                              XIN[:, t, (half * 4 + k) * P:(half * 4 + k + 1) * P], ident)
                ins.then_inc(init_turn, 1)
            nc.tensor.transpose(banks[:, 4, 0:24], LBR, ident[0:24, 0:24]).then_inc(init_turn, 1)
            pe.wait_ge(init_copy, 2 * NCH + 1)
            pe.wait_ge(init_cond, 1)

            with pe.Fori(0, DEPTH) as l:
                def slot_free(j):
                    if j >= 2:
                        pe.wait_ge(freed[j % 2], j // 2)

                def weights(name):
                    pe.wait_ge(w_loaded[number[name] % 2], loaded_at[number[name]])

                def product(out, pairs):
                    for i, (lhs, rhs) in enumerate(pairs):
                        ins = mm(out, lhs, rhs, start=i == 0, stop=i == len(pairs) - 1)
                    return ins

                def dense(name, w, c0, m, src, kt, last=False):
                    j = job[name]
                    slot_free(j)
                    for b, t0, n in SEGS:
                        ins = product(banks[0:m, slot(j) + b, 0:n],
                                      [(w[:, k, c0:c0 + m], src[:, k, t0:t0 + n]) for k in range(kt)])
                    ins.then_inc(s["done"], 1)

                def used():
                    pe.wait_ge(s["done"], dense_count[0])
                    pe.sem_inc(s["w_used"], 1)

                def side(name, w, c0, m):
                    k = SIDE.index(name)
                    if k:
                        pe.wait_ge(s["side_freed"], k)
                    if name == "vd":
                        for c in range(NCH):
                            ins = product(banks[:, 6 + c // 4, (c % 4) * P:(c % 4) * P + P],
                                          [(H[:, k, c * P:(c + 1) * P], w[:, k, c0:c0 + m]) for k in range(8)])
                    else:
                        for b, t0, n in SEGS:
                            ins = product(banks[0:m, 6 + b // 2, 0:n], [(w[:, k, c0:c0 + m], H[:, k, t0:t0 + n]) for k in range(8)])
                    ins.then_inc(s["side_done"], 1)

                def side_used(name):
                    pe.wait_ge(s["side_done"], SIDE.index(name) + 1)
                    pe.sem_inc(s["w_used"], 1)

                dense_count = [0]

                def run(name, *args):
                    dense(name, *args)
                    dense_count[0] = job[name] + 1

                def mod_fill(i, bank=6):
                    weights(f"mod{i}")
                    w = w_slot(f"mod{i}", 8, 512)
                    product(banks[0:2, bank, :], [(SC[:, k, :], w[:, k, :]) for k in range(8)]).then_inc(s["mod_row"], 1)
                    pe.wait_ge(s["mod_row"], i + 1)
                    pe.sem_inc(s["w_used"], 1)
                    pe.wait_ge(s["mrow_copied"], i + 1)
                    if i == MOD_FIRST:
                        pe.wait_ge(s["centred"], 4)
                    for m in range(4):
                        at = 256 + (4 * i + m) * 2
                        ins = nc.tensor.transpose(banks[:, 7, at:at + 2], MROW[:, m * P:(m + 1) * P], ident[0:2, 0:2])
                    ins.then_inc(s["mod_turned"], 1)

                for i in range(MOD_FIRST):
                    mod_fill(i)
                    if i == MOD_FIRST - 3:
                        pe.wait_ge(s["par_load"], 16 * N_SMALL)
                        nc.tensor.transpose(banks[:, 5, 0:ROWS1], PR1[0:ROWS1, :], ident[0:ROWS1, 0:ROWS1])
                        nc.tensor.transpose(banks[:, 5, P:P + ROWS2], PR2[0:ROWS2, :], ident[0:ROWS2, 0:ROWS2]).then_inc(s["par_turned"], 1)
                pe.wait_ge(s["par_ready"], 1)

                def ffn(sub):
                    def split_product(b0, par, c0, width, hi, lo, kt, last_hidden=0):
                        whi = WHI[par][:, 0:kt * width].rearrange("p (k c) -> p k c", k=kt) if c0 is None else WHI[par].rearrange("p (w k c) -> p w k c", w=2, k=kt)[:, c0]
                        wlo = WLO[par][:, 0:kt * width].rearrange("p (k c) -> p k c", k=kt) if c0 is None else WLO[par].rearrange("p (w k c) -> p w k c", w=2, k=kt)[:, c0]
                        order = [(hf, k) for hf in range(2) for k in range(kt)]
                        if last_hidden:
                            order = [o for o in order if o[1] < kt - 1] + [(hf, kt - 1) for hf in range(2)]
                        for i, (hf, k) in enumerate(order):
                            t = slice(hf * HALF, (hf + 1) * HALF)
                            if last_hidden and i == 2 * (kt - 1):
                                pe.wait_ge(s["hid_lo"], last_hidden)
                            for w, x in ((wlo, hi), (whi, lo), (whi, hi)):
                                ins = mm(banks[:, b0 + hf, 0:HALF], w[:, k, :], x[:, k, t], start=w is wlo and k == 0,
                                         stop=w is whi and x is hi and k == kt - 1, skip_group_check=True)
                        return ins

                    def gate_up(par):
                        for g in range(2):
                            ins = split_product(4 * par + 2 * g, par, g, P, HHI, HLO, KT_M)
                        ins.then_inc(s["f_done"], 1)

                    def first_gate_up(par):
                        whi, wlo = (x[par].rearrange("p (w k c) -> p w k c", w=2, k=KT_M) for x in (WHI, WLO))
                        for k in range(KT_M):
                            pe.wait_ge(s["h_lo"], 8 * (sub // 2) + k + 1)
                            for g in range(2):
                                for hf in range(2):
                                    t = slice(hf * HALF, (hf + 1) * HALF)
                                    out = banks[:, 4 * par + 2 * g + hf, 0:HALF]
                                    mm(out, wlo[:, g, k], HHI[:, k, t], start=k == 0, stop=False, skip_group_check=True)
                                    mm(out, whi[:, g, k], HLO[:, k, t], start=False, stop=False, skip_group_check=True)
                                    ins = mm(out, whi[:, g, k], HHI[:, k, t], start=False, stop=k == KT_M - 1, skip_group_check=True)
                        ins.then_inc(s["f_done"], 1)

                    for g in range(2):
                        n0 = sub // 2 * FFN_JOBS + g * GROUP_JOBS
                        if g == 0:
                            for c in range(2):
                                if n0 + c >= 2:
                                    pe.wait_ge(f_freed[(n0 + c) % 2], (n0 + c) // 2)
                                pe.wait_ge(s["w_lo"], n0 + c + 1)
                                (gate_up if c else first_gate_up)((n0 + c) % 2)
                        with pe.Fori(1 if g == 0 else 0, FG // 2) as i:
                            for c in range(2):
                                par = (n0 + c) % 2
                                pe.wait_ge(f_freed[par], i + (n0 + c) // 2)
                                pe.wait_ge(s["w_lo"], i * 2 + (n0 + c + 1))
                                gate_up(par)
                        n = n0 + FG - 1
                        pe.wait_ge(f_freed[n % 2], n // 2)
                        pe.wait_ge(s["w_lo"], n + 1)
                        gate_up(n % 2)
                        for m in range(KT_M):
                            n = n0 + FG + m
                            pe.wait_ge(f_freed[n % 2], n // 2)
                            if m == 0:
                                pe.wait_ge(s["hid_lo"], (sub + g + 1) * FG - 1)
                            pe.wait_ge(s["w_lo"], n + 1)
                            split_product(4 * (n % 2), n % 2, None, P, HIDHI, HIDLO, FG,
                                          last_hidden=(sub + g + 1) * FG if m == 0 else 0).then_inc(s["f_done"], 1)
                    mean_product(sub)

                def mean_product(sub):
                    pe.wait_ge(s["x_summed"], KT_M * (sub + 1))
                    for b, t0, n in SEGS:
                        ins = mm(banks[:, 6 + b // 2, 0:n], ones, GATE[:, 0, t0:t0 + n], start=True, stop=True)
                    ins.then_inc(s["mean_ready"], 1)

                def layer_norm(sub):
                    if sub == 0:
                        mod_fill(MOD_FIRST, 2)
                    tiles = (0, 2, 4, 6) if sub == 0 else (0,)
                    for i, k in enumerate(tiles):
                        pe.wait_ge(s["sq_summed"], i + 1 if sub == 0 else 4 + sub)
                        for b, t0, n in SEGS:
                            ins = mm(banks[:, 4 + b // 2, 0:n], ones, SQX[:, k, t0:t0 + n], start=i == 0, stop=i == len(tiles) - 1, skip_group_check=True)
                    ins.then_inc(s["var_ready"], 1)
                    if sub == 0:
                        mod_fill(MOD_FIRST + 1, 2)

                ffn(0)
                layer_norm(0)

                weights("zx")
                w = w_slot("zx", 8, 512)
                for k in range(KT_M):
                    pe.wait_ge(s["modded"], 8 + k + 1)
                    for ct in range(2):
                        for b, t0, n in SEGS:
                            ins = mm(banks[:, slot(job[f"x{ct}"]) + b, 0:n], w[:, k, 256 + ct * P:256 + (ct + 1) * P],
                                     H[:, k, t0:t0 + n], start=k == 0, stop=k == KT_M - 1, skip_group_check=True)
                        if k == KT_M - 1:
                            ins.then_inc(s["done"], 1)
                run("dt", W_DT, 0, 8, H, 8)
                weights("bc")
                w2 = w_slot("bc", 8, 512)
                for g, name in enumerate(("b0", "b1", "c0", "c1")):
                    run(name, w2, g * P, P, H, 8)
                def spread(d):
                    j = job[f"sel{d}"]
                    slot_free(j)
                    mm(banks[:, slot(j), :], sel[:, d, :], DT_B[:, 0, 0:LAT], start=True, stop=True)
                    mm(banks[:, slot(j) + 1, :], sel[:, d, :], DT_B[:, 1, 0:LAT], start=True, stop=True)
                    mm(banks[:, slot(j) + 2, 0:P], sel[:, d, :], DT_B[:, 0, LAT:TOK], start=True, stop=True)
                    mm(banks[:, slot(j) + 2, P:2 * P], sel[:, d, :], DT_B[:, 1, LAT:TOK], start=True, stop=True).then_inc(s["done"], 1)

                run("z0", w, 0, P, H, 8)
                pe.wait_ge(s["bc_ready"], 2)
                for c in range(NCH):
                    if c >= 2:
                        pe.wait_ge(s["v_ready"], c - 1)
                    for ct in range(2):
                        ins = nc.tensor.transpose(banks[:, 6 + c % 2, ct * P:(ct + 1) * P], XT[:, ct, c * P:(c + 1) * P], ident)
                    ins.then_inc(s["xt_turned"], 1)

                pe.wait_ge(s["dt_ready"], 1)
                spread(0)
                spread(1)
                run("z1", w, P, P, H, 8)
                used()
                pe.sem_inc(s["w_used"], 1)
                spread(2)
                spread(3)

                def gla(mx):
                    pe.wait_ge(s["gla_act"], mx + 1)
                    if mx == 1:
                        pe.wait_ge(s["side_freed"], SIDE.index("hq1") + 1)
                    for p in range(2):
                        pe.wait_ge(freed[p], len([j for j in range(job[f"y{mx}"]) if j % 2 == p]))
                    for lev in range(LEVELS + 1):
                        if lev == 0:
                            pe.wait_ge(s["level_k"], mx + 1)
                            q, k = Q, KL
                        else:
                            pe.wait_ge(s["prods"], 3 * (LEVELS * mx + lev))
                            q, k = QL, KL
                        for c in range(NCH):
                            n = (mx * (LEVELS + 1) + lev) * NCH + c
                            if n - mx * (LEVELS + 1) * NCH >= 3:
                                pe.wait_ge(s["att_used"], n - 2)
                            for h in (0, 2, 1, 3):
                                rows = slice(64 * (h % 2), 64 * (h % 2) + 64)
                                cols = slice(c * P, (c + 1) * P)
                                ins = mm(banks[:, 2 * (n % 3) + h % 2, (h // 2) * P:(h // 2 + 1) * P], k[rows, h // 2, cols],
                                         q[rows, h // 2, cols], start=True, stop=True)
                            ins.then_inc(s["att_done"], 1)
                        if mx == 0:
                            if lev < MOD_FILLS - MOD_NORM:
                                mod_fill(MOD_NORM + lev)
                            else:
                                if lev == MOD_FILLS - MOD_NORM:
                                    pe.wait_ge(s["mod_ready"], 2)
                                    weights("g")
                                ct = lev - (MOD_FILLS - MOD_NORM)
                                side(f"g{ct}", w_slot("g", 8, 256), ct * P, P)
                        else:
                            if lev in (0, 4):
                                weights("a" if lev < 4 else "d")
                            if lev == LEVELS - 1:
                                continue
                            name = SIDE[SIDE.index("cq0") + min(lev, LEVELS - 1)]
                            c0, m = {"cq0": (0, P), "cq1": (P, 64), "ckv": (C_CKV, P), "kr": (256, QK_A),
                                     "qd0": (0, P), "qd1": (P, P), "kd": (2 * P, P)}[name]
                            side(name, w_slot("a", 8, 352) if lev < 4 else w_slot("d", 8, 512), c0, m)
                            if lev == 3:
                                side_used(name)
                    if mx == 0:
                        side_used("g1")
                    pe.wait_ge(s["fin_prod"], 4 * (mx + 1))
                    pe.wait_ge(s["att_used"], (mx + 1) * (LEVELS + 1) * NCH)
                    for c in range(NCH):
                        if c >= 4:
                            pe.wait_ge(s["k_copied"], NCH * mx + c - 3)
                        for d in range(4):
                            ins = nc.tensor.transpose(banks[:, c % 4, d * P:(d + 1) * P], (KF, KB)[d // 2][:, d % 2, c * P:(c + 1) * P], ident)
                        ins.then_inc(s["k_turned"], 1)
                    if mx == 0:
                        pe.wait_ge(s["side_freed"], 2)
                        for d in range(4):
                            ins = nc.tensor.transpose(banks[:, 6, d * 64:(d + 1) * 64], S0B[:, d * P:(d + 1) * P], ident[0:64, 0:64])
                        ins.then_inc(s["s0_turned"], 1)
                        pe.wait_ge(s["s0_ready"], 1)
                        weights("qf")
                        side("hq0", w_slot("qf", 8, 512), 0, P)
                    pe.wait_ge(s["k_copied"], NCH * (mx + 1))
                    for t in range(4):
                        if t >= 2:
                            pe.wait_ge(s["cs_used"], 4 * mx + t - 1)
                        for d in range(4):
                            c = 4 if t == 3 else (t, 3 - t)[d // 2]
                            ct = d % 2
                            ins = mm(banks[:, 4 + t % 2, d * P:(d + 1) * P], KTOK[:, c, d, :], V[:, c, ct * P:(ct + 1) * P], start=True, stop=True)
                        ins.then_inc(s["cs_done"], 1)
                    if mx == 0:
                        side("f0", w_slot("qf", 8, 512), 2 * P, P)
                        pe.wait_ge(s["fin_out"], 1)
                        for d in range(4):
                            ins = nc.tensor.transpose(banks[0:64, slot(job["ms0"]), d * P:(d + 1) * P], FIN[:, d * 64:(d + 1) * 64], ident)
                        ins.then_inc(s["ft_turned"], 1)
                    pe.wait_ge(s["sin_ready"], mx + 1)
                    j = job[f"y{mx}"]
                    b0 = slot(j)
                    for ct in range(2):
                        for c in range(NCH):
                            out = banks[:, b0 + ct, c * P:(c + 1) * P] if c < 4 else banks[:, b0 + 2, ct * P:(ct + 1) * P]
                            for hh in range(2):
                                h = 2 * ct + hh
                                ins = mm(out[64 * hh:64 * hh + 64], V[:, c, h * 64:(h + 1) * 64], ATT[:, c, 2 * hh + ct, :],
                                         start=True, stop=c == 4, skip_group_check=True)
                            if c < 4:
                                cols = slice(c * P, (c + 1) * P)
                                mm(out, SIN[:, c, ct, :], PF[:, ct, cols], start=False, stop=False, skip_group_check=True)
                                ins = mm(out, SIN[:, c, 2 + ct, :], SI[:, ct, cols], start=False, stop=True, skip_group_check=True)
                    ins.then_inc(s["done"], 1)
                    if mx == 0:
                        side("hq1", w_slot("qf", 8, 512), P, P)
                        pe.wait_ge(s["ft_ready"], 1)
                    pe.wait_ge(s["ysq"], mx + 1)
                    j = job[f"ms{mx}"]
                    slot_free(j)
                    for ct in range(2):
                        mm(banks[:, slot(j) + ct, :], block1, SQ[:, ct, 0:LAT], start=True, stop=True)
                        ins = mm(banks[:, slot(j) + 2, ct * P:(ct + 1) * P], block1, SQ[:, ct, LAT:TOK], start=True, stop=True)
                    ins.then_inc(s["done"], 1)

                gla(0)
                w = w_slot("qf", 8, 512)
                run("f1", w, 3 * P, P, H, 8)
                used()
                weights("fi")
                w = w_slot("fi", 8, 512)
                run("f2", w, 0, P, H, 8)
                run("f3", w, P, P, H, 8)
                j = job["iv"]
                slot_free(j)
                for c in range(NCH):
                    out = banks[:, slot(j) + c // 2, (c % 2) * 256:(c % 2) * 256 + 256]
                    ins = product(out, [(H[:, k, c * P:(c + 1) * P], w[:, k, 256:512]) for k in range(8)])
                ins.then_inc(s["done"], 1)
                dense_count[0] = j + 1
                used()
                gla(1)

                j = job["msq"]
                slot_free(j)
                pe.wait_ge(s["aq_sq"], 2)
                for b, t0, n in SEGS:
                    mm(banks[:, slot(j) + b, 0:n], ones, SQA[:, 0, t0:t0 + n], start=True, stop=False)
                    ins = mm(banks[:, slot(j) + b, 0:n], ones[0:64, :], SQA[0:64, 1, t0:t0 + n], start=False, stop=True)
                ins.then_inc(s["done"], 1)
                side("vd", w_slot("d", 8, 512), 3 * P, P)
                side_used("vd")
                j = job["mskv"]
                slot_free(j)
                pe.wait_ge(s["aq_sq"], 3)
                for b, t0, n in SEGS:
                    ins = mm(banks[:, slot(j) + b, 0:n], ones, SQA[:, 0, t0:t0 + n], start=True, stop=True)
                ins.then_inc(s["done"], 1)
                pe.wait_ge(s["side_freed"], len(SIDE))
                pe.wait_ge(s["akv_norm"], 1)
                nc.tensor.transpose(banks[:, 7, 0:P], CKT[:, 0:P], ident)
                nc.tensor.transpose(banks[0:QK_A, 7, P:2 * P], CKT[:, P:P + QK_A], ident)
                nc.tensor.transpose(banks[:, 7, 2 * P:3 * P], CKT[:, 2 * P:3 * P], ident).then_inc(s["cache_turned"], 1)
                pe.wait_ge(s["aq_norm"], 2)
                def rotate(n):
                    ap, rows = rotated[n]
                    if n >= 1:
                        pe.wait_ge(s["rot_used"], n)
                    if n >= 4:
                        j = job[f"q{n - 4}"]
                        pe.wait_ge(freed[j % 2], j // 2 + 1)
                    mm(banks[0:rows, 6, :], (cc("swap_a", QK_A) if rows == QK_A else cc("swap_d")), ap, start=True, stop=True).then_inc(s["rot_done"], 1)

                for h in range(4):
                    j = job[f"q{h}"]
                    slot_free(j)
                    cols = slice(h * QK_A, (h + 1) * QK_A)
                    for b, t0, n in SEGS:
                        out = banks[0:QK_A, slot(j) + b, 0:n]
                        mm(out, W_UQ[:, 0, cols], CQN[:, 0, t0:t0 + n], start=True, stop=False)
                        ins = mm(out, W_UQ[0:64, 1, cols], CQN[0:64, 1, t0:t0 + n], start=False, stop=True)
                    ins.then_inc(s["done"], 1)
                    rotate(h)
                pe.wait_ge(s["cache_ready"], 1)
                for h in range(4):
                    j = job[f"k{h}"]
                    slot_free(j)
                    wk = W_UKV[:, h * P:h * P + NOPE]
                    mm(banks[0:NOPE, slot(j), :], wk, CKN[:, 0:LAT], start=True, stop=True)
                    mm(banks[0:NOPE, slot(j) + 2, 0:256], wk, CKN[:, LAT:EXT], start=True, stop=True).then_inc(s["done"], 1)
                    if h < 3:
                        rotate(4 + h)
                j = job["va"]
                slot_free(j)
                wv = W_UKV.rearrange("p (h w c) -> p h w c", h=4, w=2)[:, :, 1, :]
                for c in range(6):
                    out = banks[:, slot(j) + c // 2, (c % 2) * 256:(c % 2) * 256 + 256]
                    ins = mm(out, CKN[:, c * P:(c + 1) * P], wv, start=True, stop=True)
                ins.then_inc(s["done"], 1)
                rotate(7)
                pe.wait_ge(s["attn_in_act"], 1)
                nc.tensor.transpose(banks[:, 7, 0:P], CKN[:, LAT:TOK], ident)
                nc.tensor.transpose(banks[:, 7, P:2 * P], KD[:, LAT:TOK], ident)
                nc.tensor.transpose(banks[:, 7, 2 * P:2 * P + QK_A], KR[0:QK_A, LAT:TOK], ident[0:QK_A, 0:QK_A]).then_inc(s["new_turned"], 1)
                def score(u):
                    un = units[u]
                    sl = 2 * (u % 2)
                    if u >= 2:
                        pe.wait_ge(s["expd"], u - 1)
                    if un["kind"] == "A":
                        q = QA[0:QK_A, un["h"], un["q"]:un["q"] + P]
                        key = KA[0:QK_A, un["h"], :]
                    else:
                        rows = slice(64 * (un["h"] // 2), 64 * (un["h"] // 2) + 64)
                        q = QD[rows, un["h"] % 2, un["q"]:un["q"] + P]
                        key = KD[rows, :]
                    n = (un["hi"] - un["lo"]) * P
                    flat = banks[:, sl:sl + 2, :].rearrange("p b n -> p (b n)")
                    if un["cache"]:
                        ins = mm(flat[:, n:n + P], q, key[:, TOK:EXT], start=True, stop=True)
                    masked = []
                    if un["kind"] == "D" and un["cache"]:
                        if un["t"] > 0:
                            masked.append((0, cc("far_before")))
                        if un["t"] < 3:
                            masked.append((n - P, cc("far_after")))
                    ins = mm(flat[:, 0:n], q, key[:, un["lo"] * P:un["hi"] * P], start=True, stop=not masked, skip_group_check=True)
                    for i, (at, m) in enumerate(masked):
                        ins = mm(flat[:, at:at + P], ident, m, start=False, stop=i == len(masked) - 1, skip_group_check=True)
                    ins.then_inc(s["scored"], 1)

                pe.wait_ge(s["roped"], 8)
                pe.wait_ge(s["kcopied"], 2)
                pe.wait_ge(s["new_ready"], 1)
                pe.wait_ge(s["pool_load"], 16)
                for p in range(2):
                    pe.wait_ge(freed[p], len([j for j in range(job["o0"]) if j % 2 == p]))
                score(0)
                score(1)
                for u in range(len(units) + 4):
                    if u < len(units):
                        un = units[u]
                        pe.wait_ge(s["expd"], u + 1)
                        if u >= 1:
                            pe.wait_ge(s["p_copied"], u)
                        pt = banks[:, 4:6, :].rearrange("p b n -> p (b n)")
                        for i in range(len(un["tiles"])):
                            ins = nc.tensor.transpose(pt[:, i * P:(i + 1) * P], PRB[:, u % 2, i * P:(i + 1) * P], ident)
                        ins.then_inc(s["p_turned"], 1)
                        if u + 2 < len(units):
                            score(u + 2)
                        pe.wait_ge(s["p_copied"], u + 1)
                        g, h = u // 4, un["h"]
                        if h == 0 and g >= 2:
                            pe.wait_ge(s["on_used"], g - 1)
                        v = [VA[:, t, h * 64:(h + 1) * 64] if un["kind"] == "A" else VD[t][:, (h // 2) * 64:(h // 2) * 64 + 64]
                             for t in un["tiles"]]
                        product(banks[:, 6 + g % 2, h * 64:(h + 1) * 64],
                                [(PTS[:, u % 2, i * P:(i + 1) * P], vt) for i, vt in enumerate(v)]).then_inc(s["pv_done"], 1)
                    if u >= 6 and u % 4 == 2:
                        g = u // 4 - 1
                        pe.wait_ge(s["on_ready"], g + 1)
                        for i in range(2):
                            ins = nc.tensor.transpose(banks[:, 6 + g % 2, (2 + i) * P:(3 + i) * P], ON[:, g % 2, i * P:(i + 1) * P], ident)
                        ins.then_inc(s["on_turned"], 1)
                pe.wait_ge(s["on_used"], len(units) // 4)

                for m in range(KT_M):
                    if m % 4 == 0:
                        weights(f"o{m // 4}")
                    run(f"o{m}", w_slot(f"o{m // 4}", 8, 512), (m % 4) * P, P, MIX, 8)
                    if m % 4 == 3:
                        used()
                mean_product(1)
                layer_norm(1)
                ffn(2)
                layer_norm(2)
                pe.wait_ge(s["affine"], 24)
                pe.sem_inc(arrived, 1)
                pe.wait_ge(go, l + 1)

            for n in range(2 * NCH):
                t, half = n // 2, n % 2
                if n >= 4:
                    pe.wait_ge(fin_copy, n - 3)
                for k in range(4):
                    ins = nc.tensor.transpose(banks[:, n % 4, k * P:(k + 1) * P], X[:, half * 4 + k, t * P:(t + 1) * P], ident)
                ins.then_inc(fin_turn, 1)


        def scale_of(un):
            return float((QK_A if un["kind"] == "A" else 64) ** -0.5)

        def flat(ap):
            return ap.rearrange("p k t -> p (k t)")

        def halves(ap, m):
            v = flat(ap).rearrange("p (b h m) -> p b h m", h=2, m=m)
            return v[:, :, 0, :], v[:, :, 1, :]

        def group_cols(j, b, n, rows=P):
            return banks[0:rows, slot(j) + b, 0:n]

        @blockctx.scalar
        def _(act):
            def f(out, in_, func=ACT.Copy, **kw):
                return nc.scalar.activation(out, in_, func, **kw)

            act.wait_ge(init_lb, 1)
            f(LBT[:, 0:8], LBT[:, 0:8], ACT.Exp).then_inc(init_lb, 1)
            f(SC, LBT[:, 8:24].rearrange("p (g k) -> p k g", g=2), ACT.Silu).then_inc(init_cond, 1)

            with act.Fori(0, DEPTH) as l:
                link = chain(act, s["act_chain"])

                def finish(ins, signal, value):
                    ins.then_inc(signal, 1)
                    act.wait_ge(signal, value)

                def evacuate(name, dsts, func=ACT.Copy, rows=P, **kw):
                    j = job[name]
                    act.wait_ge(s["done"], j + 1)
                    for src, dst in dsts:
                        ins = f(dst, src, func, **kw)
                    ins.then_inc(freed[j % 2], 1)

                def both(name, dst, rows=P):
                    j = job[name]
                    return [(group_cols(j, b, n, rows), dst[:, t0:t0 + n]) for b, t0, n in SEGS]


                def mod_row(i, bank=6):
                    act.wait_ge(s["mod_row"], i + 1)
                    if i:
                        act.wait_ge(s["mod_turned"], i)
                    f(MROW, banks[0:2, bank, :]).then_inc(s["mrow_copied"], 1)

                def weights_hi(n, i=None):
                    act.wait_ge(raw_loaded[n % 2], 32 * (n // 2 + 1) if i is None else i * 32 + 32 * (n // 2 + 1))
                    if n >= 2:
                        act.wait_ge(s["f_done"], n - 1 if i is None else i * 2 + (n - 1))
                    f(WHI[n % 2], WRAW[n % 2]).then_inc(s["w_hi"], 1)

                def modulate(sub):
                    act.wait_ge(s["mod_ready"], 1 + (sub == 2))
                    for m in range(KT_M):
                        if sub:
                            act.wait_ge(s["affine"], 8 * (sub - 1) + m + 1)
                        at = 8 * (sub // 2) + m
                        if sub != 1 and m >= 2:
                            act.wait_ge(s["h_lo"], at - 1)
                        dst = H[:, m] if sub == 1 else GATE[:, m % 2]
                        for g, (b, t0, n) in enumerate(SEGS):
                            ins = f(dst[:, t0:t0 + n], X[:, m, t0:t0 + n], ACT.Identity,
                                    scale=MOD[:, sub, 1, m, g:g + 1], bias=MOD[:, sub, 0, m, g:g + 1])
                        ins.then_inc(s["modded"], 1)
                        if sub == 1 and m == 1:
                            mod_row(MOD_FIRST + 1, 2)
                        if sub != 1:
                            act.wait_ge(s["modded"], 8 * sub + m + 1)
                            f(HHI[:, m], GATE[:, m % 2]).then_inc(s["h_hi"], 1)

                def ffn(sub):
                    def gate(par, c, n, hid, dst, split_next):
                        act.wait_ge(s["f_done"], n + 1)
                        act.wait_ge(s["hid_lo"], hid)
                        f(GATE[:, c], banks[:, 4 * par:4 * par + 2, 0:HALF], ACT.Silu).then_inc(s["gated"], 1)
                        split_next()
                        act.wait_ge(s["product"], hid + 1)
                        f(dst, GATE[:, c:c + 1]).then_inc(s["hid_hi"], 1)

                    for g in range(2):
                        n0 = sub // 2 * FFN_JOBS + g * GROUP_JOBS
                        h0 = (sub + g) * FG
                        pairs = HIDHI[:, 0:FG - 1].rearrange("p (i c) t -> p i c t", c=2)
                        with act.Fori(0, FG // 2) as i:
                            for c in range(2):
                                n = n0 + c
                                gate(n % 2, c, i * 2 + n, i * 2 + (h0 + c), pairs[:, bass.ds(i, 1), c, :],
                                     lambda: weights_hi(n + 2, i))
                        n = n0 + FG - 1
                        gate(n % 2, 0, n, h0 + FG - 1, HIDHI[:, FG - 1:FG, :], lambda: weights_hi(n + 2))
                        for m in range(KT_M):
                            n = n0 + FG + m
                            if n + 2 < (sub // 2 + 1) * FFN_JOBS:
                                weights_hi(n + 2)

                def layer_norm(sub, meanwhile=None):
                    for i in range(4):
                        act.wait_ge(s["centred"], 4 * sub + i + 1)
                        f(SQX[:, 2 * i:2 * i + 2, :], X[:, 2 * i:2 * i + 2, :], ACT.Square).then_inc(s["squared"], 1)
                    if meanwhile:
                        meanwhile()
                    act.wait_ge(s["var_ready"], sub + 1)
                    for b, t0, n in SEGS:
                        link(f(RS[:, t0:t0 + n], banks[:, 4 + b // 2, 0:n], ACT.Ln, scale=1.0 / D_MODEL, bias=eps))
                    finish(f(RS[:], RS[:], ACT.Exp, scale=-0.5), s["rstd"], sub + 1)

                for i in range(MOD_FIRST):
                    mod_row(i)
                    if i == MOD_FIRST - 3:
                        act.wait_ge(s["par_load"], 16 * N_SMALL)
                        f(DTP[:, 2:3], DTP[:, 1:2], ACT.Exp).then_inc(s["dt_step"], 1)
                act.wait_ge(s["w_used"], MOD_FIRST)
                weights_hi(0)
                weights_hi(1)
                modulate(0)
                ffn(0)
                layer_norm(0, lambda: mod_row(MOD_FIRST, 2))
                modulate(1)

                act.wait_ge(s["pads"], 1)
                conv_jobs = ("x0", "x1", "b0", "b1", "c0", "c1")
                conv_dst = (XT[:, 0], XT[:, 1], BB[:, 0], BB[:, 1], Q[:, 0], Q[:, 1])

                def conv_silu(i):
                    act.wait_ge(s["conv_out"], i + 1)
                    bias = PT2[:, R_CB + i:R_CB + i + 1]
                    f(conv_dst[i][:, 0:LAT], CONV[:, 0:LAT], ACT.Silu, bias=bias)
                    finish(f(conv_dst[i][:, LAT:TOK], CONV[:, LAT + 4:644], ACT.Silu, bias=bias), s["bc_ready"], i + 1)

                r, e, w1, lg = (DTW[:, k, :] for k in range(4))
                for i, name in enumerate(conv_jobs):
                    j = job[name]
                    act.wait_ge(s["done"], j + 1)
                    if i >= 2:
                        act.wait_ge(s["conv_out"], i - 1)
                    f(CPAD[:, i % 2, 2:2 + LAT], group_cols(j, 0, LAT))
                    finish(f(CPAD[:, i % 2, 6 + LAT:6 + TOK], group_cols(j, 2, CTX)), s["conv_in"], i + 1)
                    act.sem_inc(freed[j % 2], 1)
                    if i >= 1:
                        conv_silu(i - 1)
                    if i == 2:
                        act.wait_ge(s["dt_step"], 2)
                        link(f(e, r, ACT.Abs))
                        finish(f(e, e, ACT.Exp, scale=-1.0), s["dt_step"], 3)
                    if i == 3:
                        act.wait_ge(s["dt_step"], 4)
                        finish(f(lg, w1, ACT.Ln), s["dt_step"], 5)
                conv_silu(5)
                evacuate("z0", both("z0", ZS[:, 0]), ACT.Silu)
                for c in range(NCH):
                    act.wait_ge(s["xt_turned"], c + 1)
                    finish(f(V[:, c, :], banks[:, 6 + c % 2, 0:256]), s["v_ready"], c + 1)
                for d in range(4):
                    j = job[f"sel{d}"]
                    act.wait_ge(s["done"], j + 1)
                    dst = (PF, SI)[d // 2][:, d % 2]
                    f(dst[:, 0:LAT], banks[:, slot(j) + 1, :])
                    finish(f(dst[:, LAT:TOK], banks[:, slot(j) + 2, P:2 * P]), s["adt_copied"], d + 1)
                    if d == 1:
                        evacuate("z1", both("z1", ZS[:, 1]), ACT.Silu)
                act.sem_inc(s["gla_act"], 1)

                def side_out(name, dst, func=ACT.Copy, rows=P):
                    act.wait_ge(s["side_done"], SIDE.index(name) + 1)
                    if name == "vd":
                        f(VD_LAT, banks[:, 6, :].rearrange("p (c n) -> p c n", n=P))
                        ins = f(VD_CTX, banks[:, 7, 0:P])
                    else:
                        for b, t0, n in SEGS:
                            ins = f(dst[:, t0:t0 + n], banks[0:rows, 6 + b // 2, 0:n], func)
                    ins.then_inc(s["side_freed"], 1)

                side1 = (("cq0", CQ[:, 0]), ("cq1", CQ[0:64, 1], ACT.Copy, 64), ("ckv", KVR), ("kr", KR[0:QK_A], ACT.Copy, QK_A),
                         ("qd0", QD[:, 0]), ("qd1", QD[:, 1]), ("kd", KD))

                def gla(mx):
                    act.wait_ge(s["excl_zero"], mx + 1)
                    for lev in range(1, LEVELS + 1):
                        m = 2 ** (lev - 1)
                        act.wait_ge(s["att_done"], (mx * (LEVELS + 1) + lev) * NCH)
                        if lev > 1:
                            act.wait_ge(s["sums"], 4 * (LEVELS * mx + lev - 1))
                        (q1, q2), (k1, k2) = halves(QL, m), halves(KL, m)
                        for dst, src in ((q1, halves(SI, m)[0]), (q2, halves(PF, m)[1]),
                                         (k1, halves(SE, m)[0]), (k2, halves(PB, m)[1])):
                            f(dst, src, ACT.Exp).then_inc(s["exps"], 1)
                        if mx == 0:
                            if lev <= MOD_FILLS - MOD_NORM:
                                mod_row(MOD_NORM + lev - 1)
                            else:
                                side_out("g0", MIX[:, 4], ACT.Silu)
                        else:
                            if lev < LEVELS:
                                side_out(*side1[lev - 1])
                    act.wait_ge(s["sums"], 4 * LEVELS * (mx + 1))
                    ends = lambda ap, i: ap.rearrange("p k (c i) -> p k c i", i=P)[:, :, :, i]
                    link(f(DEC[:, 0], ends(PF, P - 1), ACT.Exp))
                    link(f(DEC[:, 1], ends(SI, 0), ACT.Exp))
                    for ap in (PF, SI, SE, PB):
                        f(ap, ap, ACT.Exp).then_inc(s["fin_exp"], 1)
                    if mx == 0:
                        side_out("g1", MIX[:, 5], ACT.Silu)
                    else:
                        side_out(*side1[LEVELS - 1])
                    for c in range(NCH):
                        act.wait_ge(s["k_turned"], NCH * mx + c + 1)
                        f(KTOK[:, c], banks[:, c % 4, :].rearrange("p (d n) -> p d n", d=4)).then_inc(s["k_copied"], 1)
                    if mx == 0:
                        side_out("hq0", Q[:, 0])
                        side_out("f0", MIX[:, 0])
                        act.wait_ge(s["ft_turned"], 1)
                        f(FINT[:], banks[0:64, slot(job["ms0"]), :]).then_inc(s["ft_ready"], 1)
                    else:
                        act.wait_ge(s["side_freed"], len(SIDE) - 1)
                        f(SQA[:, 0], CQ[:, 0], ACT.Square).then_inc(s["aq_sq"], 1)
                        f(SQA[0:64, 1], CQ[0:64, 1], ACT.Square).then_inc(s["aq_sq"], 1)
                    act.wait_ge(s["y_ready"], mx + 1)
                    f(SQ, Y, ACT.Square).then_inc(s["ysq"], 1)
                    if mx == 0:
                        side_out("hq1", Q[:, 1])
                    j = job[f"ms{mx}"]
                    act.wait_ge(s["done"], j + 1)
                    b0 = slot(j)
                    link(f(RB[:, :, 0:LAT], banks[:, b0:b0 + 2, :], ACT.Ln, scale=1.0 / 64, bias=eps))
                    link(f(RB[:, :, LAT:TOK], banks[:, b0 + 2, 0:256].rearrange("p (k n) -> p k n", k=2), ACT.Ln, scale=1.0 / 64, bias=eps))
                    act.sem_inc(freed[j % 2], 1)
                    f(RB, RB, ACT.Exp, scale=-0.5).then_inc(s["y_rstd"], 1)

                gla(0)
                act.wait_ge(s["mixed_ready"], 1)
                act.wait_ge(s["side_freed"], SIDE.index("f0") + 1)
                f(PF[:, 0], MIX[:, 0], ACT.Sigmoid)
                finish(f(KF[:, 0], MIX[:, 0], ACT.Sigmoid, scale=-1.0), s["f_raw"], 1)
                for i in range(1, 4):
                    j = job[f"f{i}"]
                    act.wait_ge(s["done"], j + 1)
                    for b, t0, n in SEGS:
                        f((PF, SI)[i // 2][:, i % 2, t0:t0 + n], group_cols(j, b, n), ACT.Sigmoid)
                        ins = f((KF, KB)[i // 2][:, i % 2, t0:t0 + n], group_cols(j, b, n), ACT.Sigmoid, scale=-1.0)
                    finish(ins, s["f_raw"], i + 1)
                    act.sem_inc(freed[j % 2], 1)
                j = job["iv"]
                b0 = slot(j)
                pair = lambda ap: ap.rearrange("p (c n) -> p c n", n=256)
                evacuate("iv", [(pair(banks[:, b0, :]), V[:, 0:2, :]), (pair(banks[:, b0 + 1, :]), V[:, 2:4, :]),
                                (banks[:, b0 + 2, 0:256], V[:, 4, :])])
                act.wait_ge(s["f_ready"], 4)
                link(f(PF, PF, ACT.Ln))
                link(f(SI, SI, ACT.Ln))
                act.sem_inc(s["gla_act"], 1)
                gla(1)

                for n, (name, size) in enumerate((("msq", Q_RANK), ("mskv", KV_RANK))):
                    j = job[name]
                    act.wait_ge(s["done"], j + 1)
                    if n == 0:
                        f(SQA[:, 0], KVR, ACT.Square).then_inc(s["aq_sq"], 1)
                    else:
                        act.wait_ge(s["aq_norm"], 2)
                    for b, t0, k in SEGS:
                        link(f(RA[:, t0:t0 + k], group_cols(j, b, k), ACT.Ln, scale=1.0 / size, bias=eps))
                    act.sem_inc(freed[j % 2], 1)
                    finish(f(RA, RA, ACT.Exp, scale=-0.5), s["aq_rstd"], n + 1)
                    if n == 0:
                        side_out("vd", None)
                act.wait_ge(s["mixed_ready"], 2)
                act.wait_ge(s["cache_turned"], 1)
                link(f(CKN[:, TOK:EXT], banks[:, 7, 0:P]))
                link(f(KR[0:QK_A, TOK:EXT], banks[0:QK_A, 7, P:2 * P]))
                finish(f(KD[:, TOK:EXT], banks[:, 7, 2 * P:3 * P]), s["cache_ready"], 1)
                for h in range(4):
                    evacuate(f"q{h}", both(f"q{h}", QA[0:QK_A, h], QK_A))
                for h in range(4):
                    b0 = slot(job[f"k{h}"])
                    evacuate(f"k{h}", [(banks[0:NOPE, b0, :], KA[0:NOPE, h, 0:LAT]), (banks[0:NOPE, b0 + 2, 0:256], KA[0:NOPE, h, LAT:EXT])])
                b0 = slot(job["va"])
                evacuate("va", [(pair(banks[:, b0 + i, :]), VA[:, 2 * i:2 * i + 2, :]) for i in range(3)])
                for p in range(2):
                    act.wait_ge(freed[p], len([j for j in range(job["va"] + 1) if j % 2 == p]))
                act.sem_inc(s["attn_in_act"], 1)
                act.wait_ge(s["new_turned"], 1)
                finish(f(NEWROWS[:, 0:2 * P + QK_A], banks[:, 7, 0:2 * P + QK_A]), s["new_ready"], 1)
                act.wait_ge(s["roped"], 1)
                for i in range(2):
                    f(KA[NOPE:QK_A, 2 * i:2 * i + 2, :], bc(KR[NOPE:QK_A, :].unsqueeze(1), [ROPE, 2, EXT])).then_inc(s["kcopied"], 1)

                def probs(u):
                    un = units[u]
                    n = len(un["tiles"]) * P
                    sc = SM[:, u // 4 % 2, :, un["h"]]
                    act.wait_ge(s["maxed"], u + 1)
                    if u >= 2:
                        act.wait_ge(s["p_turned"], u - 1)
                    src = banks[:, 2 * (u % 2):2 * (u % 2) + 2, :].rearrange("p b n -> p (b n)")[:, 0:n]
                    if un["kind"] == "D":
                        f(sc[:, 3:4], SINK[:, un["h"]:un["h"] + 1], ACT.Exp, bias=sc[:, 1:2])
                    f(PRB[:, u % 2, 0:n], src, ACT.Exp, scale=scale_of(un), bias=sc[:, 1:2], accum_out=sc[:, 2:3]).then_inc(s["expd"], 1)

                probs(0)
                for u, un in enumerate(units):
                    if u + 1 < len(units):
                        probs(u + 1)
                    n = len(un["tiles"]) * P
                    act.wait_ge(s["p_turned"], u + 1)
                    if u >= 2:
                        act.wait_ge(s["pv_done"], u - 1)
                    f(PTS[:, u % 2, 0:n], banks[:, 4:6, :].rearrange("p b n -> p (b n)")[:, 0:n]).then_inc(s["p_copied"], 1)

                layer_norm(1, lambda: (weights_hi(FFN_JOBS), weights_hi(FFN_JOBS + 1)))
                modulate(2)
                ffn(2)
                layer_norm(2)
                for m in range(KT_M):
                    act.wait_ge(s["normed"], m + 1)
                    f(X[:, m, :], X[:, m, :], ACT.Identity, scale=PT1[:, R_LNG + 16 + m:R_LNG + 17 + m],
                      bias=PT1[:, R_LNB + 16 + m:R_LNB + 17 + m]).then_inc(s["affine"], 1)
                act.wait_ge(s["affine"], 24)
                act.sem_inc(arrived, 1)
                act.wait_ge(go, l + 1)

        @blockctx.vector
        def _(dve):
            v = nc.vector
            for n in range(2 * NCH):
                t, half = n // 2, n % 2
                dve.wait_ge(init_turn, n + 1)
                v.tensor_copy(X[:, 4 * half:4 * half + 4, t * P:(t + 1) * P],
                              banks[:, n % 4, :].rearrange("p (k n) -> p k n", k=4)).then_inc(init_copy, 1)
            dve.wait_ge(init_turn, 2 * NCH + 1)
            v.tensor_copy(LBT[:], banks[:, 4, 0:24]).then_inc(init_copy, 1)
            dve.wait_ge(init_copy, 2 * NCH + 1)
            v.tensor_tensor(LBW[:], LBT[:, 0:4], LBT[:, 4:8], ALU.max).then_inc(init_copy, 1)
            dve.wait_ge(init_copy, 2 * NCH + 2)
            v.tensor_tensor(LBT[:, 0:8].rearrange("p (l c) -> p l c", l=2), LBT[:, 0:8].rearrange("p (l c) -> p l c", l=2),
                            bc(LBW[:].unsqueeze(1), [P, 2, 4]), ALU.subtract).then_inc(init_lb, 1)
            dve.wait_ge(init_lb, 2)
            v.tensor_tensor(LBW[:], LBT[:, 0:4], LBT[:, 4:8], ALU.add).then_inc(init_lb, 1)
            dve.wait_ge(init_lb, 3)
            v.reciprocal(LBW[:], LBW[:]).then_inc(init_lb, 1)
            dve.wait_ge(init_lb, 4)
            v.tensor_tensor(LBN[:], LBT[:, 4:8], LBW[:], ALU.mult).then_inc(init_lb, 1)
            v.memset(LB[:], 0.0).then_inc(init_lb, 1)
            dve.wait_ge(init_lb, 6)

            with dve.Fori(0, DEPTH) as l:
                link = chain(dve, s["dve_chain"])

                def finish(ins, signal, value):
                    ins.then_inc(signal, 1)
                    dve.wait_ge(signal, value)

                dve.wait_ge(s["par_turned"], 1)
                link(v.tensor_copy(PT1[:], banks[:, 5, 0:ROWS1]))
                finish(v.tensor_copy(PT2[:], banks[:, 5, P:P + ROWS2]), s["par_ready"], 1)
                link(v.tensor_scalar(OML[:], LB[:], -1.0, 1.0, ALU.mult, ALU.add))
                link(v.tensor_scalar(SINK[:, 4:8], SINK[:, 0:4], -1.0, None, ALU.mult))
                for hh in range(2):
                    rows = slice(64 * hh, 64 * hh + 64)
                    sk = SKIP[rows, :].rearrange("p (d c h) -> p d c h", d=2, c=2)
                    link(v.tensor_tensor(DS[rows, :], sk[:, 0, :, hh], sk[:, 1, :, hh], ALU.add))
                dve.wait_ge(s["dt_step"], 1)
                link(v.tensor_scalar(DTP[:, 3:4], DTP[:, 2:3], -1.0, None, ALU.mult))

                def modulation(r0, r1, turned):
                    dve.wait_ge(s["mod_turned"], turned)
                    rows = MOD.rearrange("p s w m g -> p (s w m) g")[:, r0:r1]
                    link(v.tensor_tensor(rows, banks[:, 7, 256 + 2 * r0:256 + 2 * r1].rearrange("p (r g) -> p r g", g=2),
                                         bc(PT1[:, r0:r1].unsqueeze(2), [P, r1 - r0, 2]), ALU.add))

                modulation(0, 4 * MOD_FIRST, MOD_FIRST)
                for sub in range(2):
                    link(v.tensor_scalar(MOD[:, sub, 1], MOD[:, sub, 1], 1.0, None, ALU.add))
                link(v.tensor_scalar(MOD[:, 0, 2], MOD[:, 0, 2], 0.5, None, ALU.mult))
                dve.sem_inc(s["mod_ready"], 1)

                def weights_lo(n, i=None):
                    dve.wait_ge(s["w_hi"], n + 1 if i is None else i * 2 + (n + 1))
                    v.tensor_tensor(WLO[n % 2], WRAW[n % 2], WHI[n % 2].bitcast(F32), ALU.subtract).then_inc(s["w_lo"], 1)

                def input_lo_tile(sub, m):
                    dve.wait_ge(s["h_hi"], 8 * (sub // 2) + m + 1)
                    v.tensor_tensor(HLO[:, m], GATE[:, m % 2], HHI[:, m].bitcast(F32), ALU.subtract).then_inc(s["h_lo"], 1)

                def scale_residual(sub):
                    dve.wait_ge(s["modded"], 8 * (sub + 1))
                    link(v.tensor_scalar(X, X, float(ALPHA), None, ALU.mult))

                def add_up(sub, m):
                    if m == 0:
                        dve.sem_inc(s["x_summed"], 1)
                    else:
                        finish(v.tensor_tensor(GATE[:, 0], X[:, 0] if m == 1 else GATE[:, 0], X[:, m], ALU.add), s["x_summed"], KT_M * sub + m + 1)

                def residual(name, sub, m):
                    j = job[name]
                    dve.wait_ge(s["done"], j + 1)
                    for g, (b, t0, n) in enumerate(SEGS):
                        ins = v.scalar_tensor_tensor(out=X[:, m, t0:t0 + n], in0=group_cols(j, b, n), scalar=MOD[:, sub, 2, m, g:g + 1],
                                                     in1=X[:, m, t0:t0 + n], op0=ALU.mult, op1=ALU.add)
                    ins.then_inc(freed[j % 2], 1)
                    dve.wait_ge(freed[j % 2], j // 2 + 1)
                    add_up(sub, m)

                def ffn(sub):
                    def hidden(par, c, hid, hi, lo, split_next):
                        dve.wait_ge(s["gated"], hid + 1)
                        v.tensor_tensor(GATE[:, c].rearrange("p (h t) -> p h t", h=2), GATE[:, c].rearrange("p (h t) -> p h t", h=2),
                                        banks[:, 4 * par + 2:4 * par + 4, 0:HALF], ALU.mult).then_inc(s["product"], 1)
                        dve.wait_ge(s["product"], hid + 1)
                        dve.sem_inc(f_freed[par], 1)
                        split_next()
                        dve.wait_ge(s["hid_hi"], hid + 1)
                        v.tensor_tensor(lo, GATE[:, c:c + 1], hi.bitcast(F32), ALU.subtract).then_inc(s["hid_lo"], 1)

                    for g in range(2):
                        n0 = sub // 2 * FFN_JOBS + g * GROUP_JOBS
                        h0 = (sub + g) * FG
                        hi2, lo2 = (x[:, 0:FG - 1].rearrange("p (i c) t -> p i c t", c=2) for x in (HIDHI, HIDLO))
                        with dve.Fori(0, FG // 2) as i:
                            for c in range(2):
                                n = n0 + c
                                hidden(n % 2, c, i * 2 + (h0 + c), hi2[:, bass.ds(i, 1), c, :], lo2[:, bass.ds(i, 1), c, :],
                                       lambda: weights_lo(n + 2, i))
                        n = n0 + FG - 1
                        hidden(n % 2, 0, h0 + FG - 1, HIDHI[:, FG - 1:FG, :], HIDLO[:, FG - 1:FG, :], lambda: weights_lo(n + 2))
                        for m in range(KT_M):
                            n = n0 + FG + m
                            if n + 2 < (sub // 2 + 1) * FFN_JOBS:
                                weights_lo(n + 2)
                            dve.wait_ge(s["f_done"], n + 1)
                            b = 4 * (n % 2)
                            for src, t0, cols, grp in ((banks[:, b, 0:HALF], 0, HALF, 0), (banks[:, b + 1, 0:LAT - HALF], HALF, LAT - HALF, 0),
                                                       (banks[:, b + 1, LAT - HALF:HALF], LAT, CTX, 1)):
                                ins = v.scalar_tensor_tensor(out=X[:, m, t0:t0 + cols], in0=src, scalar=MOD[:, sub, 2, m, grp:grp + 1],
                                                             in1=X[:, m, t0:t0 + cols], op0=ALU.mult, op1=ALU.add)
                            ins.then_inc(f_freed[n % 2], 1)
                            if g == 1:
                                dve.wait_ge(f_freed[n % 2], n // 2 + 1)
                                add_up(sub, m)

                def layer_norm(sub, meanwhile=None):
                    dve.wait_ge(s["mean_ready"], sub + 1)
                    for i in range(4):
                        for b, t0, n in SEGS:
                            x2 = X[:, 2 * i:2 * i + 2, t0:t0 + n]
                            ins = v.scalar_tensor_tensor(out=x2, in0=bc(banks[:, 6 + b // 2, 0:n].unsqueeze(1), [P, 2, n]),
                                                         scalar=-1.0 / D_MODEL, in1=x2, op0=ALU.mult, op1=ALU.add)
                        ins.then_inc(s["centred"], 1)
                    for i in range(4):
                        dve.wait_ge(s["squared"], 4 * sub + i + 1)
                        ins = v.tensor_tensor(SQX[:, 2 * i], SQX[:, 2 * i], SQX[:, 2 * i + 1], ALU.add)
                        if sub == 0:
                            ins.then_inc(s["sq_summed"], 1)
                            continue
                        link(ins)
                        if i:
                            link(v.tensor_tensor(SQX[:, 0], SQX[:, 0], SQX[:, 2 * i], ALU.add))
                    if sub:
                        dve.sem_inc(s["sq_summed"], 1)
                    if meanwhile:
                        meanwhile()
                    dve.wait_ge(s["rstd"], sub + 1)
                    dve.wait_ge(s["centred"], 4 * sub + 4)
                    for m in range(KT_M):
                        if sub == 2:
                            v.tensor_tensor(X[:, m, :], X[:, m, :], RS[:], ALU.mult).then_inc(s["normed"], 1)
                            continue
                        link(v.tensor_tensor(X[:, m, :], X[:, m, :], RS[:], ALU.mult))
                        v.tensor_scalar(X[:, m, :], X[:, m, :], PT1[:, R_LNG + 8 * sub + m:R_LNG + 8 * sub + m + 1],
                                        PT1[:, R_LNB + 8 * sub + m:R_LNB + 8 * sub + m + 1], ALU.mult, ALU.add).then_inc(s["affine"], 1)
                        if sub == 1:
                            if m >= 2:
                                input_lo_tile(2, m - 2)
                    if sub == 1:
                        input_lo_tile(2, 6)
                        input_lo_tile(2, 7)

                weights_lo(0)
                weights_lo(1)
                for m in range(KT_M):
                    input_lo_tile(0, m)
                scale_residual(0)
                ffn(0)
                layer_norm(0)
                scale_residual(1)

                r, e, w1, lg = (DTW[:, k, :] for k in range(4))
                for i in range(6):
                    dve.wait_ge(s["conv_in"], i + 1)
                    if i >= 1:
                        dve.wait_ge(s["bc_ready"], i)
                    for tap in range(TAPS):
                        src = CPAD[:, i % 2, tap:tap + 644]
                        wt = PT2[:, R_CW + 6 * tap + i:R_CW + 6 * tap + i + 1]
                        if tap == 0:
                            link(v.tensor_scalar(CONV, src, wt, None, ALU.mult))
                        else:
                            ins = v.scalar_tensor_tensor(out=CONV, in0=src, scalar=wt, in1=CONV, op0=ALU.mult, op1=ALU.add)
                            if tap < TAPS - 1:
                                link(ins)
                            else:
                                finish(ins, s["conv_out"], i + 1)
                    if i == 1:
                        j = job["dt"]
                        dve.wait_ge(s["done"], j + 1)
                        for b, t0, n in SEGS:
                            link(v.tensor_scalar(r[:, t0:t0 + n], group_cols(j, b, n, 8), DTP[:, 0:1], None, ALU.add))
                        dve.sem_inc(freed[j % 2], 1)
                        dve.sem_inc(s["dt_step"], 1)
                    if i == 2:
                        dve.wait_ge(s["dt_step"], 3)
                        finish(v.tensor_scalar(w1, e, 1.0, None, ALU.add), s["dt_step"], 4)
                    if i == 3:
                        dve.wait_ge(s["dt_step"], 5)
                        t2 = DT_B[:, 0]
                        link(v.tensor_scalar(t2, w1, -1.0, None, ALU.add))
                        link(v.tensor_tensor(e, e, t2, ALU.subtract))
                        link(v.reciprocal(w1, w1))
                        link(v.tensor_tensor(e, e, w1, ALU.mult))
                        link(v.tensor_tensor(lg, lg, e, ALU.add))
                        link(v.scalar_tensor_tensor(out=DT_B[:, 0], in0=r, scalar=0.0, in1=lg, op0=ALU.max, op1=ALU.add))
                        finish(v.tensor_scalar(DT_B[:, 1], DT_B[:, 0], DTP[:, 3:4], None, ALU.mult), s["dt_ready"], 1)
                dve.wait_ge(s["bc_ready"], 6)
                for d in range(4):
                    j = job[f"sel{d}"]
                    dve.wait_ge(s["adt_copied"], d + 1)
                    ct = d % 2
                    for b, t0, n in SEGS:
                        ins = v.tensor_tensor((KF, KB)[d // 2][:, ct, t0:t0 + n], group_cols(j, b, n), BB[:, ct, t0:t0 + n], ALU.mult)
                    ins.then_inc(freed[j % 2], 1)

                def gla(mx):
                    if mx == 1:
                        dve.wait_ge(s["side_freed"], SIDE.index("hq1") + 1)
                    for p in range(2):
                        dve.wait_ge(freed[p], len([j for j in range(job[f"y{mx}"]) if j % 2 == p]))
                    finish(v.tensor_tensor(KL, KF, KB, ALU.add), s["level_k"], mx + 1)

                    def merge(lev):
                        mask = bc(masks[:, lev, :].unsqueeze(1).unsqueeze(1), [P, 2, 2, P])
                        for c in range(NCH):
                            n = (mx * (LEVELS + 1) + lev) * NCH + c
                            dve.wait_ge(s["att_done"], n + 1)
                            v.copy_predicated(ATT[:, c].rearrange("p (a b) n -> p a b n", a=2), mask,
                                              banks[:, 2 * (n % 3):2 * (n % 3) + 2, 0:256].rearrange("p a (b n) -> p a b n", b=2)).then_inc(s["att_used"], 1)

                    merge(0)
                    for lev in range(1, LEVELS + 1):
                        m = 2 ** (lev - 1)
                        at = LEVELS * mx + lev
                        dve.wait_ge(s["exps"], 4 * at)
                        v.tensor_tensor(QL, QL, Q, ALU.mult).then_inc(s["prods"], 1)
                        (k1, k2) = halves(KL, m)
                        v.tensor_tensor(k1, k1, halves(KF, m)[0], ALU.mult).then_inc(s["prods"], 1)
                        v.tensor_tensor(k2, k2, halves(KB, m)[1], ALU.mult).then_inc(s["prods"], 1)
                        if mx == 0 and lev == MOD_FILLS - MOD_NORM:
                            modulation(4 * MOD_FIRST, 72, MOD_FILLS)
                            link(v.tensor_scalar(MOD[:, 2, 1], MOD[:, 2, 1], 1.0, None, ALU.add))
                            link(v.tensor_scalar(MOD[:, 2, 2], MOD[:, 2, 2], 0.5, None, ALU.mult))
                            dve.sem_inc(s["mod_ready"], 1)
                        merge(lev)
                    dve.wait_ge(s["fin_exp"], 4 * mx + 4)
                    for x, y in ((PF, Q), (SI, Q)):
                        v.tensor_tensor(x, x, y, ALU.mult).then_inc(s["fin_prod"], 1)
                    for x, y in ((KF, SE), (KB, PB)):
                        v.tensor_tensor(x, x, y, ALU.mult).then_inc(s["fin_prod"], 1)
                    dve.wait_ge(s["sin_zero"], mx + 1)
                    if mx == 0:
                        dve.wait_ge(s["s0_turned"], 1)
                        src = banks[:, 6, 0:256].rearrange("p (d n) -> p d n", d=4)
                    else:
                        src = S0C[:].rearrange("p (d n) -> p d n", d=4)
                    for d in range(2):
                        for hh in range(2):
                            rows = slice(64 * hh, 64 * hh + 64)
                            link(v.tensor_copy(SIN[rows, 3 * d, 2 * d:2 * d + 2, rows], src[rows, 2 * d:2 * d + 2, :]))
                    dve.sem_inc(s["s0_ready"], 1)
                    for t in range(4):
                        dve.wait_ge(s["cs_done"], 4 * mx + t + 1)
                        cs = banks[:, 4 + t % 2, :].rearrange("p (d n) -> p d n", d=4)
                        for hh in range(2):
                            rows = slice(64 * hh, 64 * hh + 64)
                            if t == 3:
                                link(v.tensor_copy(FIN[rows, :].rearrange("p (d n) -> p d n", d=4), cs[rows, :, rows]))
                                continue
                            for d in range(4):
                                src_c, dst_c = (t, t + 1) if d < 2 else (3 - t, 2 - t)
                                link(v.scalar_tensor_tensor(out=SIN[rows, dst_c, d, rows], in0=SIN[rows, src_c, d, rows],
                                                            scalar=DEC[rows, d // 2, d % 2, src_c:src_c + 1], in1=cs[rows, d, rows],
                                                            op0=ALU.mult, op1=ALU.add))
                        dve.sem_inc(s["cs_used"], 1)
                    dve.sem_inc(s["fin_out"], 1)
                    dve.sem_inc(s["sin_ready"], 1)
                    j = job[f"y{mx}"]
                    b0 = slot(j)
                    dve.wait_ge(s["done"], j + 1)
                    parts = ((banks[:, b0:b0 + 2, :], slice(0, LAT)), (banks[:, b0 + 2, 0:256].rearrange("p (k n) -> p k n", k=2), slice(LAT, TOK)))
                    for src, cols in parts:
                        if mx == 1:
                            link(v.tensor_copy(Y[:, :, cols], src))
                        else:
                            for ct in range(2):
                                link(v.scalar_tensor_tensor(out=Y[:, ct, cols], in0=XT[:, ct, cols], scalar=DS[:, ct:ct + 1],
                                                            in1=src[:, ct], op0=ALU.mult, op1=ALU.add))
                    dve.sem_inc(freed[j % 2], 1)
                    if mx == 0:
                        link(v.tensor_tensor(Y, Y, ZS, ALU.mult))
                    dve.sem_inc(s["y_ready"], 1)
                    dve.wait_ge(s["y_rstd"], mx + 1)
                    g0 = (R_SN, R_HN)[mx]
                    for ct in range(2):
                        dst = MIX[:, 2 + ct] if mx == 0 else Y[:, ct]
                        link(v.scalar_tensor_tensor(out=dst, in0=Y[:, ct], scalar=PT2[:, g0 + ct:g0 + ct + 1], in1=RB[:, ct],
                                                    op0=ALU.mult, op1=ALU.mult))
                    if mx == 1:
                        link(v.tensor_tensor(MIX[:, 4:6], Y, MIX[:, 4:6], ALU.mult))
                    dve.sem_inc(s["mixed_ready"], 1)

                gla(0)
                for i in range(4):
                    dve.wait_ge(s["f_raw"], i + 1)
                    d, ct = i // 2, i % 2
                    lb, oml = LB[:, i:i + 1], OML[:, i:i + 1]
                    fg, key = (PF, SI)[d][:, ct], (KF, KB)[d][:, ct]
                    link(v.tensor_scalar(fg, fg, oml, lb, ALU.mult, ALU.add))
                    link(v.tensor_scalar(key, key, oml, None, ALU.mult))
                    finish(v.tensor_scalar(fg, fg, F_MIN, None, ALU.max), s["f_ready"], i + 1)
                gla(1)

                dve.wait_ge(s["aq_rstd"], 1)
                for ct, rows in ((0, P), (1, 64)):
                    v.scalar_tensor_tensor(out=CQN[0:rows, ct], in0=CQ[0:rows, ct], scalar=PT2[0:rows, R_QN + ct:R_QN + ct + 1],
                                           in1=RA[0:rows], op0=ALU.mult, op1=ALU.mult).then_inc(s["aq_norm"], 1)
                dve.wait_ge(s["aq_rstd"], 2)
                v.scalar_tensor_tensor(out=CKN[:, 0:TOK], in0=KVR, scalar=PT2[:, R_KVN:R_KVN + 1], in1=RA,
                                       op0=ALU.mult, op1=ALU.mult).then_inc(s["akv_norm"], 1)
                for n, (ap, rows) in enumerate(rotated):
                    cos, sin = (cc("cos_a", QK_A), cc("sin_a", QK_A)) if rows == QK_A else (cc("cos_d"), cc("sin_d"))
                    dve.wait_ge(s["rot_done"], n + 1)
                    finish(v.tensor_tensor(ROT[0:rows], banks[0:rows, 6, :], sin, ALU.mult), s["rot_used"], n + 1)
                    link(v.tensor_tensor(ap, ap, cos, ALU.mult))
                    finish(v.tensor_tensor(ap, ap, ROT[0:rows], ALU.add), s["roped"], n + 1)

                def row_max(u):
                    un = units[u]
                    sc = SM[:, u // 4 % 2, :, un["h"]]
                    n = len(un["tiles"]) * P
                    src = banks[:, 2 * (u % 2):2 * (u % 2) + 2, :].rearrange("p b n -> p (b n)")[:, 0:n]
                    dve.wait_ge(s["scored"], u + 1)
                    link(v.reduce_max(sc[:, 0:1], src, AX_X))
                    if un["kind"] == "A":
                        ins = v.tensor_scalar(sc[:, 1:2], sc[:, 0:1], -scale_of(un), None, ALU.mult)
                    else:
                        ins = v.tensor_scalar(sc[:, 1:2], sc[:, 0:1], -scale_of(un), SINK[:, 4 + un["h"]:5 + un["h"]], ALU.mult, ALU.min)
                    ins.then_inc(s["maxed"], 1)

                row_max(0)
                for u in range(len(units) + 4):
                    if u + 1 < len(units):
                        row_max(u + 1)
                    g = u // 4 - 1
                    if g < 0:
                        continue
                    un, sc = units[4 * g], SM[:, g % 2]
                    if u % 4 == 1:
                        dve.wait_ge(s["pv_done"], 4 * g + 4)
                        total = sc[:, 2]
                        if un["kind"] == "D":
                            link(v.tensor_tensor(sc[:, 4], sc[:, 2], sc[:, 3], ALU.add))
                            total = sc[:, 4]
                        link(v.reciprocal(sc[:, 5], total))
                        v.tensor_tensor(ON[:, g % 2].rearrange("p (h n) -> p h n", h=4),
                                        banks[:, 6 + g % 2, 0:256].rearrange("p (h n) -> p h n", h=4),
                                        bc(sc[:, 5].unsqueeze(2), [P, 4, 64]), ALU.mult).then_inc(s["on_ready"], 1)
                    if u % 4 == 3:
                        tile = 0 if un["kind"] == "A" else 6
                        dve.wait_ge(s["on_turned"], g + 1)
                        v.tensor_copy(MIX[:, tile:tile + 2, un["q"]:un["q"] + P],
                                      banks[:, 6 + g % 2, 256:512].rearrange("p (k n) -> p k n", k=2)).then_inc(s["on_used"], 1)
                for m in range(KT_M):
                    residual(f"o{m}", 1, m)
                layer_norm(1, lambda: (weights_lo(FFN_JOBS), weights_lo(FFN_JOBS + 1)))
                scale_residual(2)
                ffn(2)
                layer_norm(2)
                dve.wait_ge(s["affine"], 24)
                link(v.tensor_tensor(LB[:], LB[:], LBN[:], ALU.add))
                dve.sem_inc(arrived, 1)
                dve.wait_ge(go, l + 1)

            for n in range(2 * NCH):
                t, half = n // 2, n % 2
                dve.wait_ge(fin_turn, n + 1)
                v.tensor_copy(XIN[:, t, half * 512:(half + 1) * 512], banks[:, n % 4, :]).then_inc(fin_copy, 1)

        @blockctx.gpsimd
        def _(pool):
            g = nc.gpsimd
            g.memset(CKT[:, P:P + NOPE], 0.0).then_inc(init_ready, 1)
            pool.wait_ge(init_ready, 1)

            with pool.Fori(0, DEPTH) as l:
                link = chain(pool, s["pool_chain"])
                pool.wait_ge(s["modded"], 16)
                for c0, c1 in ((0, 2), (2 + LAT, 6 + LAT), (6 + TOK, 8 + TOK)):
                    link(g.memset(CPAD[:, :, c0:c1], 0.0))
                pool.sem_inc(s["pads"], 1)
                sums_done = [0]
                for mx in range(2):
                    if mx == 1:
                        pool.wait_ge(s["mixed_ready"], 1)
                    link(g.memset(SIN, 0.0))
                    pool.sem_inc(s["sin_zero"], 1)
                    pool.wait_ge(s["gla_act"], mx + 1)
                    pool.wait_ge(s["level_k"], mx + 1)
                    link(g.memset(SE, 0.0))
                    link(g.memset(PB, 0.0))
                    pool.sem_inc(s["excl_zero"], 1)
                    for lev in range(1, LEVELS + 1):
                        m = 2 ** (lev - 1)
                        nb = 2 * TOK // (2 * m)
                        pool.wait_ge(s["exps"], 4 * (LEVELS * mx + lev))
                        (p1, p2), (i1, i2), (e1, _), (_, b2) = (halves(x, m) for x in (PF, SI, SE, PB))
                        wide = lambda ap: bc(ap, [P, nb, m])
                        for dst, add in ((e1, p2[:, :, m - 1:m]), (b2, i1[:, :, 0:1]), (p2, p1[:, :, m - 1:m]), (i1, i2[:, :, 0:1])):
                            ins = g.tensor_tensor(dst, dst, wide(add), ALU.add)
                            ins.then_inc(s["sums"], 1)
                            sums_done[0] += 1
                            pool.wait_ge(s["sums"], sums_done[0])
                pool.sem_inc(pool_arrived, 1)
                pool.wait_ge(go, l + 1)


_INS = ["x_prompt", "x_sample", "cache_a_ckv", "cache_a_krope", "state_b_ssm", "state_c_hgrn", "cache_d_k", "cache_d_v",
        "c", "c_ctx", "w_mod", "b_mod", "ln_g", "ln_b", "ffn_w_gu", "ffn_w_down", "w_in", "w_out", "mla_q_norm",
        "mla_kv_norm", "mla_w_uq", "mla_w_ukv", "ssd_conv_w", "ssd_conv_b", "ssd_a_log", "ssd_dt_bias", "ssd_d",
        "ssd_norm", "hgrn_lb_logits", "hgrn_norm", "gqa_sink"]
_OUTS = [("y_p", (1, CTX, D_MODEL)), ("y_s", (1, LAT, D_MODEL)), ("out_ckv", (1, DEPTH, CTX, KV_RANK)),
         ("out_krope", (1, DEPTH, CTX, ROPE)), ("out_b", (1, DEPTH, 2, 4, 64, 64)), ("out_c", (1, DEPTH, 2, 4, 64, 64)),
         ("out_dk", (1, DEPTH, CTX, 2, 64)), ("out_dv", (1, DEPTH, CTX, 2, 64))]


def kernel(**inputs):
    import concourse.bacc as bacc
    from concourse.bass_utils import run_bass_kernel_spmd

    nc = bacc.Bacc("TRN2", target_bir_lowering=False, num_devices=1)
    consts, const_at = constants()
    arrays, aps = {"in_consts": consts}, {}
    aps["consts"] = nc.dram_tensor("in_consts", consts.shape, F32, kind="ExternalInput").ap()
    for name in _INS:
        x = np.ascontiguousarray(inputs[name])
        arrays[f"in_{name}"] = x
        aps[name] = nc.dram_tensor(f"in_{name}", x.shape, mybir.dt.from_np(x.dtype), kind="ExternalInput").ap()
    for name, shape in _OUTS:
        aps[name] = nc.dram_tensor(name, shape, F32, kind="ExternalOutput").ap()
    trunk_kernel(nc, aps, consts, const_at)
    r = run_bass_kernel_spmd(nc, [arrays], core_ids=[0])
    return tuple(r.results[0][name] for name, _ in _OUTS)
```
